# Optimizing a Trainium2 kernel written in Bass

```python
import math
import jax, jax.numpy as jnp
from jax import lax
import numpy as np

D_MODEL = 1024
BATCH = 1
SEQ = 256
DEPTH = 1
DEC_BATCH = 1
DEC_SEQ = 512
PAST_LEN = 128

EPS = 1e-6
NEG_INF = -1e30
N_Q_HEADS = 16
N_KV_HEADS = 4
Q_PER_KV = N_Q_HEADS // N_KV_HEADS
HEAD_DIM = 64
ATTN_WIDTH = N_Q_HEADS * HEAD_DIM
KV_WIDTH = N_KV_HEADS * HEAD_DIM
WINDOW = 128
ATTN_BLOCK = 128
ROPE_THETA = 10000.0
D_INNER = 2 * D_MODEL
SSM_HEAD_DIM = 64
N_SSM_HEADS = D_INNER // SSM_HEAD_DIM
N_SSM_GROUPS = 4
HEADS_PER_GROUP = N_SSM_HEADS // N_SSM_GROUPS
D_STATE = 128
BC_WIDTH = N_SSM_GROUPS * D_STATE
CONV_DIM = D_INNER + 2 * BC_WIDTH
CONV_W = 7
CHUNK = 128
N_EXPERT_GROUPS = 4
EXPERTS_PER_GROUP = 8
N_EXPERTS = N_EXPERT_GROUPS * EXPERTS_PER_GROUP
TOP_K = 2
D_EXPERT = 512
ROW_BLOCK = 128
PROJ_SIZES = (ATTN_WIDTH, KV_WIDTH, KV_WIDTH, D_INNER, CONV_DIM, N_SSM_HEADS, N_SSM_HEADS, D_MODEL, D_MODEL)
D_PROJ = sum(PROJ_SIZES)

kernel_name = 'hybrid_swa_ssd_hmoe_encoder'

def rmsnorm(x, gain):
    xf = x.astype(jnp.float32)
    y = xf * lax.rsqrt(jnp.mean(xf * xf, axis=-1, keepdims=True) + EPS)
    return (y * gain.astype(jnp.float32)).astype(x.dtype)

def rope_tables(seq):
    inv = 1.0 / (ROPE_THETA ** (jnp.arange(0, HEAD_DIM, 2, dtype=jnp.float32) / HEAD_DIM))
    ang = jnp.arange(seq, dtype=jnp.float32)[:, None] * inv[None, :]
    return jnp.cos(ang), jnp.sin(ang)

def apply_rope(x, cos, sin):
    half = HEAD_DIM // 2
    shape = (1, x.shape[1]) + (1,) * (x.ndim - 3) + (half,)
    c = cos.reshape(shape)
    s = sin.reshape(shape)
    xf = x.astype(jnp.float32)
    x1, x2 = xf[..., :half], xf[..., half:]
    return jnp.concatenate([x1 * c - x2 * s, x2 * c + x1 * s], axis=-1).astype(x.dtype)

def window_attention(q, k, v, sink):
    b, s = q.shape[0], q.shape[1]
    nb = s // ATTN_BLOCK
    pad = ((0, 0), (ATTN_BLOCK, ATTN_BLOCK), (0, 0), (0, 0))
    kp = jnp.pad(k, pad)
    vp = jnp.pad(v, pad)
    scale = HEAD_DIM ** -0.5
    sink_f = sink.astype(jnp.float32)[None, :, :, None, None]
    key_off = jnp.arange(3 * ATTN_BLOCK) - ATTN_BLOCK
    q_off = jnp.arange(ATTN_BLOCK)

    def one_block(i):
        start = i * ATTN_BLOCK
        qb = lax.dynamic_slice_in_dim(q, start, ATTN_BLOCK, axis=1)
        kb = lax.dynamic_slice_in_dim(kp, start, 3 * ATTN_BLOCK, axis=1)
        vb = lax.dynamic_slice_in_dim(vp, start, 3 * ATTN_BLOCK, axis=1)
        sc = jnp.einsum('bqkgd,bskd->bkgqs', qb, kb).astype(jnp.float32) * scale
        kpos = start + key_off
        qpos = start + q_off
        valid = (jnp.abs(qpos[:, None] - kpos[None, :]) <= WINDOW) & (kpos >= 0)[None, :] & (kpos < s)[None, :]
        sc = jnp.where(valid, sc, NEG_INF)
        m = jnp.maximum(jnp.max(sc, axis=-1, keepdims=True), sink_f)
        p = jnp.exp(sc - m)
        p = p / (jnp.sum(p, axis=-1, keepdims=True) + jnp.exp(sink_f - m))
        return jnp.einsum('bkgqs,bskd->bqkgd', p.astype(vb.dtype), vb)

    out = lax.map(one_block, jnp.arange(nb))
    return jnp.moveaxis(out, 0, 1).reshape(b, s, ATTN_WIDTH)

def ssd_scan(xh, dt, a_head, bm, cm):
    b, s, g, e, p = xh.shape
    n = bm.shape[-1]
    c = s // CHUNK
    X = (xh * dt[..., None]).reshape(b, c, CHUNK, g, e, p)
    Bc = bm.reshape(b, c, CHUNK, g, n)
    Cc = cm.reshape(b, c, CHUNK, g, n)
    a = jnp.moveaxis((dt * a_head).reshape(b, c, CHUNK, g, e), 2, -1)
    a_cum = jnp.cumsum(a, axis=-1)
    diff = a_cum[..., :, None] - a_cum[..., None, :]
    lower = jnp.tril(jnp.ones((CHUNK, CHUNK), dtype=bool))
    decay = jnp.exp(jnp.where(lower, diff, -jnp.inf))
    cb = jnp.einsum('bclgn,bcsgn->bcgls', Cc, Bc)
    y_diag = jnp.einsum('bcgels,bcsgep->bclgep', cb[:, :, :, None] * decay, X)
    decay_to_end = jnp.exp(a_cum[..., -1:] - a_cum)
    chunk_states = jnp.einsum('bclgn,bcgel,bclgep->bcgepn', Bc, decay_to_end, X)
    chunk_decay = jnp.exp(a_cum[..., -1])

    def step(h, inp):
        st, dec = inp
        return dec[..., None, None] * h + st, h

    h0 = jnp.zeros((b, g, e, p, n), jnp.float32)
    _, h_in = lax.scan(step, h0, (jnp.moveaxis(chunk_states, 1, 0), jnp.moveaxis(chunk_decay, 1, 0)))
    h_in = jnp.moveaxis(h_in, 0, 1)
    y_off = jnp.einsum('bclgn,bcgepn,bcgel->bclgep', Cc, h_in, jnp.exp(a_cum))
    return (y_diag + y_off).reshape(b, s, g, e, p)

def ssd_branch(z, xbc, dt_f_raw, dt_b_raw, conv_w, conv_b, a_log_fwd, a_log_bwd,
               dt_bias_fwd, dt_bias_bwd, d_skip, ssm_norm):
    dtype = xbc.dtype
    b, s, _ = xbc.shape
    xbc = lax.conv_general_dilated(xbc, conv_w[:, None, :], window_strides=(1,),
                                   padding=[(CONV_W // 2, CONV_W // 2)],
                                   dimension_numbers=('NWC', 'WIO', 'NWC'),
                                   feature_group_count=CONV_DIM)
    xbc = jax.nn.silu((xbc + conv_b).astype(jnp.float32))
    xs = xbc[..., :D_INNER].reshape(b, s, N_SSM_GROUPS, HEADS_PER_GROUP, SSM_HEAD_DIM)
    bm = xbc[..., D_INNER:D_INNER + BC_WIDTH].reshape(b, s, N_SSM_GROUPS, D_STATE)
    cm = xbc[..., D_INNER + BC_WIDTH:].reshape(b, s, N_SSM_GROUPS, D_STATE)

    def direction(dt_raw, dt_bias, a_log, reverse):
        dt = jax.nn.softplus(dt_raw.astype(jnp.float32) + dt_bias.astype(jnp.float32))
        dt = dt.reshape(b, s, N_SSM_GROUPS, HEADS_PER_GROUP)
        a_head = -jnp.exp(a_log.astype(jnp.float32)).reshape(N_SSM_GROUPS, HEADS_PER_GROUP)
        if reverse:
            y = ssd_scan(jnp.flip(xs, 1), jnp.flip(dt, 1), a_head, jnp.flip(bm, 1), jnp.flip(cm, 1))
            return jnp.flip(y, 1)
        return ssd_scan(xs, dt, a_head, bm, cm)

    y = (direction(dt_f_raw, dt_bias_fwd, a_log_fwd, False)
         + direction(dt_b_raw, dt_bias_bwd, a_log_bwd, True)
         + d_skip.astype(jnp.float32).reshape(N_SSM_GROUPS, HEADS_PER_GROUP)[..., None] * xs)
    y = y.reshape(b, s, D_INNER) * jax.nn.silu(z.astype(jnp.float32))
    return rmsnorm(y, ssm_norm).astype(dtype)

def hier_moe(h, w_router_group, b_router_group, w_router_expert, b_router_expert, w_gate, w_up, w_down):
    b, s, d = h.shape
    t = b * s
    hf = h.reshape(t, d)
    g_prob = jax.nn.softmax((hf @ w_router_group).astype(jnp.float32) + b_router_group.astype(jnp.float32), axis=-1)
    g_idx = jnp.argmax(g_prob, axis=-1)
    g_w = jnp.max(g_prob, axis=-1)
    e_logits = ((hf @ w_router_expert).astype(jnp.float32) + b_router_expert.astype(jnp.float32))
    e_logits = e_logits.reshape(t, N_EXPERT_GROUPS, EXPERTS_PER_GROUP)[jnp.arange(t), g_idx]
    e_prob = jax.nn.softmax(e_logits, axis=-1)
    top_v, top_i = lax.top_k(e_prob, TOP_K)
    weights = g_w[:, None] * top_v / jnp.sum(top_v, axis=-1, keepdims=True)
    expert = g_idx[:, None] * EXPERTS_PER_GROUP + top_i
    flat_e = expert.reshape(-1).astype(jnp.int32)
    flat_w = weights.reshape(-1)
    flat_tok = jnp.repeat(jnp.arange(t, dtype=jnp.int32), TOP_K)
    counts = jnp.bincount(flat_e, length=N_EXPERTS)
    padded = ((counts + ROW_BLOCK - 1) // ROW_BLOCK) * ROW_BLOCK
    pad_end = jnp.cumsum(padded)
    pad_start = pad_end - padded
    raw_start = jnp.cumsum(counts) - counts
    order = jnp.argsort(flat_e)
    sorted_e = flat_e[order]
    dest = pad_start[sorted_e] + jnp.arange(t * TOP_K) - raw_start[sorted_e]
    n_blocks = -(-(t * TOP_K) // ROW_BLOCK) + N_EXPERTS
    n_rows = n_blocks * ROW_BLOCK
    row_tok = jnp.full((n_rows,), t, jnp.int32).at[dest].set(flat_tok[order])
    row_w = jnp.zeros((n_rows,), jnp.float32).at[dest].set(flat_w[order])
    block_e = jnp.minimum(jnp.searchsorted(pad_end, jnp.arange(n_blocks) * ROW_BLOCK, side='right'), N_EXPERTS - 1)
    h_pad = jnp.concatenate([hf, jnp.zeros((1, d), hf.dtype)], axis=0)
    rows = h_pad[row_tok].reshape(n_blocks, ROW_BLOCK, d)

    def expert_block(args):
        xb, e = args
        return (jax.nn.silu(xb @ w_gate[e]) * (xb @ w_up[e])) @ w_down[e]

    out = lax.map(expert_block, (rows, block_e)).reshape(n_rows, d)
    y = jnp.zeros((t + 1, d), jnp.float32).at[row_tok].add(out.astype(jnp.float32) * row_w[:, None])
    return y[:t].reshape(b, s, d).astype(h.dtype)

def encoder_layer(x, cos, sin, norm_mix, w_in, q_norm, k_norm, attn_sink, conv_w, conv_b,
                  a_log_fwd, a_log_bwd, dt_bias_fwd, dt_bias_bwd, d_skip, ssm_norm,
                  w_out_attn, w_out_ssm, w_o, norm_ffn, w_router_group, b_router_group,
                  w_router_expert, b_router_expert, w_gate, w_up, w_down):
    b, s, _ = x.shape
    h = rmsnorm(x, norm_mix)
    proj = h @ w_in
    split_points = np.cumsum(PROJ_SIZES)[:-1].tolist()
    q, k, v, z, xbc, dt_f, dt_b, gate_a, gate_s = jnp.split(proj, split_points, axis=-1)
    q = q.reshape(b, s, N_KV_HEADS, Q_PER_KV, HEAD_DIM)
    k = k.reshape(b, s, N_KV_HEADS, HEAD_DIM)
    v = v.reshape(b, s, N_KV_HEADS, HEAD_DIM)
    q = apply_rope(rmsnorm(q, q_norm), cos, sin)
    k = apply_rope(rmsnorm(k, k_norm), cos, sin)
    attn = window_attention(q, k, v, attn_sink.reshape(N_KV_HEADS, Q_PER_KV))
    a_out = attn @ w_out_attn
    ssm = ssd_branch(z, xbc, dt_f, dt_b, conv_w, conv_b, a_log_fwd, a_log_bwd,
                     dt_bias_fwd, dt_bias_bwd, d_skip, ssm_norm)
    s_out = ssm @ w_out_ssm
    merged = jax.nn.sigmoid(gate_a) * a_out + jax.nn.sigmoid(gate_s) * s_out
    x = x + merged @ w_o
    x = x + hier_moe(rmsnorm(x, norm_ffn), w_router_group, b_router_group, w_router_expert,
                     b_router_expert, w_gate, w_up, w_down)
    return x

def encoder_trunk(x, weights):
    cos, sin = rope_tables(x.shape[1])
    for layer in range(DEPTH):
        x = encoder_layer(x, cos, sin, *[w[layer] for w in weights])
    return x

def setup_inputs(seed: int = 0) -> dict:
    key = jax.random.key(seed)
    ks = jax.random.split(key, 32)
    f32 = jnp.float32
    L = DEPTH

    def nrm(k, shape, scale):
        return jax.random.normal(k, shape, f32) * scale

    def gain(k, shape):
        return 1.0 + 0.02 * jax.random.normal(k, shape, f32)

    def dt_bias(k):
        dt = jnp.exp(jax.random.uniform(k, (L, N_SSM_HEADS), f32, math.log(1e-3), math.log(1e-1)))
        return dt + jnp.log(-jnp.expm1(-dt))

    return {
        'x_prompt': nrm(ks[0], (BATCH, SEQ, D_MODEL), 1.0),
        'x_sample': nrm(ks[1], (DEC_BATCH, DEC_SEQ, D_MODEL), 1.0),
        'norm_mix': gain(ks[2], (L, D_MODEL)),
        'w_in': nrm(ks[3], (L, D_MODEL, D_PROJ), D_MODEL ** -0.5),
        'q_norm': gain(ks[4], (L, HEAD_DIM)),
        'k_norm': gain(ks[5], (L, HEAD_DIM)),
        'attn_sink': nrm(ks[6], (L, N_Q_HEADS), 0.5),
        'conv_w': nrm(ks[7], (L, CONV_W, CONV_DIM), CONV_W ** -0.5),
        'conv_b': nrm(ks[8], (L, CONV_DIM), 0.02),
        'a_log_fwd': jnp.log(jax.random.uniform(ks[9], (L, N_SSM_HEADS), f32, 1.0, 16.0)),
        'a_log_bwd': jnp.log(jax.random.uniform(ks[10], (L, N_SSM_HEADS), f32, 1.0, 16.0)),
        'dt_bias_fwd': dt_bias(ks[11]),
        'dt_bias_bwd': dt_bias(ks[12]),
        'd_skip': gain(ks[13], (L, N_SSM_HEADS)),
        'ssm_norm': gain(ks[14], (L, D_INNER)),
        'w_out_attn': nrm(ks[15], (L, ATTN_WIDTH, D_MODEL), ATTN_WIDTH ** -0.5),
        'w_out_ssm': nrm(ks[16], (L, D_INNER, D_MODEL), D_INNER ** -0.5),
        'w_o': nrm(ks[17], (L, D_MODEL, D_MODEL), D_MODEL ** -0.5),
        'norm_ffn': gain(ks[18], (L, D_MODEL)),
        'w_router_group': nrm(ks[19], (L, D_MODEL, N_EXPERT_GROUPS), D_MODEL ** -0.5),
        'b_router_group': nrm(ks[20], (L, N_EXPERT_GROUPS), 0.01),
        'w_router_expert': nrm(ks[21], (L, D_MODEL, N_EXPERTS), D_MODEL ** -0.5),
        'b_router_expert': nrm(ks[22], (L, N_EXPERTS), 0.01),
        'w_gate': nrm(ks[23], (L, N_EXPERTS, D_MODEL, D_EXPERT), D_MODEL ** -0.5),
        'w_up': nrm(ks[24], (L, N_EXPERTS, D_MODEL, D_EXPERT), D_MODEL ** -0.5),
        'w_down': nrm(ks[25], (L, N_EXPERTS, D_EXPERT, D_MODEL), D_EXPERT ** -0.5),
    }

def reference(x_prompt, x_sample, norm_mix, w_in, q_norm, k_norm, attn_sink, conv_w, conv_b,
              a_log_fwd, a_log_bwd, dt_bias_fwd, dt_bias_bwd, d_skip, ssm_norm,
              w_out_attn, w_out_ssm, w_o, norm_ffn, w_router_group, b_router_group,
              w_router_expert, b_router_expert, w_gate, w_up, w_down):
    weights = (norm_mix, w_in, q_norm, k_norm, attn_sink, conv_w, conv_b,
               a_log_fwd, a_log_bwd, dt_bias_fwd, dt_bias_bwd, d_skip, ssm_norm,
               w_out_attn, w_out_ssm, w_o, norm_ffn, w_router_group, b_router_group,
               w_router_expert, b_router_expert, w_gate, w_up, w_down)
    y_prompt = encoder_trunk(x_prompt, weights)
    y_sample = encoder_trunk(x_sample, weights)
    return (y_prompt, y_sample)


_drawn_inputs = setup_inputs


def setup_inputs(seed=0):
    import zlib

    import numpy as np

    out = dict(_drawn_inputs(seed))
    spreads = {}
    factors = {'q_norm': 8.0,
     'k_norm': 8.0,
     'attn_sink': 8.0,
     'd_skip': 4.065,
     'ssm_norm': 3.053,
     'b_router_group': 24.594,
     'b_router_expert': 17.082,
     'norm_ffn': 3.056}
    for name, (base, spread) in spreads.items():
        noise = np.random.default_rng([zlib.crc32(name.encode()), seed]).standard_normal(out[name].shape)
        drawn = base * np.exp(spread * noise) if base else spread * noise
        out[name] = __import__('jax').numpy.asarray(drawn.astype(out[name].dtype))
    for name, factor in factors.items():
        out[name] = (out[name] * factor).astype(out[name].dtype)
    return out
```

```python
from contextlib import ExitStack

import concourse.bass as bass
import numpy as np
from concourse import mybir

F32 = mybir.dt.float32
I32 = mybir.dt.int32
ALU = mybir.AluOpType
ACT = mybir.ActivationFunctionType
AX = mybir.AxisListType

P = 128
SEQS = (256, 512)
TOK = sum(SEQS)
NT = TOK // P
FIRST = (0, SEQS[0] // P)
TILES = tuple(n // P for n in SEQS)
D = 1024
KD = D // P
EPS = 1e-6
HQ, HKV, HD = 16, 4, 64
QPK = HQ // HKV
HALF = HD // 2
NQK = HQ + HKV
DI = 2 * D
SG, SH, SP_ = 4, 32, 64
HPG = SH // SG
GW = HPG * SP_
NS = 128
CW = 7
PAD = CW // 2
XBC0 = HQ * HD + 2 * HKV * HD + DI
Z0 = HQ * HD + 2 * HKV * HD
DT0 = XBC0 + DI + 2 * SG * NS
GA0 = DT0 + 2 * SH
GS0 = GA0 + D
GC = (GW + 2 * NS) // P
GCOLS = GW + 2 * NS
RAW = sum(n + 2 * PAD for n in SEQS)
CONV = RAW - 2 * PAD
POS = [t * P + (2 * PAD if t >= FIRST[1] else 0) for t in range(NT)]
NG, NE_G, NEXP = 4, 8, 32
DE = 512
KE = DE // P
CAP = 96
NBLK = -(-TOK // CAP)
NOV = (2 * TOK - 1) // CAP
ROWS = (NEXP + NOV) * CAP
BIG = 1e30
WIDE = 3 * P

C_ID, C_UP, C_LO, C_SU, C_ONE = 0, P, 2 * P, 3 * P, 4 * P
C_MASK = 5 * P
C_COS = C_MASK + WIDE
NPOS = max(TILES)
C_SIN = C_COS + NPOS * HD
C_R4 = C_SIN + NPOS * HD
C_R8 = C_R4 + NG
C_EC = C_R8 + NE_G
C_BLK = C_EC + NEXP
NBI = 16
C_NH = C_BLK + NBI
C_N = C_NH + 1
P_GMIX, P_GSSM, P_CONV = 0, KD, KD + DI // P
P_N = P_CONV + SG * GC * (CW + 1)
R_DTB, R_ALOG, R_SKIP, R_SINK = 0, 64, 128, 160
R_BR = 176
R_QK = R_BR + NG + NEXP
R_FFN = R_QK + NQK * HD
R_N = R_FFN + D


def pack_constants():
    c = np.zeros((P, C_N), np.float32)
    i = np.arange(P)
    c[:, C_ID:C_ID + P] = np.eye(P)
    c[:, C_UP:C_UP + P] = i[:, None] <= i[None, :]
    c[:, C_LO:C_LO + P] = i[:, None] >= i[None, :]
    c[:, C_SU:C_SU + P] = i[:, None] < i[None, :]
    c[:, C_ONE:C_ONE + P] = 1.0
    c[:, C_MASK:C_MASK + P] = np.where(i[None, :] >= i[:, None], 0.0, -BIG)
    c[:, C_MASK + 2 * P:C_MASK + WIDE] = np.where(i[None, :] <= i[:, None], 0.0, -BIG)
    inv = 1.0 / (np.float32(10000.0) ** (np.arange(0, HD, 2, dtype=np.float32) / np.float32(HD)))
    ang = (np.arange(NPOS * P, dtype=np.float32)[:, None] * inv[None, :].astype(np.float32))
    cos = np.cos(ang).astype(np.float32).reshape(NPOS, P, HALF).transpose(1, 0, 2)
    sin = np.sin(ang).astype(np.float32).reshape(NPOS, P, HALF).transpose(1, 0, 2)
    c[:, C_COS:C_COS + NPOS * HD] = np.concatenate([cos, cos], -1).reshape(P, -1)
    c[:, C_SIN:C_SIN + NPOS * HD] = np.concatenate([-sin, sin], -1).reshape(P, -1)
    c[:, C_R4:C_R4 + NG] = NG - np.arange(NG)
    c[:, C_R8:C_R8 + NE_G] = NE_G - np.arange(NE_G)
    c[:, C_EC:C_EC + NEXP] = CAP * np.arange(NEXP)
    c[:, C_BLK:C_BLK + NBI] = np.arange(NBI)
    c[:, C_NH] = -0.5
    return c


class Core:
    pass


def open_stage(core):
    nc, own = core.nc, ExitStack()

    def sb(name, shape, dt=F32):
        return own.enter_context(nc.sbuf_tensor(name, shape, dt))

    def sem(name):
        return own.enter_context(nc.semaphore(name))

    return own, sb, sem


def rsqrt(core, pool, out, mean):
    pool.tensor_scalar(mean, mean, EPS, None, ALU.add)
    pool.drain()
    half = core.const[:, C_NH:C_NH + 1].to_broadcast([P, mean.shape[-1]])
    return pool.tensor_tensor(out, mean, half, ALU.pow)


def norm_and_transpose(core):
    nc = core.nc
    own, sb, sem = open_stage(core)
    with own:
        x_all = sb("x_all", [P, NT, D])
        square = sb("norm_square", [P, D])
        mean = sb("norm_mean", [P, NT])
        rstd = sb("norm_rstd", [P, NT])
        h = [sb(f"norm_h{u}", [P, D]) for u in range(2)]
        x_in = [sem(f"x_in{t}") for t in range(NT)]
        const_in, mean_ok, rstd_ok = sem("const_in"), sem("mean_ok"), sem("rstd_ok")
        h_ok, tr_done, tr_free = sem("h_ok"), sem("tr_done"), sem("tr_free")
        zero_ok, zero_out = sem("zero_ok"), sem("zero_out")
        zeros = sb("zeros", [CAP, D])
        with nc.Block() as block:

            @block.sync
            def _(sp):
                for t in range(NT):
                    sp.dma_start(x_all[:, t, :], core.x_tile(t)).then_inc(x_in[t], 16)
                sp.wait_ge(zero_ok, 1)
                blocks = core.rows_in.rearrange("(b p) d -> p b d", p=CAP)
                sp.dma_start(blocks, zeros[:, :].unsqueeze(1).to_broadcast([CAP, NEXP + NOV, D]))\
                    .then_inc(zero_out, 16)
                blocks = core.rows_out[NEXP * CAP:ROWS, :].rearrange("(b p) d -> p b d", p=CAP)
                sp.dma_start(blocks, zeros[:, :].unsqueeze(1).to_broadcast([CAP, NOV, D])).then_inc(zero_out, 16)
                sp.wait_ge(zero_out, 32)

            @block.scalar
            def _(act):
                act.dma_start(core.const[:, :], core.d["constants"]).then_inc(const_in, 16)
                act.dma_start(core.feat[:, :], core.d["features"]).then_inc(const_in, 16)
                act.dma_start(core.row[:, :], core.d["rows"].partition_broadcast(P)).then_inc(const_in, 16)
                for t in range(NT):
                    act.wait_ge(x_in[t], 16)
                    act.activation(square[:, :], x_all[:, t, :], ACT.Square, scale=D ** -0.5,
                                   accum_out=mean[:, t:t + 1]).then_inc(mean_ok, 1)
                    act.drain()

            @block.gpsimd
            def _(pool):
                pool.memset(zeros[:, :], 0.0).then_inc(zero_ok, 1)
                pool.wait_ge(const_in, 48)
                for t in range(NT):
                    pool.wait_ge(mean_ok, t + 1)
                    rsqrt(core, pool, rstd[:, t:t + 1], mean[:, t:t + 1]).then_inc(rstd_ok, 1)

            @block.vector
            def _(dve):
                dve.wait_ge(const_in, 48)
                for t in range(NT):
                    dve.wait_ge(rstd_ok, t + 1)
                    if t >= 2:
                        dve.wait_ge(tr_done, 2 * (t - 1))
                    dve.tensor_scalar(h[t % 2][:, :], x_all[:, t, :], rstd[:, t:t + 1], None,
                                      ALU.mult).then_inc(h_ok, 1)
                    for j in range(2):
                        n = 2 * t + j
                        dve.wait_ge(tr_done, n + 1)
                        gain = core.feat[:, P_GMIX + 4 * j:P_GMIX + 4 * j + 4]
                        dve.tensor_tensor(core.hT[:, 4 * j:4 * j + 4, t * P:(t + 1) * P],
                                          core.bank[n % 8][:, :].rearrange("p (k t) -> p k t", k=4),
                                          gain.unsqueeze(2).to_broadcast([P, 4, P]),
                                          ALU.mult).then_inc(tr_free, 1)

            @block.tensor
            def _(pe):
                pe.wait_ge(const_in, 48)
                for t in range(NT):
                    pe.wait_ge(h_ok, t + 1)
                    for j in range(2):
                        n = 2 * t + j
                        if n >= 8:
                            pe.wait_ge(tr_free, n - 7)
                        for k in range(4):
                            last = pe.transpose(core.bank[n % 8][:, k * P:(k + 1) * P],
                                                h[t % 2][:, (4 * j + k) * P:(4 * j + k + 1) * P],
                                                core.ident)
                        last.then_inc(tr_done, 1)


def step_sizes(core):
    nc = core.nc
    own, sb, sem = open_stage(core)
    H2 = 2 * SH
    with own:
        w_dt = sb("w_dt", [P, KD, H2])
        raw = sb("dt_raw", [P, NT, H2])
        low = sb("dt_low", [P, NT, H2])
        a = sb("dt_a", [P, NT, H2])
        rate = sb("dt_rate", [P, H2])
        sumT = sb("dt_sumT", [SH, 2, TOK])
        w_in, dt_mm, raw_ok, soft_ok, rate_ok, a_ok = (
            sem("w_dt_in"), sem("dt_mm"), sem("dt_raw_ok"), sem("dt_soft_ok"), sem("dt_rate_ok"), sem("dt_a_ok"))
        low_ok, sums_done, exp_in_ok, exp_ok, sumT_ok, sumT_out, dt_ok = (
            sem("dt_low_ok"), sem("dt_sums_done"), sem("dt_exp_in_ok"), sem("dt_exp_ok"),
            sem("dt_sumT_ok"), sem("dt_sumT_out"), sem("dt_ok"))
        tab = core.tab
        flat = "p t h -> p (t h)"
        with nc.Block() as block:

            @block.sync
            def _(sp):
                sp.dma_start(w_dt[:, :, :], core.w_in_cols(DT0, H2)).then_inc(w_in, 16)
                sp.wait_ge(sumT_ok, 2)
                for d in range(2):
                    sp.dma_start(core.sums[d], sumT[:, d, :]).then_inc(sumT_out, 16)
                sp.wait_ge(sumT_out, 32)

            @block.tensor
            def _(pe):
                pe.wait_ge(w_in, 16)
                for t in range(NT):
                    for k in range(KD):
                        last = pe.matmul(core.bank[0][:, t * H2:(t + 1) * H2],
                                         core.hT[:, k, t * P:(t + 1) * P], w_dt[:, k, :],
                                         start=(k == 0), stop=(k == KD - 1))
                last.then_inc(dt_mm, 1)
                pe.wait_ge(a_ok, 1)
                tri = (core.upper, core.lower)
                for d in range(2):
                    last = pe.matmul(core.bank[1 + d][:, 0:NT * SH], tri[d],
                                     a[:, :, d * SH:(d + 1) * SH], start=True, stop=True)
                last = pe.matmul(core.bank[3][:, 0:NT * H2], core.ones, a[:, :, :].rearrange(flat),
                                 start=True, stop=True)
                last.then_inc(sums_done, 1)
                for d in range(2):
                    for t in range(NT):
                        last = pe.matmul(core.bank[4 + 2 * d + t // 4][0:SH, (t % 4) * P:(t % 4 + 1) * P],
                                         a[:, t, d * SH:(d + 1) * SH], tri[d], start=True, stop=True)
                    last.then_inc(sums_done, 1)

            @block.scalar
            def _(act):
                act.activation(rate[:, :], core.row[:, R_ALOG:R_ALOG + H2], ACT.Exp).then_inc(rate_ok, 1)
                act.wait_ge(raw_ok, 1)
                act.activation(low[:, :, :], low[:, :, :], ACT.Exp)
                act.drain()
                act.activation(low[:, :, :], low[:, :, :], ACT.Ln, bias=core.ones[:, 0:1]).then_inc(low_ok, 1)
                act.wait_ge(exp_in_ok, 1)
                for name in ("reach", "to_end", "decay"):
                    last = act.activation(tab[name], tab[name], ACT.Exp)
                last.then_inc(exp_ok, 1)

            @block.vector
            def _(dve):
                dve.wait_ge(dt_mm, 1)
                bias = core.row[:, R_DTB:R_DTB + H2].unsqueeze(1).to_broadcast([P, NT, H2])
                dve.tensor_tensor(raw[:, :, :], core.bank[0][:, 0:NT * H2].rearrange("p (t h) -> p t h", t=NT),
                                  bias, ALU.add)
                dve.drain()
                dve.scalar_tensor_tensor(low[:, :, :], raw[:, :, :], -1.0, raw[:, :, :], ALU.mult, ALU.min)\
                    .then_inc(raw_ok, 1)
                dve.wait_ge(low_ok, 1)
                dve.scalar_tensor_tensor(tab["dt"], raw[:, :, :], 0.0, low[:, :, :], ALU.max, ALU.add)
                dve.drain()
                dve.wait_ge(rate_ok, 1)
                dve.scalar_tensor_tensor(a[:, :, :], tab["dt"], -1.0,
                                         rate[:, :].unsqueeze(1).to_broadcast([P, NT, H2]),
                                         ALU.mult, ALU.mult).then_inc(a_ok, 1)
                dve.wait_ge(sums_done, 1)
                for d in range(2):
                    psum = core.bank[1 + d][:, 0:NT * SH].rearrange("p (t h) -> p t h", t=NT)
                    dve.tensor_copy(tab["cum"][:, :, d * SH:(d + 1) * SH], psum)
                total = core.bank[3][:, 0:NT * H2].rearrange("p (t h) -> p t h", t=NT)
                dve.tensor_copy(tab["decay"], total)
                dve.drain()
                dve.tensor_copy(tab["reach"], tab["cum"])
                dve.tensor_tensor(tab["to_end"], tab["decay"], tab["cum"], ALU.subtract).then_inc(exp_in_ok, 1)
                for d in range(2):
                    dve.wait_ge(sums_done, 2 + d)
                    dve.tensor_copy(sumT[:, d, 0:4 * P], core.bank[4 + 2 * d][0:SH, :])
                    dve.tensor_copy(sumT[:, d, 4 * P:TOK], core.bank[5 + 2 * d][0:SH, 0:TOK - 4 * P])\
                        .then_inc(sumT_ok, 1)
                dve.wait_ge(exp_ok, 1)
                dve.tensor_tensor(tab["to_end"], tab["to_end"], tab["dt"], ALU.mult).then_inc(dt_ok, 1)


def ssd_groups(core):
    nc = core.nc
    own, sb, sem = open_stage(core)
    STATES = []
    for d in range(2):
        for s in range(2):
            chunks = list(range(FIRST[s], FIRST[s] + TILES[s]))
            chunks = chunks if d == 0 else chunks[::-1]
            STATES += [(t, d, n == 0) for n, t in enumerate(chunks[:-1])]
    ENTERS = {(t + 1 if d == 0 else t - 1, d): n for n, (t, d, _) in enumerate(STATES)}
    NST = len(STATES)
    NPROD = 2 * GC
    TABLES = ("dt", "cum", "reach", "to_end", "decay")
    with own:
        w = sb("ssd_w", [P, KD, GCOLS])
        raw = sb("ssd_raw", [P, GC, RAW])
        xc = sb("ssd_xc", [P, GC, CONV])
        xs = sb("ssd_xs", [P, NT, GW])
        b_tok = sb("ssd_b", [P, NT, NS])
        cb = sb("ssd_cb", [P, 2, NT, P])
        decays = [sb(f"ssd_decays{u}", [P, 2, HPG, P]) for u in range(2)]
        x_dt = [sb(f"ssd_x_dt{u}", [P, 2, GW]) for u in range(2)]
        x_end = [sb(f"ssd_x_end{u}", [P, GW]) for u in range(2)]
        state = sb("ssd_state", [P, NST, GW])
        y = [sb(f"ssd_y{u}", [P, GW]) for u in range(2)]
        part = sb("ssd_part", [P, GW])
        tabs = sb("ssd_tabs", [P, len(TABLES), NT, 2, HPG])
        conv_p = sb("ssd_conv_p", [P, GC, CW + 1])
        skip = sb("ssd_skip", [P, HPG])
        gt = {name: tabs[:, n] for n, name in enumerate(TABLES)}

        w_ok, proj_done, proj_free, conv_done, silu_done = (
            sem("ssd_w_ok"), sem("ssd_proj_done"), sem("ssd_proj_free"), sem("ssd_conv_done"), sem("ssd_silu_done"))
        tr_done, tr_free, cb_done, cb_ok, pads_ok, tabs_ok = (
            sem("ssd_tr_done"), sem("ssd_tr_free"), sem("ssd_cb_done"), sem("ssd_cb_ok"), sem("ssd_pads_ok"),
            sem("ssd_tabs_ok"))
        xend_ok, st_done, st_ok, xdt_ok = sem("ssd_xend_ok"), sem("ssd_st_done"), sem("ssd_st_ok"), sem("ssd_xdt_ok")
        sums_in = [sem(f"ssd_sums_in{u}") for u in range(2)]
        diff_ok, exp_ok, decay_ok, y_mm, y_ok = (
            sem("ssd_diff_ok"), sem("ssd_exp_ok"), sem("ssd_decay_ok"), sem("ssd_y_mm"), sem("ssd_y_ok"))
        y_out = [sem(f"ssd_y_out{u}") for u in range(2)]

        def off_banks(t):
            return (4, 5) if t % 2 == 0 else (6, 7)

        def heads(ap, width):
            return ap.unsqueeze(2).to_broadcast([P, HPG, width])

        def by_head(ap):
            return ap.rearrange("p (e c) -> p e c", e=HPG)

        with nc.Block() as block:

            @block.sync
            def _(sp):
                def load_w(g):
                    for col, width, at in ((XBC0 + g * GW, GW, 0), (XBC0 + DI + g * NS, NS, GW),
                                           (XBC0 + DI + SG * NS + g * NS, NS, GW + NS)):
                        sp.dma_start(w[:, :, at:at + width], core.w_in_cols(col, width)).then_inc(w_ok, 16)

                def load_sums(g, t):
                    for d in range(2):
                        sums = core.sums[d][bass.ds(g * HPG, HPG), t * P:(t + 1) * P]
                        sp.dma_start(decays[t % 2][:, d, :, :], sums.partition_broadcast(P))\
                            .then_inc(sums_in[t % 2], 16)

                def group(g, last):
                    load_sums(g, 0)
                    load_sums(g, 1)
                    if not last:
                        sp.wait_ge(proj_done, NPROD * g + NPROD)
                        load_w(g + 1)
                    for t in range(NT):
                        if t + 2 < NT:
                            sp.wait_ge(y_mm, NT * g + t + 1)
                            load_sums(g, t + 2)
                        sp.wait_ge(y_ok, NT * g + t + 1)
                        sp.dma_start(core.y_ssd[t * P:(t + 1) * P, bass.ds(g * GW, GW)], y[t % 2][:, :])\
                            .then_inc(y_out[t % 2], 16)

                load_w(0)
                with sp.Fori(0, SG - 1) as g:
                    group(g, False)
                group(SG - 1, True)
                for u in range(2):
                    sp.wait_ge(y_out[u], SG * (NT // 2) * 16)

            @block.tensor
            def _(pe):
                with pe.Fori(0, SG) as g:
                    pe.wait_ge(w_ok, 48 * g + 48)
                    for n in range(NPROD):
                        ct, s = divmod(n, 2)
                        if n == 2:
                            pe.wait_ge(y_ok, NT * g)
                        if n >= 4:
                            pe.wait_ge(proj_free, NPROD * g + n - 3)
                        at = FIRST[s] * P
                        for k in range(KD):
                            last = pe.matmul(core.bank[n % 4][:, 0:SEQS[s]], w[:, k, ct * P:(ct + 1) * P],
                                             core.hT[:, k, at:at + SEQS[s]], start=(k == 0), stop=(k == KD - 1))
                        last.then_inc(proj_done, 1)
                    pe.wait_ge(silu_done, GC * g + 4)
                    for t in range(NT):
                        if t >= 2:
                            pe.wait_ge(tr_free, 8 * g + t - 1)
                        for c in range(4):
                            last = pe.transpose(core.bank[4 + t % 2][:, c * P:(c + 1) * P],
                                                xc[:, c, POS[t]:POS[t] + P], core.ident)
                        last.then_inc(tr_done, 1)
                    pe.wait_ge(silu_done, GC * g + 5)
                    for j, tiles in enumerate((range(0, 4), range(4, NT))):
                        pe.wait_ge(tr_free, 8 * g + 5 + j)
                        for t in tiles:
                            last = pe.transpose(core.bank[4 + j][:, (t % 4) * P:(t % 4 + 1) * P],
                                                xc[:, 4, POS[t]:POS[t] + P], core.ident)
                        last.then_inc(tr_done, 1)
                    pe.wait_ge(silu_done, GC * g + 6)
                    for j, tiles in enumerate((range(0, 4), range(4, NT))):
                        for t in tiles:
                            last = pe.matmul(core.bank[6 + j][:, (t % 4) * P:(t % 4 + 1) * P],
                                             xc[:, 4, POS[t]:POS[t] + P], xc[:, 5, POS[t]:POS[t] + P],
                                             start=True, stop=True)
                        last.then_inc(cb_done, 1)
                    pe.wait_ge(tr_free, 8 * g + 8)
                    for n, (t, d, _) in enumerate(STATES):
                        pe.wait_ge(xend_ok, NST * g + n + 1)
                        if n >= 2:
                            pe.wait_ge(st_ok, NST * g + n - 1)
                        pe.matmul(core.bank[n % 2][:, :], b_tok[:, t, :], x_end[n % 2][:, :],
                                  start=True, stop=True).then_inc(st_done, 1)
                    pe.wait_ge(cb_ok, 2 * g + 2)
                    for t in range(NT):
                        if t >= 2:
                            pe.wait_ge(y_ok, NT * g + t - 1)
                        for d in range(2):
                            if (t, d) in ENTERS:
                                pe.wait_ge(st_ok, NST * g + ENTERS[t, d] + 1)
                                pe.matmul(core.bank[off_banks(t)[d]][:, :], xc[:, 5, POS[t]:POS[t] + P],
                                          state[:, ENTERS[t, d], :], start=True, stop=True)
                        pe.wait_ge(decay_ok, NT * g + t + 1)
                        pe.wait_ge(xdt_ok, NT * g + t + 1)
                        for e in range(HPG):
                            for d in range(2):
                                last = pe.matmul(core.bank[2 + t % 2][:, e * SP_:(e + 1) * SP_],
                                                 decays[t % 2][:, d, e, :],
                                                 x_dt[t % 2][:, d, e * SP_:(e + 1) * SP_],
                                                 start=(d == 0), stop=(d == 1))
                        last.then_inc(y_mm, 1)

            @block.scalar
            def _(act):
                def silu(g, ct):
                    act.wait_ge(conv_done, GC * g + ct + 1)
                    act.activation(xc[:, ct, :], xc[:, ct, :], ACT.Silu).then_inc(silu_done, 1)

                act.wait_ge(pads_ok, 1)
                with act.Fori(0, SG) as g:
                    for ct in range(GC):
                        for s in range(2):
                            act.wait_ge(proj_done, NPROD * g + 2 * ct + s + 1)
                            at = FIRST[s] * P + PAD + 2 * PAD * s
                            act.activation(raw[:, ct, at:at + SEQS[s]], core.bank[(2 * ct + s) % 4][:, 0:SEQS[s]],
                                           ACT.Copy).then_inc(proj_free, 1)
                        if ct:
                            silu(g, ct - 1)
                    silu(g, GC - 1)
                    for t in range(NT):
                        act.wait_ge(tr_done, 8 * g + t + 1)
                        act.activation(xs[:, t, :], core.bank[4 + t % 2][:, :], ACT.Copy).then_inc(tr_free, 1)
                    for j, (t0, n) in enumerate(((0, 4), (4, NT - 4))):
                        act.wait_ge(tr_done, 8 * g + NT + j + 1)
                        act.activation(b_tok[:, t0:t0 + n, :],
                                       core.bank[4 + j][:, 0:n * P].rearrange("p (t c) -> p t c", t=n),
                                       ACT.Copy).then_inc(tr_free, 1)
                    for t in range(NT):
                        act.wait_ge(diff_ok, NT * g + t + 1)
                        act.activation(decays[t % 2][:, :, :, :], decays[t % 2][:, :, :, :], ACT.Exp)\
                            .then_inc(exp_ok, 1)

            @block.gpsimd
            def _(pool):
                with pool.Fori(0, SG) as g:
                    pool.wait_ge(tabs_ok, g + 1)
                    for n, (t, d, _) in enumerate(STATES):
                        pool.wait_ge(tr_free, 8 * g + t + 1)
                        if n >= 2:
                            pool.wait_ge(st_done, NST * g + n - 1)
                        pool.tensor_tensor(by_head(x_end[n % 2][:, :]), by_head(xs[:, t, :]),
                                           heads(gt["to_end"][:, t, d, :], SP_), ALU.mult).then_inc(xend_ok, 1)
                    for t in range(NT):
                        if t >= 2:
                            pool.wait_ge(y_mm, NT * g + t - 1)
                            pool.wait_ge(y_out[t % 2], 48 * g + 16 * (t // 2))
                        else:
                            pool.wait_ge(y_out[t % 2], 48 * g)
                        pool.wait_ge(tr_free, 8 * g + t + 1)
                        for d in range(2):
                            pool.tensor_tensor(by_head(x_dt[t % 2][:, d, :]), by_head(xs[:, t, :]),
                                               heads(gt["dt"][:, t, d, :], SP_), ALU.mult)
                        pool.tensor_tensor(by_head(y[t % 2][:, :]), by_head(xs[:, t, :]),
                                           heads(skip[:, :], SP_), ALU.mult).then_inc(xdt_ok, 1)

            @block.vector
            def _(dve):
                for s in range(2):
                    at = FIRST[s] * P + 2 * PAD * s
                    dve.memset(raw[:, :, at:at + PAD], 0.0)
                    last = dve.memset(raw[:, :, at + PAD + SEQS[s]:at + 2 * PAD + SEQS[s]], 0.0)
                last.then_inc(pads_ok, 1)
                with dve.Fori(0, SG) as g:
                    dve.tensor_copy(conv_p[:, :, :], core.feat[:, bass.ds(P_CONV + g * (GC * (CW + 1)), GC * (CW + 1))]
                                    .rearrange("p (c k) -> p c k", c=GC))
                    dve.tensor_copy(skip[:, :], core.row[:, bass.ds(R_SKIP + g * HPG, HPG)])
                    dve.tensor_copy(tabs[:, :, :, :, :].rearrange("p n t d h -> p (n t d) h"),
                                    core.tables[:, :, bass.ds(g * HPG, HPG)]).then_inc(tabs_ok, 1)
                    dve.drain()
                    for ct in range(GC):
                        dve.wait_ge(proj_free, NPROD * g + 2 * ct + 2)
                        dve.tensor_scalar(xc[:, ct, :], raw[:, ct, 0:CONV], conv_p[:, ct, 0:1],
                                          conv_p[:, ct, CW:CW + 1], ALU.mult, ALU.add)
                        for k in range(1, CW):
                            dve.drain()
                            last = dve.scalar_tensor_tensor(xc[:, ct, :], raw[:, ct, k:k + CONV], conv_p[:, ct, k:k + 1],
                                                            xc[:, ct, :], ALU.mult, ALU.add)
                        last.then_inc(conv_done, 1)
                    for j, (t0, n) in enumerate(((0, 4), (4, NT - 4))):
                        dve.wait_ge(cb_done, 2 * g + j + 1)
                        psum = core.bank[6 + j][:, 0:n * P].rearrange("p (t c) -> p t c", t=n)
                        for d, tri in enumerate((core.upper, core.lower)):
                            last = dve.tensor_tensor(cb[:, d, t0:t0 + n, :], psum,
                                                     tri.unsqueeze(1).to_broadcast([P, n, P]), ALU.mult)
                        last.then_inc(cb_ok, 1)

                    def differences(t):
                        dve.wait_ge(sums_in[t % 2], 96 * g + 32 * (t // 2) + 32)
                        for d in range(2):
                            dve.tensor_tensor(decays[t % 2][:, d, :, :], decays[t % 2][:, d, :, :],
                                              heads(gt["cum"][:, t, d, :], P), ALU.subtract)
                        dve.drain()
                        flat = decays[t % 2][:, :, :, :].rearrange("p d e l -> p (d e l)")
                        dve.tensor_scalar(flat, flat, 0.0, None, ALU.min).then_inc(diff_ok, 1)

                    differences(0)
                    for n, (t, d, opens) in enumerate(STATES):
                        dve.wait_ge(st_done, NST * g + n + 1)
                        if opens:
                            dve.tensor_copy(state[:, n, :], core.bank[n % 2][:, :]).then_inc(st_ok, 1)
                        else:
                            dve.tensor_tensor(by_head(part[:, :]), by_head(state[:, n - 1, :]),
                                              heads(gt["decay"][:, t, d, :], SP_), ALU.mult)
                            dve.drain()
                            dve.tensor_tensor(state[:, n, :], part[:, :], core.bank[n % 2][:, :], ALU.add)\
                                .then_inc(st_ok, 1)
                        dve.drain()
                    for t in range(NT):
                        if t + 1 < NT:
                            differences(t + 1)
                        dve.wait_ge(exp_ok, NT * g + t + 1)
                        for d in range(2):
                            last = dve.tensor_tensor(decays[t % 2][:, d, :, :], decays[t % 2][:, d, :, :],
                                                     cb[:, d, t, :].unsqueeze(1).to_broadcast([P, HPG, P]), ALU.mult)
                        last.then_inc(decay_ok, 1)
                        dve.wait_ge(y_mm, NT * g + t + 1)
                        last = dve.tensor_tensor(y[t % 2][:, :], y[t % 2][:, :], core.bank[2 + t % 2][:, :], ALU.add)
                        for d in range(2):
                            if (t, d) in ENTERS:
                                dve.tensor_tensor(by_head(part[:, :]), by_head(core.bank[off_banks(t)[d]][:, :]),
                                                  heads(gt["reach"][:, t, d, :], SP_), ALU.mult)
                                dve.drain()
                                last = dve.tensor_tensor(y[t % 2][:, :], y[t % 2][:, :], part[:, :], ALU.add)
                                dve.drain()
                        last.then_inc(y_ok, 1)


def gate_and_norm(core):
    nc = core.nc
    own, sb, sem = open_stage(core)
    NJ = DI // 512
    with own:
        w = [sb(f"z_w{u}", [P, KD, 512]) for u in range(2)]
        y = sb("z_y", [P, NT, DI])
        zs = [sb(f"z_silu{u}", [P, 512]) for u in range(2)]
        square = sb("z_square", [P, DI])
        mean, rstd = sb("z_mean", [P, NT]), sb("z_rstd", [P, NT])
        y_in = [sem(f"z_y_in{t}") for t in range(NT)]
        w_ok = [sem(f"z_w_ok{u}") for u in range(2)]
        z_mm, silu_ok, gated, mean_ok, rstd_ok, y_ok, tr_done, tr_free = (
            sem("z_mm"), sem("z_silu_ok"), sem("z_gated"), sem("z_mean_ok"), sem("z_rstd_ok"), sem("z_y_ok"),
            sem("z_tr_done"), sem("z_tr_free"))
        with nc.Block() as block:

            @block.sync
            def _(sp):
                for j in range(NJ):
                    if j >= 2:
                        sp.wait_ge(z_mm, NT * (j - 1))
                    sp.dma_start(w[j % 2][:, :, :], core.w_in_cols(Z0 + j * 512, 512)).then_inc(w_ok[j % 2], 16)
                    if j == 0:
                        for t in range(NT):
                            sp.dma_start(y[:, t, :], core.y_ssd[t * P:(t + 1) * P, :]).then_inc(y_in[t], 16)

            @block.tensor
            def _(pe):
                with pe.Fori(0, NJ // 2) as i:
                    for u in range(2):
                        pe.wait_ge(w_ok[u], 16 * i + 16)
                        for t in range(NT):
                            n = NT * u + t
                            pe.wait_ge(silu_ok, 2 * NT * i + max(n - 3, 0))
                            for k in range(KD):
                                last = pe.matmul(core.bank[n % 4][:, :], core.hT[:, k, t * P:(t + 1) * P],
                                                 w[u][:, k, :], start=(k == 0), stop=(k == KD - 1))
                            last.then_inc(z_mm, 1)
                for t in range(NT):
                    pe.wait_ge(y_ok, t + 1)
                    for q in range(NJ):
                        n = NJ * t + q
                        if n >= 8:
                            pe.wait_ge(tr_free, n - 7)
                        elif n < 4:
                            pe.wait_ge(silu_ok, NJ * NT)
                        for c in range(4):
                            last = pe.transpose(core.bank[n % 8][:, c * P:(c + 1) * P],
                                                y[:, t, (4 * q + c) * P:(4 * q + c + 1) * P], core.ident)
                        last.then_inc(tr_done, 1)

            @block.scalar
            def _(act):
                with act.Fori(0, NJ // 2) as i:
                    for u in range(2):
                        for t in range(NT):
                            n = NT * u + t
                            act.wait_ge(z_mm, 2 * NT * i + n + 1)
                            act.wait_ge(gated, 2 * NT * i + max(n - 1, 0))
                            act.activation(zs[n % 2][:, :], core.bank[n % 4][:, :], ACT.Silu).then_inc(silu_ok, 1)
                for t in range(NT):
                    act.wait_ge(gated, NT * (NJ - 1) + t + 1)
                    act.activation(square[:, :], y[:, t, :], ACT.Square, scale=DI ** -0.5,
                                   accum_out=mean[:, t:t + 1]).then_inc(mean_ok, 1)
                    act.drain()

            @block.gpsimd
            def _(pool):
                for t in range(NT):
                    pool.wait_ge(mean_ok, t + 1)
                    rsqrt(core, pool, rstd[:, t:t + 1], mean[:, t:t + 1]).then_inc(rstd_ok, 1)

            @block.vector
            def _(dve):
                with dve.Fori(0, NJ // 2) as i:
                    for u in range(2):
                        for t in range(NT):
                            n = NT * u + t
                            dve.wait_ge(y_in[t], 16)
                            dve.wait_ge(silu_ok, 2 * NT * i + n + 1)
                            part = y[:, t, bass.ds((2 * i + u) * 512, 512)]
                            dve.tensor_tensor(part, part, zs[n % 2][:, :], ALU.mult).then_inc(gated, 1)
                dve.drain()
                for t in range(NT):
                    dve.wait_ge(rstd_ok, t + 1)
                    dve.tensor_scalar(y[:, t, :], y[:, t, :], rstd[:, t:t + 1], None, ALU.mult).then_inc(y_ok, 1)
                    for q in range(NJ):
                        n = NJ * t + q
                        dve.wait_ge(tr_done, n + 1)
                        gain = core.feat[:, P_GSSM + 4 * q:P_GSSM + 4 * q + 4]
                        dve.tensor_tensor(core.yT[:, 4 * q:4 * q + 4, t * P:(t + 1) * P],
                                          core.bank[n % 8][:, :].rearrange("p (k t) -> p k t", k=4),
                                          gain.unsqueeze(2).to_broadcast([P, 4, P]), ALU.mult).then_inc(tr_free, 1)


def merge_branch(core, name, branchT, w_out, gate_col, first):
    nc = core.nc
    own, sb, sem = open_stage(core)
    KB = branchT.shape[1]
    w_view = w_out.rearrange("o (k p) n -> (o p) k n", p=P)
    with own:
        wo = [sb(f"{name}_wo{u}", [P, KB, P]) for u in range(2)]
        wg = [sb(f"{name}_wg{u}", [P, KD, P]) for u in range(2)]
        gate = [sb(f"{name}_gate{u}", [P, TOK]) for u in range(2)]
        part = sb(f"{name}_part", [P, TOK])
        w_ok = [sem(f"{name}_w_ok{u}") for u in range(2)]
        mm, gate_ok, merged = sem(f"{name}_mm"), sem(f"{name}_gate_ok"), sem(f"{name}_merged")
        with nc.Block() as block:

            @block.sync
            def _(sp):
                with sp.Fori(0, KD // 2) as i:
                    for u in range(2):
                        c = 2 * i + u
                        sp.wait_ge(mm, 4 * c)
                        sp.dma_start(wg[u][:, :, :], core.w_in_cols(gate_col + c * P, P)).then_inc(w_ok[u], 16)
                        sp.dma_start(wo[u][:, :, :], w_view[:, :, bass.ds(c * P, P)]).then_inc(w_ok[u], 16)

            @block.tensor
            def _(pe):
                pe.sem_inc(mm, 4)
                with pe.Fori(0, KD // 2) as i:
                    for u in range(2):
                        c = 2 * i + u
                        pe.wait_ge(w_ok[u], 32 * i + 32)
                        pe.wait_ge(merged, c)
                        for q, (weights, rhs, depth) in enumerate(((wg, core.hT, KD), (wo, branchT, KB))):
                            for s in range(2):
                                at = FIRST[s] * P
                                for k in range(depth):
                                    last = pe.matmul(core.bank[4 * u + 2 * q + s][:, 0:SEQS[s]],
                                                     weights[u][:, k, :], rhs[:, k, at:at + SEQS[s]],
                                                     start=(k == 0), stop=(k == depth - 1))
                                last.then_inc(mm, 1)

            @block.scalar
            def _(act):
                with act.Fori(0, KD // 2) as i:
                    for u in range(2):
                        c = 2 * i + u
                        act.wait_ge(merged, c)
                        for s in range(2):
                            act.wait_ge(mm, 4 * c + s + 5)
                            at = FIRST[s] * P
                            act.activation(gate[u][:, at:at + SEQS[s]], core.bank[4 * u + s][:, 0:SEQS[s]],
                                           ACT.Sigmoid).then_inc(gate_ok, 1)

            @block.vector
            def _(dve):
                dve.sem_inc(merged, 1)
                with dve.Fori(0, KD // 2) as i:
                    for u in range(2):
                        c = 2 * i + u
                        dve.wait_ge(gate_ok, 2 * c + 2)
                        for s in range(2):
                            dve.wait_ge(mm, 4 * c + s + 7)
                            at = FIRST[s] * P
                            out = core.mergedT[:, bass.ds(c, 1), at:at + SEQS[s]].rearrange("p c t -> p (c t)")
                            last = dve.tensor_tensor(out if first else part[:, at:at + SEQS[s]],
                                                     core.bank[4 * u + 2 + s][:, 0:SEQS[s]],
                                                     gate[u][:, at:at + SEQS[s]], ALU.mult)
                        if not first:
                            dve.drain()
                            out = core.mergedT[:, bass.ds(c, 1), :].rearrange("p c t -> p (c t)")
                            last = dve.tensor_tensor(out, out, part[:, :], ALU.add)
                        last.then_inc(merged, 1)
                        dve.drain()


def project_qkv(core):
    nc = core.nc
    own, sb, sem = open_stage(core)
    QK = NQK * HD
    NPRD = 3
    NTR = NQK // 4
    with own:
        w = sb("qkv_w", [P, KD, NPRD * 512])
        qk = [sb(f"qkv_qk{u}", [P, QK]) for u in range(2)]
        rot = [sb(f"qkv_rot{u}", [P, QK]) for u in range(2)]
        part = sb("qkv_part", [P, QK])
        mean, rstd = sb("qkv_mean", [P, NT, NQK]), sb("qkv_rstd", [P, NT, NQK])
        w_ok = [sem(f"qkv_w_ok{j}") for j in range(NPRD)]
        mm, copied, mean_ok, rstd_ok, rope_ok, tr_done, tr_free = (
            sem("qkv_mm"), sem("qkv_copied"), sem("qkv_mean_ok"), sem("qkv_rstd_ok"), sem("qkv_rope_ok"),
            sem("qkv_tr_done"), sem("qkv_tr_free"))

        def heads(ap, width=HD):
            return ap.rearrange("p (h c) -> p h c", h=NQK)

        with nc.Block() as block:

            @block.sync
            def _(sp):
                for j in range(NPRD):
                    sp.dma_start(w[:, :, j * 512:(j + 1) * 512], core.w_in_cols(j * 512, 512)).then_inc(w_ok[j], 16)

            @block.tensor
            def _(pe):
                def products(t):
                    for j in range(NPRD):
                        n = NPRD * t + j
                        if t == 0:
                            pe.wait_ge(w_ok[j], 16)
                        if n >= 4:
                            pe.wait_ge(copied, n - 3)
                        for k in range(KD):
                            last = pe.matmul(core.bank[n % 4][:, :], core.hT[:, k, t * P:(t + 1) * P],
                                             w[:, k, j * 512:(j + 1) * 512], start=(k == 0), stop=(k == KD - 1))
                        last.then_inc(mm, 1)

                def transposes(t):
                    pe.wait_ge(rope_ok, t + 1)
                    for q in range(NTR):
                        n = NTR * t + q
                        if n >= 4:
                            pe.wait_ge(tr_free, n - 3)
                        for c in range(4):
                            head = 4 * q + c
                            last = pe.transpose(core.bank[4 + n % 4][0:HD, c * P:(c + 1) * P],
                                                rot[t % 2][:, head * HD:(head + 1) * HD], core.ident)
                        last.then_inc(tr_done, 1)

                products(0)
                for t in range(NT):
                    if t + 1 < NT:
                        products(t + 1)
                    transposes(t)

            @block.scalar
            def _(act):
                def copies(t):
                    if t >= 2:
                        act.wait_ge(rope_ok, t - 1)
                    for j in range(NPRD):
                        n = NPRD * t + j
                        act.wait_ge(mm, n + 1)
                        width = min(512, QK - j * 512)
                        last = act.activation(qk[t % 2][:, j * 512:j * 512 + width], core.bank[n % 4][:, 0:width],
                                              ACT.Copy)
                        if width < 512:
                            last = act.activation(core.v[:, t, :], core.bank[n % 4][:, width:512], ACT.Copy)
                        last.then_inc(copied, 1)

                def leave(t):
                    for q in range(NTR):
                        n = NTR * t + q
                        act.wait_ge(tr_done, n + 1)
                        into = core.qT[:, 4 * q:4 * q + 4] if q < HQ // 4 else core.kT[:, :]
                        act.activation(into[:, :, t * P:(t + 1) * P],
                                       core.bank[4 + n % 4][0:HD, :].rearrange("p (h t) -> p h t", h=4),
                                       ACT.Copy).then_inc(tr_free, 1)

                copies(0)
                for t in range(NT):
                    if t + 1 < NT:
                        copies(t + 1)
                    leave(t)

            @block.gpsimd
            def _(pool):
                for t in range(NT):
                    pool.wait_ge(mean_ok, t + 1)
                    pool.tensor_scalar(mean[:, t, :], mean[:, t, :], 1.0 / HD, None, ALU.mult)
                    pool.drain()
                    rsqrt(core, pool, rstd[:, t, :], mean[:, t, :]).then_inc(rstd_ok, 1)

            @block.vector
            def _(dve):
                for t in range(NT):
                    x, r = qk[t % 2][:, :], rot[t % 2][:, :]
                    at = (t - (FIRST[1] if t >= FIRST[1] else 0)) * HD
                    cos = core.const[:, C_COS + at:C_COS + at + HD].unsqueeze(1).to_broadcast([P, NQK, HD])
                    sin = core.const[:, C_SIN + at:C_SIN + at + HD]
                    dve.wait_ge(copied, NPRD * (t + 1))
                    dve.tensor_tensor(part[:, :], x, x, ALU.mult)
                    dve.drain()
                    dve.tensor_reduce(mean[:, t, :], heads(part[:, :]), AX.X, ALU.add).then_inc(mean_ok, 1)
                    dve.wait_ge(rstd_ok, t + 1)
                    dve.tensor_tensor(heads(x), heads(x), rstd[:, t, :].unsqueeze(2).to_broadcast([P, NQK, HD]),
                                      ALU.mult)
                    dve.drain()
                    dve.tensor_tensor(x, x, core.row[:, R_QK:R_QK + QK], ALU.mult)
                    dve.drain()
                    for half in range(2):
                        a, b = half * HALF, (1 - half) * HALF
                        dve.tensor_tensor(heads(part[:, :])[:, :, a:a + HALF], heads(x)[:, :, b:b + HALF],
                                          sin[:, a:a + HALF].unsqueeze(1).to_broadcast([P, NQK, HALF]), ALU.mult)
                    if t >= 2:
                        dve.wait_ge(tr_done, NTR * (t - 1))
                    dve.tensor_tensor(heads(r), heads(x), cos, ALU.mult)
                    dve.drain()
                    dve.tensor_tensor(r, r, part[:, :], ALU.add).then_inc(rope_ok, 1)
                    dve.drain()


def attend(core):
    nc = core.nc
    own, sb, sem = open_stage(core)
    SCALE = HD ** -0.5
    GROUPS = [(t, kv) for t in range(NT) for kv in range(HKV)]

    def window(t):
        s = 0 if t < FIRST[1] else 1
        lo, hi = max(FIRST[s], t - 1), min(FIRST[s] + TILES[s] - 1, t + 1)
        return lo, hi - lo + 1

    PLAN = []
    for g, (t, kv) in enumerate(GROUPS):
        PLAN += [("probs", t, kv, QPK * g + c) for c in range(QPK)]
        if kv == 0 and t > 0:
            PLAN += [("out", t - 1, j, 0) for j in range(2)]
    PLAN += [("out", NT - 1, j, 0) for j in range(2)]
    ORDER = {item: n for n, item in enumerate(PLAN)}
    with own:
        score = [sb(f"att_score{u}", [P, QPK, WIDE]) for u in range(2)]
        top, den = sb("att_top", [P, NT, HQ]), sb("att_den", [P, NT, HQ])
        neg, sunk = sb("att_neg", [P, NT, HQ]), sb("att_sunk", [P, NT, HQ])
        pT = [sb(f"att_pT{u}", [P, WIDE]) for u in range(4)]
        o = [sb(f"att_o{u}", [P, HQ * HD]) for u in range(2)]
        s_mm, s_read, top_ok, p_ok, t_mm, t_free, pv_mm, o_ok = (
            sem("att_s_mm"), sem("att_s_read"), sem("att_top_ok"), sem("att_p_ok"), sem("att_t_mm"),
            sem("att_t_free"), sem("att_pv_mm"), sem("att_o_ok"))
        with nc.Block() as block:

            @block.tensor
            def _(pe):
                def scores(g):
                    t, kv = GROUPS[g]
                    lo, n = window(t)
                    for c in range(QPK):
                        m = QPK * g + c
                        if m >= 2:
                            pe.wait_ge(s_read, m - 1)
                        pe.matmul(core.bank[m % 2][:, 0:n * P], core.qT[:, QPK * kv + c, t * P:(t + 1) * P],
                                  core.kT[:, kv, lo * P:(lo + n) * P], start=True, stop=True).then_inc(s_mm, 1)

                def values(m):
                    t, kv = GROUPS[m // QPK]
                    head = m % HQ
                    lo, n = window(t)
                    pe.wait_ge(t_free, ORDER["probs", t, kv, m] + 1)
                    if head % 8 == 0 and t >= 2:
                        pe.wait_ge(o_ok, t - 1)
                    at = (head % 8) * HD
                    for b in range(n):
                        last = pe.matmul(core.bank[4 + 2 * (t % 2) + head // 8][:, at:at + HD],
                                         pT[m % 4][:, b * P:(b + 1) * P],
                                         core.v[:, lo + b, kv * HD:(kv + 1) * HD], start=(b == 0), stop=(b == n - 1))
                    last.then_inc(pv_mm, 1)

                scores(0)
                for r, (kind, t, j, m) in enumerate(PLAN):
                    if r >= 2:
                        pe.wait_ge(t_free, r - 1)
                    if kind == "probs":
                        if m % QPK == 0 and m // QPK + 1 < len(GROUPS):
                            scores(m // QPK + 1)
                        pe.wait_ge(p_ok, m + 1)
                        for b in range(window(t)[1]):
                            last = pe.transpose(core.bank[2 + r % 2][:, b * P:(b + 1) * P],
                                                score[(m // QPK) % 2][:, m % QPK, b * P:(b + 1) * P], core.ident)
                        last.then_inc(t_mm, 1)
                        if m >= 1:
                            values(m - 1)
                    else:
                        if t == NT - 1 and j == 0:
                            values(NT * HQ - 1)
                        pe.wait_ge(o_ok, t + 1)
                        for c in range(4):
                            last = pe.transpose(core.bank[2 + r % 2][:, c * P:(c + 1) * P],
                                                o[t % 2][:, (4 * j + c) * P:(4 * j + c + 1) * P], core.ident)
                        last.then_inc(t_mm, 1)

            @block.scalar
            def _(act):
                def probabilities(g):
                    t, kv = GROUPS[g]
                    act.wait_ge(top_ok, g + 1)
                    h = QPK * kv
                    act.activation(sunk[:, t, h:h + QPK], sunk[:, t, h:h + QPK], ACT.Exp)
                    for c in range(QPK):
                        p = score[g % 2][:, c, 0:window(t)[1] * P]
                        act.activation(p, p, ACT.Exp, bias=neg[:, t, h + c:h + c + 1], scale=SCALE,
                                       accum_out=den[:, t, h + c:h + c + 1]).then_inc(p_ok, 1)

                probabilities(0)
                for r, (kind, t, j, m) in enumerate(PLAN):
                    if kind == "probs" and m % QPK == 0 and m // QPK + 1 < len(GROUPS):
                        probabilities(m // QPK + 1)
                    act.wait_ge(t_mm, r + 1)
                    if kind == "probs":
                        width = window(t)[1] * P
                        if m >= 4:
                            act.wait_ge(pv_mm, m - 3)
                        act.activation(pT[m % 4][:, 0:width], core.bank[2 + r % 2][:, 0:width], ACT.Copy)\
                            .then_inc(t_free, 1)
                    else:
                        act.activation(core.attnT[:, 4 * j:4 * j + 4, t * P:(t + 1) * P],
                                       core.bank[2 + r % 2][:, :].rearrange("p (k t) -> p k t", k=4),
                                       ACT.Copy).then_inc(t_free, 1)

            @block.vector
            def _(dve):
                def tops(g):
                    t, kv = GROUPS[g]
                    lo, n = window(t)
                    h = QPK * kv
                    mask = core.const[:, C_MASK + (lo - t + 1) * P:C_MASK + (lo - t + 1 + n) * P]
                    if g >= 2:
                        dve.wait_ge(t_mm, ORDER["probs", *GROUPS[g - 2], QPK * (g - 2) + QPK - 1] + 1)
                    for c in range(QPK):
                        m = QPK * g + c
                        dve.wait_ge(s_mm, m + 1)
                        dve.tensor_tensor_reduce(score[g % 2][:, c, 0:n * P], core.bank[m % 2][:, 0:n * P], mask,
                                                 1.0, -3e38, ALU.add, ALU.max,
                                                 top[:, t, h + c:h + c + 1]).then_inc(s_read, 1)
                    dve.drain()
                    sink = core.row[:, R_SINK + h:R_SINK + h + QPK]
                    dve.scalar_tensor_tensor(top[:, t, h:h + QPK], top[:, t, h:h + QPK], SCALE, sink,
                                             ALU.mult, ALU.max)
                    dve.drain()
                    dve.tensor_scalar(neg[:, t, h:h + QPK], top[:, t, h:h + QPK], -1.0, None, ALU.mult)
                    dve.tensor_tensor(sunk[:, t, h:h + QPK], sink, top[:, t, h:h + QPK], ALU.subtract)\
                        .then_inc(top_ok, 1)

                def finish(t):
                    dve.wait_ge(p_ok, HQ * (t + 1))
                    dve.tensor_tensor(den[:, t, :], den[:, t, :], sunk[:, t, :], ALU.add)
                    dve.drain()
                    dve.reciprocal(den[:, t, :], den[:, t, :])
                    dve.drain()
                    dve.wait_ge(pv_mm, HQ * (t + 1))
                    if t >= 2:
                        dve.wait_ge(t_mm, ORDER["out", t - 2, 1, 0] + 1)
                    for j in range(2):
                        last = dve.tensor_tensor(
                            o[t % 2][:, j * 512:(j + 1) * 512].rearrange("p (h c) -> p h c", h=8),
                            core.bank[4 + 2 * (t % 2) + j][:, :].rearrange("p (h c) -> p h c", h=8),
                            den[:, t, 8 * j:8 * j + 8].unsqueeze(2).to_broadcast([P, 8, HD]), ALU.mult)
                    last.then_inc(o_ok, 1)

                for g, (t, kv) in enumerate(GROUPS):
                    tops(g)
                    if kv == 1 and t > 0:
                        finish(t - 1)
                finish(NT - 1)


def mix_and_route(core):
    nc = core.nc
    own, sb, sem = open_stage(core)
    NL = NG + NEXP
    with own:
        wo = sb("mix_wo", [P, KD, D])
        wr = sb("mix_wr", [P, KD, NL])
        x = [sb(f"mix_x{u}", [P, D]) for u in range(2)]
        square = sb("mix_square", [P, D])
        mean, rstd = sb("mix_mean", [P, NT]), sb("mix_rstd", [P, NT])
        h2 = sb("mix_h2", [P, NT, D])
        h2T = [sb(f"mix_h2T{u}", [P, KD, P]) for u in range(2)]
        logit = sb("r_logit", [P, NT, NL])
        g_exp, g_pick, cand4 = sb("r_g_exp", [P, NT, NG]), sb("r_g_pick", [P, NT, NG]), sb("r_cand4", [P, NT, NG])
        g_top, g_best, g_w = sb("r_g_top", [P, NT]), sb("r_g_best", [P, NT]), sb("r_g_w", [P, NT])
        spread = sb("r_spread", [P, NT, NG, NE_G])
        e_logit, cand8 = sb("r_e_logit", [P, NT, NE_G]), sb("r_cand8", [P, NT, NE_G])
        e_top, e_best = sb("r_e_top", [P, 2, NT]), sb("r_e_best", [P, NT])
        e_pick = sb("r_e_pick", [P, 2, NT, NE_G])
        ratio = sb("r_ratio", [P, NT])
        takes = sb("r_takes", [P, 2, NT, NEXP])
        both, before = sb("r_both", [P, NT, NEXP]), sb("r_before", [P, NT + 1, NEXP])
        rank, slot = sb("r_rank", [P, NT, NEXP]), sb("r_slot", [P, NT, NEXP])
        counts, over, shift = sb("r_counts", [P, NEXP]), sb("r_over", [P, NEXP]), sb("r_shift", [P, NEXP])
        until = [sb(f"r_until{u}", [P, NEXP]) for u in range(2)]
        place = sb("r_place", [P, 2, NT])
        blocks = sb("r_blocks", [P, NBI, NEXP])
        owner = sb("r_owner", [P, NBI + 1])
        x_in = [sem(f"mix_x_in{u}") for u in range(2)]
        wo_ok, wr_ok, mm, x1_ok, mean_ok, rstd_ok, h2_ok, tr_mm, tr_free, r_mm, logit_ok = (
            sem("mix_wo_ok"), sem("mix_wr_ok"), sem("mix_mm"), sem("mix_x1_ok"), sem("mix_mean_ok"),
            sem("mix_rstd_ok"), sem("mix_h2_ok"), sem("mix_tr_mm"), sem("mix_tr_free"), sem("mix_r_mm"),
            sem("r_logit_ok"))
        exp_in_ok, exp_ok, both_ok, rank_mm, place_ok, scattered = (
            sem("r_exp_in_ok"), sem("r_exp_ok"), sem("r_both_ok"), sem("r_rank_mm"), sem("r_place_ok"),
            sem("r_scattered"))
        with nc.Block() as block:

            @block.sync
            def _(sp):
                sp.dma_start(wo[:, :, :], core.d["w_o"].rearrange("o (k p) n -> (o p) k n", p=P)).then_inc(wo_ok, 16)
                sp.dma_start(wr[:, :, :], core.d["router"].rearrange("(k p) n -> p k n", p=P)).then_inc(wr_ok, 16)
                for t in range(NT):
                    if t >= 2:
                        sp.wait_ge(x1_ok, t - 1)
                    sp.dma_start(x[t % 2][:, :], core.x_tile(t)).then_inc(x_in[t % 2], 16)

            @block.tensor
            def _(pe):
                def mix(t):
                    for j in range(2):
                        n = 2 * t + j
                        if n >= 4:
                            pe.wait_ge(x1_ok, n // 2 - 1)
                        for k in range(KD):
                            last = pe.matmul(core.bank[n % 4][:, :], core.mergedT[:, k, t * P:(t + 1) * P],
                                             wo[:, k, j * 512:(j + 1) * 512], start=(k == 0), stop=(k == KD - 1))
                    last.then_inc(mm, 1)

                def route(t):
                    pe.wait_ge(h2_ok, t + 1)
                    for j in range(2):
                        n = 2 * t + j
                        if n >= 2:
                            pe.wait_ge(tr_free, n - 1)
                        for c in range(4):
                            k = 4 * j + c
                            last = pe.transpose(core.bank[4 + n % 2][:, c * P:(c + 1) * P],
                                                h2[:, t, k * P:(k + 1) * P], core.ident)
                        last.then_inc(tr_mm, 1)
                    pe.wait_ge(tr_free, 2 * t + 2)
                    for k in range(KD):
                        last = pe.matmul(core.bank[6][:, t * NL:(t + 1) * NL], h2T[t % 2][:, k, :], wr[:, k, :],
                                         start=(k == 0), stop=(k == KD - 1))
                    last.then_inc(r_mm, 1)

                pe.wait_ge(wo_ok, 16)
                pe.wait_ge(wr_ok, 16)
                mix(0)
                for t in range(NT):
                    if t + 1 < NT:
                        mix(t + 1)
                    route(t)
                pe.wait_ge(both_ok, 1)
                pe.matmul(core.bank[7][:, 0:NT * NEXP], core.strict, both[:, :, :].rearrange("p t e -> p (t e)"),
                          start=True, stop=False)
                pe.matmul(core.bank[7][:, 0:NT * NEXP], core.ones, before[:, 0:NT, :].rearrange("p t e -> p (t e)"),
                          start=False, stop=True)
                pe.matmul(core.bank[7][:, NT * NEXP:(NT + 1) * NEXP], core.ones, before[:, NT, :],
                          start=True, stop=True).then_inc(rank_mm, 1)

            @block.scalar
            def _(act):
                for t in range(NT):
                    act.wait_ge(x1_ok, t + 1)
                    act.activation(square[:, :], core.x1[:, t, :], ACT.Square, scale=D ** -0.5,
                                   accum_out=mean[:, t:t + 1]).then_inc(mean_ok, 1)
                    act.drain()
                    for j in range(2):
                        n = 2 * t + j
                        act.wait_ge(tr_mm, n + 1)
                        if t >= 2 and j == 0:
                            act.wait_ge(r_mm, t - 1)
                        act.activation(h2T[t % 2][:, 4 * j:4 * j + 4, :],
                                       core.bank[4 + n % 2][:, :].rearrange("p (k t) -> p k t", k=4),
                                       ACT.Copy).then_inc(tr_free, 1)
                act.wait_ge(exp_in_ok, 1)
                act.activation(g_exp[:, :, :], g_exp[:, :, :], ACT.Exp)
                act.activation(ratio[:, :], ratio[:, :], ACT.Exp).then_inc(exp_ok, 1)

            @block.gpsimd
            def _(pool):
                for t in range(NT):
                    pool.wait_ge(mean_ok, t + 1)
                    rsqrt(core, pool, rstd[:, t:t + 1], mean[:, t:t + 1]).then_inc(rstd_ok, 1)
                pool.wait_ge(place_ok, 1)
                for n in range(2):
                    for t in range(NT):
                        pool.indirect_dma_start(
                            out=core.rows_in[:, :],
                            out_offset=bass.IndirectOffsetOnAxis(ap=core.place[:, n * NT + t:n * NT + t + 1], axis=0),
                            in_=h2[:, t, :], in_offset=None).then_inc(scattered, 16)
                pool.wait_ge(scattered, 2 * NT * 16)

            @block.vector
            def _(dve):
                for t in range(NT):
                    dve.wait_ge(mm, t + 1)
                    dve.wait_ge(x_in[t % 2], 16 * (t // 2 + 1))
                    for j in range(2):
                        last = dve.tensor_tensor(core.x1[:, t, j * 512:(j + 1) * 512], core.bank[(2 * t + j) % 4][:, :],
                                                 x[t % 2][:, j * 512:(j + 1) * 512], ALU.add)
                    last.then_inc(x1_ok, 1)
                    dve.wait_ge(rstd_ok, t + 1)
                    dve.scalar_tensor_tensor(h2[:, t, :], core.x1[:, t, :], rstd[:, t:t + 1],
                                             core.row[:, R_FFN:R_FFN + D], ALU.mult, ALU.mult).then_inc(h2_ok, 1)

                def then(*_):
                    dve.drain()

                def along(ap, width):
                    return ap.unsqueeze(ap.ndim).to_broadcast([*ap.shape, width]) if hasattr(ap, "ndim") else ap

                def pick(out, values, peak, order, cand, best):
                    n = values.shape[-1]
                    wide = [P, NT, n]
                    then(dve.tensor_tensor(cand, values, peak.unsqueeze(2).to_broadcast(wide), ALU.is_equal))
                    then(dve.tensor_tensor(cand, cand, order.unsqueeze(1).to_broadcast(wide), ALU.mult))
                    then(dve.tensor_reduce(best, cand, AX.X, ALU.max))
                    then(dve.tensor_tensor(out, cand, best.unsqueeze(2).to_broadcast(wide), ALU.is_equal))

                dve.wait_ge(r_mm, NT)
                bias = core.row[:, R_BR:R_BR + NL].unsqueeze(1).to_broadcast([P, NT, NL])
                then(dve.tensor_tensor(logit[:, :, :],
                                       core.bank[6][:, 0:NT * NL].rearrange("p (t n) -> p t n", t=NT), bias, ALU.add))
                group = logit[:, :, 0:NG]
                then(dve.tensor_reduce(g_top[:, :], group, AX.X, ALU.max))
                pick(g_pick[:, :, :], group, g_top[:, :], core.const[:, C_R4:C_R4 + NG], cand4[:, :, :], g_best[:, :])
                then(dve.tensor_tensor(g_exp[:, :, :], group, g_top[:, :].unsqueeze(2).to_broadcast([P, NT, NG]),
                                       ALU.subtract))
                wide = [P, NT, NG, NE_G]
                then(dve.tensor_tensor(spread[:, :, :, :],
                                       logit[:, :, NG:NL].rearrange("p t (g e) -> p t g e", g=NG),
                                       g_pick[:, :, :].unsqueeze(3).to_broadcast(wide), ALU.mult))
                then(dve.tensor_reduce(e_logit[:, :, :], spread[:, :, :, :].rearrange("p t g e -> p t e g"),
                                       AX.X, ALU.add))
                for n in range(2):
                    then(dve.tensor_reduce(e_top[:, n, :], e_logit[:, :, :], AX.X, ALU.max))
                    pick(e_pick[:, n], e_logit[:, :, :], e_top[:, n, :], core.const[:, C_R8:C_R8 + NE_G],
                         cand8[:, :, :], e_best[:, :])
                    then(dve.tensor_tensor(takes[:, n].rearrange("p t (g e) -> p t g e", g=NG),
                                           g_pick[:, :, :].unsqueeze(3).to_broadcast(wide),
                                           e_pick[:, n].unsqueeze(2).to_broadcast(wide), ALU.mult))
                    if n == 0:
                        then(dve.scalar_tensor_tensor(e_logit[:, :, :], e_pick[:, 0], -BIG, e_logit[:, :, :],
                                                      ALU.mult, ALU.add))
                dve.tensor_tensor(ratio[:, :], e_top[:, 1, :], e_top[:, 0, :], ALU.subtract).then_inc(exp_in_ok, 1)
                then(dve.tensor_tensor(both[:, :, :], takes[:, 0], takes[:, 1], ALU.add),
                     dve.memset(before[:, 0, :], 0.0))
                for t in range(NT):
                    last = dve.tensor_tensor(before[:, t + 1, :], before[:, t, :], both[:, t, :], ALU.add)
                    if t + 1 < NT:
                        dve.drain()
                last.then_inc(both_ok, 1)
                dve.wait_ge(exp_ok, 1)
                then(dve.tensor_reduce(g_w[:, :], g_exp[:, :, :], AX.X, ALU.add))
                then(dve.scalar_tensor_tensor(g_w[:, :], ratio[:, :], 1.0, g_w[:, :], ALU.add, ALU.mult))
                then(dve.reciprocal(core.weight[:, 0:NT], g_w[:, :]))
                then(dve.tensor_tensor(core.weight[:, NT:2 * NT], core.weight[:, 0:NT], ratio[:, :], ALU.mult))
                dve.wait_ge(rank_mm, 1)
                then(dve.tensor_copy(rank[:, :, :], core.bank[7][:, 0:NT * NEXP].rearrange("p (t e) -> p t e", t=NT)),
                     dve.tensor_copy(counts[:, :], core.bank[7][:, NT * NEXP:(NT + 1) * NEXP]))
                then(dve.tensor_scalar(over[:, :], counts[:, :], float(CAP), None, ALU.is_gt))
                for n in range(2, NBLK):
                    then(dve.scalar_tensor_tensor(over[:, :], counts[:, :], float(n * CAP), over[:, :],
                                                  ALU.is_gt, ALU.add))
                then(dve.tensor_copy(until[0][:, :], over[:, :]))
                n, step = 0, 1
                while step < NEXP:
                    a, b = until[n % 2], until[(n + 1) % 2]
                    then(dve.tensor_copy(b[:, 0:step], a[:, 0:step]),
                         dve.tensor_tensor(b[:, step:NEXP], a[:, step:NEXP], a[:, 0:NEXP - step], ALU.add))
                    n, step = n + 1, 2 * step
                until_all = until[n % 2]
                then(dve.tensor_tensor(shift[:, :], until_all[:, :], over[:, :], ALU.subtract))
                then(dve.tensor_scalar(shift[:, :], shift[:, :], float(CAP), float((NEXP - 1) * CAP),
                                       ALU.mult, ALU.add))
                experts_row = core.const[:, C_EC:C_EC + NEXP]
                then(dve.tensor_tensor(shift[:, :], shift[:, :], experts_row, ALU.subtract))
                wide = [P, NT, NEXP]
                then(dve.scalar_tensor_tensor(slot[:, :, :], rank[:, :, :], float(CAP),
                                              shift[:, :].unsqueeze(1).to_broadcast(wide), ALU.is_ge, ALU.mult))
                then(dve.tensor_tensor(slot[:, :, :], slot[:, :, :], rank[:, :, :], ALU.add))
                then(dve.tensor_tensor(slot[:, :, :], slot[:, :, :], experts_row.unsqueeze(1).to_broadcast(wide),
                                       ALU.add))
                for n in range(2):
                    then(dve.tensor_tensor(takes[:, n], takes[:, n], slot[:, :, :], ALU.mult))
                    then(dve.tensor_reduce(place[:, n, :], takes[:, n], AX.X, ALU.add))
                dve.tensor_copy(core.place[:, :], place[:, :, :].rearrange("p n t -> p (n t)")).then_inc(place_ok, 1)
                wide = [P, NBI, NEXP]
                then(dve.tensor_tensor(blocks[:, :, :], until_all[:, :].unsqueeze(1).to_broadcast(wide),
                                       core.const[:, C_BLK:C_BLK + NBI].unsqueeze(2).to_broadcast(wide), ALU.is_le))
                then(dve.tensor_reduce(owner[:, 0:NBI], blocks[:, :, :], AX.X, ALU.add))
                then(dve.tensor_scalar(owner[:, 0:NBI], owner[:, 0:NBI], float(NEXP - 1), None, ALU.min),
                     dve.tensor_copy(owner[:, NBI:NBI + 1], until_all[:, NEXP - 1:NEXP]))
                dve.tensor_copy(core.overflow[:, :], owner[0:1, :])


def experts(core):
    nc = core.nc
    own, sb, sem = open_stage(core)
    with own:
        wg = [sb(f"e_wg{u}", [P, KD, DE]) for u in range(2)]
        wu = [sb(f"e_wu{u}", [P, KD, DE]) for u in range(2)]
        wd = [sb(f"e_wd{u}", [P, KE, D]) for u in range(2)]
        x = [sb(f"e_x{u}", [CAP, D]) for u in range(2)]
        xT = [sb(f"e_xT{u}", [P, KD, CAP]) for u in range(2)]
        silu = [sb(f"e_silu{u}", [P, KE, CAP]) for u in range(2)]
        act_T = [sb(f"e_act{u}", [P, KE, CAP]) for u in range(2)]
        y = [sb(f"e_y{u}", [CAP, D]) for u in range(2)]
        wg_in, wu_in, wd_in, x_in, y_out = (
            [sem(f"{name}{u}") for u in range(2)] for name in ("e_wg_in", "e_wu_in", "e_wd_in", "e_x_in", "e_y_out"))
        tr_mm, xt_ok, gate_mm, up_mm, silu_ok, act_ok, down_mm, y_ok = (
            sem("e_tr_mm"), sem("e_xt_ok"), sem("e_gate_mm"), sem("e_up_mm"), sem("e_silu_ok"), sem("e_act_ok"),
            sem("e_down_mm"), sem("e_y_ok"))

        def one(index):
            return index if isinstance(index, int) else index

        def load_weights(sp, e, u, i, first=False):
            if not first:
                sp.wait_ge(gate_mm, e - 1)
            sp.dma_start(wg[u][:, :, :], core.expert_rows("w_gate", e, KD)).then_inc(wg_in[u], 16)
            if not first:
                sp.wait_ge(tr_mm, e - 1)
            sp.dma_start(x[u][:, :], core.rows_in[bass.ds(e * CAP, CAP), :]).then_inc(x_in[u], 16)
            if not first:
                sp.wait_ge(up_mm, e - 1)
            sp.dma_start(wu[u][:, :, :], core.expert_rows("w_up", e, KD)).then_inc(wu_in[u], 16)
            if not first:
                sp.wait_ge(down_mm, e - 1)
            sp.dma_start(wd[u][:, :, :], core.expert_cols("w_down", e)).then_inc(wd_in[u], 16)

        def pe_transpose(pe, e, u, i, first=False):
            pe.wait_ge(x_in[u], 16 * i + 16)
            if not first:
                pe.wait_ge(xt_ok, e)
            for j in range(2):
                for c in range(4):
                    last = pe.transpose(core.bank[j][:, c * CAP:(c + 1) * CAP], x[u][:, bass.ds(4 * j + c, P, KD)],
                                        core.ident[0:CAP, 0:CAP])
            last.then_inc(tr_mm, 1)

        def pe_gate_up(pe, e, u, i, first=False):
            pe.wait_ge(xt_ok, e + 1)
            if not first:
                pe.wait_ge(act_ok, e - 1)
            for bank, w, w_in, done in ((2 + 2 * u, wg, wg_in, gate_mm), (3 + 2 * u, wu, wu_in, up_mm)):
                pe.wait_ge(w_in[u], 16 * i + 16)
                for j in range(KE):
                    for k in range(KD):
                        last = pe.matmul(core.bank[bank][:, j * CAP:(j + 1) * CAP], w[u][:, k, j * P:(j + 1) * P],
                                         xT[u][:, k, :], start=(k == 0), stop=(k == KD - 1))
                last.then_inc(done, 1)

        def pe_down(pe, e, u, i, first=False):
            pe.wait_ge(wd_in[u], 16 * i + 16)
            pe.wait_ge(act_ok, e + 1)
            if not first:
                pe.wait_ge(y_ok, e)
            for j in range(2):
                for k in range(KE):
                    last = pe.matmul(core.bank[6 + j][0:CAP, :], act_T[u][:, k, :], wd[u][:, k, j * 512:(j + 1) * 512],
                                     start=(k == 0), stop=(k == KE - 1))
            last.then_inc(down_mm, 1)

        def dve_xt(dve, e, u, first=False):
            dve.wait_ge(tr_mm, e + 1)
            if not first:
                dve.wait_ge(up_mm, e - 1)
            for j in range(2):
                last = dve.tensor_copy(xT[u][:, 4 * j:4 * j + 4, :],
                                       core.bank[j][:, 0:4 * CAP].rearrange("p (k r) -> p k r", k=4))
            last.then_inc(xt_ok, 1)

        def dve_act(dve, e, u, first=False):
            dve.wait_ge(silu_ok, e + 1)
            dve.wait_ge(up_mm, e + 1)
            if not first:
                dve.wait_ge(down_mm, e - 1)
            dve.tensor_tensor(act_T[u][:, :, :], silu[u][:, :, :],
                              core.bank[3 + 2 * u][:, 0:KE * CAP].rearrange("p (k r) -> p k r", k=KE),
                              ALU.mult).then_inc(act_ok, 1)

        def act_silu(act, e, u, first=False):
            act.wait_ge(gate_mm, e + 1)
            if not first:
                act.wait_ge(act_ok, e - 1)
            act.activation(silu[u][:, :, :], core.bank[2 + 2 * u][:, 0:KE * CAP]
                           .rearrange("p (k r) -> p k r", k=KE), ACT.Silu).then_inc(silu_ok, 1)

        def act_y(act, e, u, i):
            act.wait_ge(down_mm, e + 1)
            act.wait_ge(y_out[u], 16 * i)
            for j in range(2):
                last = act.activation(y[u][:, j * 512:(j + 1) * 512], core.bank[6 + j][0:CAP, :], ACT.Copy)
            last.then_inc(y_ok, 1)

        def pool_store(pool, e, u):
            pool.wait_ge(y_ok, e + 1)
            pool.dma_start(core.rows_out[bass.ds(e * CAP, CAP), :], y[u][:, :]).then_inc(y_out[u], 16)

        LAST = NEXP // 2 - 1
        with nc.Block() as block:

            @block.sync
            def _(sp):
                for u in range(2):
                    load_weights(sp, u, u, 0, first=True)
                with sp.Fori(1, NEXP // 2) as i:
                    for u in range(2):
                        load_weights(sp, 2 * i + u, u, i)

            @block.tensor
            def _(pe):
                def pair(i, first=False, last=False):
                    for u in range(2):
                        e = 2 * i + u
                        pe_gate_up(pe, e, u, i, first=first)
                        if not (first and u == 0):
                            pe_down(pe, e - 1, 1 - u, i - (1 - u), first=(first and u == 1))
                        if not (last and u == 1):
                            pe_transpose(pe, e + 1, 1 - u, i + u)

                pe_transpose(pe, 0, 0, 0, first=True)
                pair(0, first=True)
                with pe.Fori(1, LAST) as i:
                    pair(i)
                pair(LAST, last=True)
                pe_down(pe, NEXP - 1, 1, LAST)

            @block.vector
            def _(dve):
                def pair(i, first=False, last=False):
                    for u in range(2):
                        e = 2 * i + u
                        dve_act(dve, e, u, first=first)
                        if not (last and u == 1):
                            dve_xt(dve, e + 1, 1 - u, first=(first and u == 0))

                dve_xt(dve, 0, 0, first=True)
                pair(0, first=True)
                with dve.Fori(1, LAST) as i:
                    pair(i)
                pair(LAST, last=True)

            @block.scalar
            def _(act):
                def pair(i, first=False):
                    for u in range(2):
                        e = 2 * i + u
                        act_silu(act, e, u, first=first)
                        if not (first and u == 0):
                            act_y(act, e - 1, 1 - u, i - (1 - u))

                pair(0, first=True)
                with act.Fori(1, NEXP // 2) as i:
                    pair(i)
                act_y(act, NEXP - 1, 1, LAST)

            @block.gpsimd
            def _(pool):
                with pool.Fori(0, NEXP // 2) as i:
                    for u in range(2):
                        pool_store(pool, 2 * i + u, u)
                for u in range(2):
                    pool.wait_ge(y_out[u], 16 * (NEXP // 2))


def overflow_blocks(core):
    nc = core.nc
    own, sb, sem = open_stage(core)
    with own:
        wg, wu = sb("o_wg", [P, KD, DE]), sb("o_wu", [P, KD, DE])
        wd = sb("o_wd", [P, KE, D])
        x, xT = sb("o_x", [CAP, D]), sb("o_xT", [P, KD, CAP])
        silu, act_T = sb("o_silu", [P, KE, CAP]), sb("o_act", [P, KE, CAP])
        y = sb("o_y", [CAP, D])
        loaded, tr_mm, xt_ok, gate_mm, up_mm, silu_ok, act_ok, down_mm, y_ok, y_out = (
            sem(f"o_{n}") for n in ("loaded", "tr_mm", "xt_ok", "gate_mm", "up_mm", "silu_ok", "act_ok",
                                    "down_mm", "y_ok", "y_out"))

        def each_block(eng, body, skipped=None):
            there = eng.value_load(core.overflow[0:1, NBI:NBI + 1], min_val=0, max_val=NOV)
            with eng.Fori(0, NOV) as b:
                with eng.If(there > b):
                    body(b)
                if skipped:
                    with eng.Else():
                        skipped()

        with nc.Block() as block:

            @block.sync
            def _(sp):
                def body(b):
                    e = sp.value_load(core.overflow[0:1, bass.ds(b, 1)], min_val=0, max_val=NEXP - 1)
                    rows = (NEXP + b) * CAP
                    sp.dma_start(wg[:, :, :], core.expert_rows("w_gate", e, KD)).then_inc(loaded, 16)
                    sp.dma_start(x[:, :], core.rows_in[bass.ds(rows, CAP), :]).then_inc(loaded, 16)
                    sp.dma_start(wu[:, :, :], core.expert_rows("w_up", e, KD)).then_inc(loaded, 16)
                    sp.dma_start(wd[:, :, :], core.expert_cols("w_down", e)).then_inc(loaded, 16)
                    sp.wait_ge(y_ok, b + 1)
                    sp.dma_start(core.rows_out[bass.ds(rows, CAP), :], y[:, :]).then_inc(y_out, 16)
                def skipped():
                    sp.sem_inc(y_out, 16)
                each_block(sp, body, skipped)
                sp.wait_ge(y_out, 16 * NOV)

            @block.tensor
            def _(pe):
                def body(b):
                    pe.wait_ge(loaded, 64 * b + 64)
                    for j in range(2):
                        for c in range(4):
                            last = pe.transpose(core.bank[j][:, c * CAP:(c + 1) * CAP],
                                                x[:, bass.ds(4 * j + c, P, KD)], core.ident[0:CAP, 0:CAP])
                    last.then_inc(tr_mm, 1)
                    pe.wait_ge(xt_ok, b + 1)
                    for bank, w, done in ((2, wg, gate_mm), (3, wu, up_mm)):
                        for j in range(KE):
                            for k in range(KD):
                                last = pe.matmul(core.bank[bank][:, j * CAP:(j + 1) * CAP],
                                                 w[:, k, j * P:(j + 1) * P], xT[:, k, :],
                                                 start=(k == 0), stop=(k == KD - 1))
                        last.then_inc(done, 1)
                    pe.wait_ge(act_ok, b + 1)
                    for j in range(2):
                        for k in range(KE):
                            last = pe.matmul(core.bank[6 + j][0:CAP, :], act_T[:, k, :],
                                             wd[:, k, j * 512:(j + 1) * 512], start=(k == 0), stop=(k == KE - 1))
                    last.then_inc(down_mm, 1)
                each_block(pe, body)

            @block.vector
            def _(dve):
                def body(b):
                    dve.wait_ge(tr_mm, b + 1)
                    for j in range(2):
                        last = dve.tensor_copy(xT[:, 4 * j:4 * j + 4, :],
                                               core.bank[j][:, 0:4 * CAP].rearrange("p (k r) -> p k r", k=4))
                    last.then_inc(xt_ok, 1)
                    dve.wait_ge(silu_ok, b + 1)
                    dve.wait_ge(up_mm, b + 1)
                    dve.tensor_tensor(act_T[:, :, :], silu[:, :, :],
                                      core.bank[3][:, 0:KE * CAP].rearrange("p (k r) -> p k r", k=KE),
                                      ALU.mult).then_inc(act_ok, 1)
                each_block(dve, body)

            @block.scalar
            def _(act):
                def body(b):
                    act.wait_ge(gate_mm, b + 1)
                    act.activation(silu[:, :, :], core.bank[2][:, 0:KE * CAP].rearrange("p (k r) -> p k r", k=KE),
                                   ACT.Silu).then_inc(silu_ok, 1)
                    act.wait_ge(down_mm, b + 1)
                    act.wait_ge(y_out, 16 * b)
                    for j in range(2):
                        last = act.activation(y[:, j * 512:(j + 1) * 512], core.bank[6 + j][0:CAP, :], ACT.Copy)
                    last.then_inc(y_ok, 1)
                each_block(act, body)


def combine(core):
    nc = core.nc
    own, sb, sem = open_stage(core)
    with own:
        row = [[sb(f"c_row{n}_{u}", [P, D]) for u in range(2)] for n in range(2)]
        row_in = [[sem(f"c_row_in{n}_{u}") for u in range(2)] for n in range(2)]
        used, out_ok, stored = sem("c_used"), sem("c_out_ok"), sem("c_stored")
        with nc.Block() as block:

            @block.gpsimd
            def _(pool):
                for t in range(NT):
                    if t >= 2:
                        pool.wait_ge(used, t - 1)
                    for n in range(2):
                        at = core.place[:, n * NT + t:n * NT + t + 1]
                        pool.indirect_dma_start(out=row[n][t % 2][:, :], out_offset=None, in_=core.rows_out[:, :],
                                                in_offset=bass.IndirectOffsetOnAxis(ap=at, axis=0))\
                            .then_inc(row_in[n][t % 2], 16)

            @block.vector
            def _(dve):
                for t in range(NT):
                    for n in range(2):
                        dve.wait_ge(row_in[n][t % 2], 16 * (t // 2 + 1))
                        last = dve.scalar_tensor_tensor(core.x1[:, t, :], row[n][t % 2][:, :],
                                                        core.weight[:, n * NT + t:n * NT + t + 1], core.x1[:, t, :],
                                                        ALU.mult, ALU.add)
                        if n == 0:
                            dve.drain()
                    last.then_inc(used, 1)

            @block.sync
            def _(sp):
                for t in range(NT):
                    sp.wait_ge(used, t + 1)
                    sp.dma_start(core.out_tile(t), core.x1[:, t, :]).then_inc(stored, 16)
                sp.wait_ge(stored, 16 * NT)


def build(nc, d, out_prompt, out_sample, stages=None):
    core = Core()
    core.nc, core.d = nc, d
    core.out = (out_prompt, out_sample)
    w_in = d["w_in"].rearrange("o (k p) n -> (o p) k n", p=P)

    def tile_rows(pair, t):
        s = 0 if t < FIRST[1] else 1
        at = (t - FIRST[s]) * P
        return pair[s][0, at:at + P, :]

    core.x_tile = lambda t: tile_rows((d["x_prompt"], d["x_sample"]), t)
    core.out_tile = lambda t: tile_rows(core.out, t)
    core.w_in_cols = lambda col, width: w_in[:, :, bass.ds(col, width)]
    core.rows_in = nc.dram_tensor("rows_in", (ROWS, D), F32, kind="Internal").ap()
    core.rows_out = nc.dram_tensor("rows_out", (ROWS, D), F32, kind="Internal").ap()
    core.y_ssd = nc.dram_tensor("y_ssd", (TOK, DI), F32, kind="Internal").ap()
    core.sums = [nc.dram_tensor(f"decay_sums{u}", (SH, TOK), F32, kind="Internal").ap() for u in range(2)]
    core.expert_rows = lambda name, e, k: (d[name].rearrange("o e (p k) n -> (o e) p k n", k=k)
                                           [bass.ds(e, 1), :, :, :].rearrange("e p k n -> (e p) k n"))
    core.expert_cols = lambda name, e: (d[name].rearrange("o e (k p) n -> (o e) p k n", p=P)
                                        [bass.ds(e, 1), :, :, :].rearrange("e p k n -> (e p) k n"))
    with ExitStack() as life:
        def sb(name, shape, dt=F32, of=life):
            return of.enter_context(nc.sbuf_tensor(name, shape, dt))

        core.const, core.feat, core.row = sb("const", [P, C_N]), sb("feat", [P, P_N]), sb("row", [P, R_N])
        core.place, core.weight = sb("place", [P, 2 * NT], I32), sb("weight", [P, 2 * NT])
        core.overflow = sb("overflow", [1, NBI + 1], I32)
        core.bank = [life.enter_context(nc.psum_tensor(f"bank{n}", [P, 512], F32)) for n in range(8)]
        core.ident, core.upper, core.lower, core.strict, core.ones = (
            core.const[:, c:c + P] for c in (C_ID, C_UP, C_LO, C_SU, C_ONE))
        stream = sb("stream", [P, NT * D])
        core.hT = stream[:, :].rearrange("p (k t) -> p k t", k=KD)
        core.x1 = stream[:, :].rearrange("p (t d) -> p t d", t=NT)
        norm_and_transpose(core)
        with ExitStack() as ssm:
            tables = sb("ssd_tables", [P, 5 * NT * 2, SH], of=ssm)
            core.tables = tables[:, :, :]
            core.tab = {}
            for n, name in enumerate(("dt", "cum", "reach", "to_end", "decay")):
                core.tab[name] = tables[:, n * NT * 2:(n + 1) * NT * 2, :].rearrange("p (t d) h -> p t (d h)", d=2)
            step_sizes(core)
            ssd_groups(core)
        with ExitStack() as mixer:
            core.mergedT = sb("mergedT", [P, KD, TOK], of=mixer)
            with ExitStack() as ssm:
                core.yT = sb("yT", [P, DI // P, TOK], of=ssm)
                gate_and_norm(core)
                merge_branch(core, "ssm", core.yT, d["w_out_ssm"], GS0, True)
            with ExitStack() as attention:
                core.qT, core.kT = sb("qT", [HD, HQ, TOK], of=attention), sb("kT", [HD, HKV, TOK], of=attention)
                core.v = sb("v", [P, NT, HKV * HD], of=attention)
                project_qkv(core)
                core.attnT = sb("attnT", [P, KD, TOK], of=attention)
                attend(core)
                merge_branch(core, "att", core.attnT, d["w_out_attn"], GA0, False)
            mix_and_route(core)
        experts(core)
        overflow_blocks(core)
        combine(core)


_WHOLE = ['x_prompt', 'x_sample', 'w_in', 'w_out_attn', 'w_out_ssm', 'w_o', 'w_gate', 'w_up', 'w_down']


def kernel(**inputs):
    import numpy as _np
    import concourse.bacc as _bacc
    from concourse import mybir as _mybir
    from concourse.bass_utils import run_bass_kernel_spmd as _run

    def a(name):
        return _np.ascontiguousarray(inputs[name])

    def by_feature(v):
        return v.reshape(-1, P).T

    conv = _np.concatenate([a('conv_w')[0], a('conv_b')], 0).T
    conv_groups = _np.concatenate([conv[:DI].reshape(SG, GW // P, P, CW + 1),
                                   conv[DI:DI + SG * NS].reshape(SG, 1, P, CW + 1),
                                   conv[DI + SG * NS:].reshape(SG, 1, P, CW + 1)], 1)
    packed = {
        'constants': pack_constants(),
        'features': _np.concatenate([by_feature(a('norm_mix')[0]), by_feature(a('ssm_norm')[0]),
                                     conv_groups.transpose(2, 0, 1, 3).reshape(P, -1)], 1),
        'rows': _np.concatenate([a('dt_bias_fwd')[0], a('dt_bias_bwd')[0], a('a_log_fwd')[0], a('a_log_bwd')[0],
                                 a('d_skip')[0], a('attn_sink')[0], a('b_router_group')[0],
                                 a('b_router_expert')[0], _np.tile(a('q_norm')[0], HQ),
                                 _np.tile(a('k_norm')[0], HKV), a('norm_ffn')[0]]),
        'router': _np.concatenate([a('w_router_group')[0], a('w_router_expert')[0]], 1),
    }
    nc = _bacc.Bacc("TRN2", target_bir_lowering=False, num_devices=1)
    arrays, d = {}, {}
    for name, v in [(n, a(n)) for n in _WHOLE] + list(packed.items()):
        arrays[f"in_{name}"] = _np.ascontiguousarray(v)
        d[name] = nc.dram_tensor(f"in_{name}", v.shape, _mybir.dt.from_np(v.dtype), kind="ExternalInput").ap()
    outs = [nc.dram_tensor(f"out_{n}", (1, s, D), F32, kind="ExternalOutput").ap() for n, s in enumerate(SEQS)]
    build(nc, d, *outs)
    r = _run(nc, [arrays], core_ids=[0])
    return tuple(r.results[0][f"out_{n}"] for n in range(2))
```

```python
from contextlib import ExitStack

import concourse.bass as bass
import numpy as np
from concourse import mybir

F32 = mybir.dt.float32
I32 = mybir.dt.int32
F32R = mybir.dt.float32r
ALU = mybir.AluOpType
ACT = mybir.ActivationFunctionType
AX = mybir.AxisListType

P = 128
SEQS = (256, 512)
TOK = sum(SEQS)
NT = TOK // P
FIRST = (0, SEQS[0] // P)
TILES = tuple(n // P for n in SEQS)
D = 1024
KD = D // P
EPS = 1e-6
HQ, HKV, HD = 16, 4, 64
QPK = HQ // HKV
HALF = HD // 2
NQK = HQ + HKV
DI = 2 * D
SG, SH, SP_ = 4, 32, 64
HPG = SH // SG
GW = HPG * SP_
NS = 128
CW = 7
PAD = CW // 2
XBC0 = HQ * HD + 2 * HKV * HD + DI
Z0 = HQ * HD + 2 * HKV * HD
DT0 = XBC0 + DI + 2 * SG * NS
GA0 = DT0 + 2 * SH
GS0 = GA0 + D
GC = (GW + 2 * NS) // P
GCOLS = GW + 2 * NS
RAW = sum(n + 2 * PAD for n in SEQS)
CONV = RAW - 2 * PAD
POS = [t * P + (2 * PAD if t >= FIRST[1] else 0) for t in range(NT)]
NG, NE_G, NEXP = 4, 8, 32
DE = 512
KE = DE // P
CAP = 96
NBLK = -(-TOK // CAP)
NOV = (2 * TOK - 1) // CAP
ROWS = (NEXP + NOV) * CAP
BIG = 1e30
SSM_PIECE = SG * GC
QKV_PIECE = SSM_PIECE + DI // P + 3 * D // P
OUT_PIECE = QKV_PIECE + (NQK + HKV) * HD // P
ZW = D // 4
WIDE = 3 * P

C_ID, C_UP, C_LO, C_SU, C_ONE = 0, P, 2 * P, 3 * P, 4 * P
C_MASK = 5 * P
C_COS = C_MASK + WIDE
NPOS = max(SEQS)
C_SIN = C_COS + NPOS
C_MEAN = C_SIN + NPOS
C_SWAP = C_MEAN + P
C_R4 = C_SWAP + P
C_R8 = C_R4 + NG
C_EC = C_R8 + NE_G
C_BLK = C_EC + NEXP
NBI = 16
C_NH = C_BLK + NBI
C_EPS = C_NH + 1
C_N = C_EPS + 1
P_GMIX, P_GSSM, P_CONV = 0, KD, KD + DI // P
P_GQK = P_CONV + SG * GC * (CW + 1)
P_N = P_GQK + NQK * HD // P
R_DTB, R_ALOG, R_SKIP, R_SINK = 0, 64, 128, 160
R_BR = 176
R_FFN = R_BR + NG + NEXP
R_N = R_FFN + D


def pack_constants():
    c = np.zeros((P, C_N), np.float32)
    i = np.arange(P)
    c[:, C_ID:C_ID + P] = np.eye(P)
    c[:, C_UP:C_UP + P] = i[:, None] <= i[None, :]
    c[:, C_LO:C_LO + P] = i[:, None] >= i[None, :]
    c[:, C_SU:C_SU + P] = i[:, None] < i[None, :]
    c[:, C_ONE:C_ONE + P] = 1.0
    c[:, C_MASK:C_MASK + P] = np.where(i[None, :] >= i[:, None], 0.0, -BIG)
    c[:, C_MASK + 2 * P:C_MASK + WIDE] = np.where(i[None, :] <= i[:, None], 0.0, -BIG)
    inv = (1.0 / (np.float32(10000.0) ** (np.arange(0, HD, 2, dtype=np.float32) / np.float32(HD)))).astype(np.float32)
    ang = inv[i % HALF, None] * np.arange(NPOS, dtype=np.float32)[None, :]
    c[:, C_COS:C_COS + NPOS] = np.cos(ang)
    c[:, C_SIN:C_SIN + NPOS] = np.where(i[:, None] % HD < HALF, -np.sin(ang), np.sin(ang))
    c[:, C_MEAN:C_MEAN + P] = (i[:, None] // HD == i[None, :] // HD) / HD
    c[:, C_SWAP:C_SWAP + P] = i[:, None] == (i[None, :] ^ HALF)
    c[:, C_R4:C_R4 + NG] = NG - np.arange(NG)
    c[:, C_R8:C_R8 + NE_G] = NE_G - np.arange(NE_G)
    c[:, C_EC:C_EC + NEXP] = CAP * np.arange(NEXP)
    c[:, C_BLK:C_BLK + NBI] = np.arange(NBI)
    c[:, C_NH] = -0.5
    c[:, C_EPS] = EPS
    return c


class Core:
    pass


def open_stage(core):
    nc, own = core.nc, ExitStack()

    def sb(name, shape, dt=F32):
        return own.enter_context(nc.sbuf_tensor(name, shape, dt))

    def sem(name):
        return own.enter_context(nc.semaphore(name))

    return own, sb, sem


class Pair:

    def __init__(self, sb, name, shape):
        self.high, self.low = sb(f"{name}_high", shape, F32R), sb(f"{name}_low", shape, F32R)


def products(pe, out, lhs, rhs):
    last, n = None, len(lhs)
    for k in range(n):
        for m, (a, b) in enumerate(((0, 0), (0, 1), (1, 0))):
            last = pe.matmul(out, lhs[k][a], rhs[k][b], start=(k == 0 and m == 0), stop=(k == n - 1 and m == 2))
    return last


def h_parts(core, at, width):
    return [(core.h.high[:, k, at:at + width], core.h.low[:, k, at:at + width]) for k in range(KD)]


def by_sequence(s):
    return slice(FIRST[s] * P, FIRST[s] * P + SEQS[s])


def rsqrt(core, pool, out, mean):
    pool.tensor_scalar(mean, mean, EPS, None, ALU.add)
    pool.drain()
    half = core.const[:, C_NH:C_NH + 1].to_broadcast([P, mean.shape[-1]])
    return pool.tensor_tensor(out, mean, half, ALU.pow)


def norm_and_transpose(core):
    nc = core.nc
    own, sb, sem = open_stage(core)
    LOADS = ((0, 1), (1, 1), (2, 2), (4, 2))
    AHEAD = 3
    with own:
        x_all = sb("x_all", [P, NT, D])
        square = sb("norm_square", [P, D])
        mean = sb("norm_mean", [P, NT])
        rstd = sb("norm_rstd", [P, NT])
        h = [sb(f"norm_h{u}", [P, D]) for u in range(2)]
        hT = [sb(f"norm_hT{u}", [P, 4, P]) for u in range(2)]
        x_in = [sem(f"x_in{n}") for n in range(len(LOADS))]
        const_in, mean_ok, rstd_ok = sem("const_in"), sem("mean_ok"), sem("rstd_ok")
        h_ok, tr_done, gained, high_ok, low_ok = (
            sem("h_ok"), sem("tr_done"), sem("h_gained"), sem("h_high_ok"), sem("h_low_ok"))
        with nc.Block() as block:

            @block.sync
            def _(sp):
                for (t, n), x_ok in zip(LOADS, x_in):
                    source = core.d["x_prompt" if t < FIRST[1] else "x_sample"][0]
                    at = (t - (0 if t < FIRST[1] else FIRST[1])) * P
                    sp.dma_start(x_all[:, t:t + n, :], source[at:at + n * P, :].rearrange("(t p) d -> p t d", p=P))\
                        .then_inc(x_ok, 16)
                sp.dma_start(core.w_dt[:, :, :], core.w_in_cols(DT0, 2 * SH)).then_inc(core.w_dt_in, 16)

            @block.scalar
            def _(act):
                act.dma_start(core.const[:, :], core.d["constants"]).then_inc(const_in, 16)
                act.dma_start(core.feat[:, :], core.d["features"]).then_inc(core.params_in, 16)
                act.dma_start(core.row[:, :], core.d["rows"].partition_broadcast(P)).then_inc(core.params_in, 16)

                def squares(t):
                    act.wait_ge(x_in[max(n for n, (t0, _) in enumerate(LOADS) if t0 <= t)], 16)
                    act.activation(square[:, :], x_all[:, t, :], ACT.Square, scale=D ** -0.5,
                                   accum_out=mean[:, t:t + 1]).then_inc(mean_ok, 1)
                    act.drain()

                for t in range(AHEAD):
                    squares(t)
                for t in range(NT):
                    if t + AHEAD < NT:
                        squares(t + AHEAD)
                    for j in range(2):
                        act.wait_ge(gained, 2 * t + j + 1)
                        act.activation(core.h.high[:, 4 * j:4 * j + 4, t * P:(t + 1) * P], hT[j][:, :, :],
                                       ACT.Copy).then_inc(high_ok, 1)

            @block.gpsimd
            def _(pool):
                pool.memset(core.zeros[:, :], 0.0)
                pool.sem_inc(core.pieces.split, 2)
                pool.wait_ge(const_in, 16)

                def roots(t):
                    pool.wait_ge(mean_ok, t + 1)
                    rsqrt(core, pool, rstd[:, t:t + 1], mean[:, t:t + 1]).then_inc(rstd_ok, 1)

                for t in range(AHEAD):
                    roots(t)
                for t in range(NT):
                    if t + AHEAD < NT:
                        roots(t + AHEAD)
                    for j in range(2):
                        pool.wait_ge(high_ok, 2 * t + j + 1)
                        at = (slice(None), slice(4 * j, 4 * j + 4), slice(t * P, (t + 1) * P))
                        pool.tensor_tensor(core.h.low[at], hT[j][:, :, :], core.h.high[at].bitcast(F32),
                                           ALU.subtract).then_inc(low_ok, 1)

            @block.vector
            def _(dve):
                def scaled(t):
                    dve.wait_ge(rstd_ok, t + 1)
                    if t >= 2:
                        dve.wait_ge(tr_done, 2 * (t - 1))
                    dve.tensor_scalar(h[t % 2][:, :], x_all[:, t, :], rstd[:, t:t + 1], None,
                                      ALU.mult).then_inc(h_ok, 1)

                dve.wait_ge(core.params_in, 32)
                scaled(0)
                for t in range(NT):
                    if t + 1 < NT:
                        scaled(t + 1)
                    for j in range(2):
                        n = 2 * t + j
                        dve.wait_ge(tr_done, n + 1)
                        if n >= 2:
                            dve.wait_ge(low_ok, n - 1)
                        gain = core.feat[:, P_GMIX + 4 * j:P_GMIX + 4 * j + 4]
                        dve.tensor_tensor(hT[j][:, :, :], core.bank[n % 8][:, :].rearrange("p (k t) -> p k t", k=4),
                                          gain.unsqueeze(2).to_broadcast([P, 4, P]), ALU.mult).then_inc(gained, 1)

            @block.tensor
            def _(pe):
                pe.sem_inc(core.pieces.used, 2)
                pe.wait_ge(const_in, 16)
                for t in range(NT):
                    pe.wait_ge(h_ok, t + 1)
                    for j in range(2):
                        n = 2 * t + j
                        if n >= 8:
                            pe.wait_ge(gained, n - 7)
                        for k in range(4):
                            last = pe.transpose(core.bank[n % 8][:, k * P:(k + 1) * P],
                                                h[t % 2][:, (4 * j + k) * P:(4 * j + k + 1) * P],
                                                core.ident)
                        last.then_inc(tr_done, 1)


def step_sizes(core):
    nc = core.nc
    own, sb, sem = open_stage(core)
    H2 = 2 * SH
    with own:
        w_pair = Pair(sb, "w_dt", [P, KD, H2])
        raw = sb("dt_raw", [P, NT, H2])
        low = sb("dt_low", [P, NT, H2])
        a = sb("dt_a", [P, NT, H2])
        rate = sb("dt_rate", [P, H2])
        sumT = sb("dt_sumT", [SH, 2, TOK])
        dtT = sb("dt_T", [H2, TOK])
        dtT_mm, dtT_ok = sem("dt_T_mm"), sem("dt_T_ok")
        w_high_ok, w_low_ok = sem("dt_w_high_ok"), sem("dt_w_low_ok")
        dt_mm, raw_ok, soft_ok, rate_ok, a_ok = (
            sem("dt_mm"), sem("dt_raw_ok"), sem("dt_soft_ok"), sem("dt_rate_ok"), sem("dt_a_ok"))
        low_ok, sums_done, exp_in_ok, exp_ok, sumT_ok, sumT_out = (
            sem("dt_low_ok"), sem("dt_sums_done"), sem("dt_exp_in_ok"), sem("dt_exp_ok"),
            sem("dt_sumT_ok"), sem("dt_sumT_out"))
        tab = core.tab
        flat = "p t h -> p (t h)"
        with nc.Block() as block:

            @block.sync
            def _(sp):
                for u in range(2):
                    core.pieces.load(sp, u, u, core.w_in_cols(XBC0 + u * P, P))
                sp.wait_ge(sumT_ok, 2)
                for d in range(2):
                    sp.dma_start(core.sums[d], sumT[:, d, :]).then_inc(sumT_out, 16)
                sp.wait_ge(sumT_out, 32)

            @block.tensor
            def _(pe):
                pe.wait_ge(w_low_ok, 1)
                weights = [(w_pair.high[:, k, :], w_pair.low[:, k, :]) for k in range(KD)]
                for s in range(2):
                    products(pe, core.bank[1 + s][0:H2, 0:SEQS[s]], weights, h_parts(core, FIRST[s] * P, SEQS[s]))\
                        .then_inc(dtT_mm, 1)
                for t in range(NT):
                    s = 0 if t < FIRST[1] else 1
                    pe.wait_ge(dtT_ok, s + 1)
                    last = pe.transpose(core.bank[0][:, t * H2:(t + 1) * H2], dtT[:, t * P:(t + 1) * P],
                                        core.ident[0:H2, 0:H2])
                last.then_inc(dt_mm, 1)
                pe.wait_ge(a_ok, 1)
                tri = (core.upper, core.lower)
                for d in range(2):
                    last = pe.matmul(core.bank[1 + d][:, 0:NT * SH], tri[d],
                                     a[:, :, d * SH:(d + 1) * SH], start=True, stop=True)
                last = pe.matmul(core.bank[3][:, 0:NT * H2], core.ones, a[:, :, :].rearrange(flat),
                                 start=True, stop=True)
                last.then_inc(sums_done, 1)
                for d in range(2):
                    for t in range(NT):
                        last = pe.matmul(core.bank[4 + 2 * d + t // 4][0:SH, (t % 4) * P:(t % 4 + 1) * P],
                                         a[:, t, d * SH:(d + 1) * SH], tri[d], start=True, stop=True)
                    last.then_inc(sums_done, 1)

            @block.scalar
            def _(act):
                act.wait_ge(core.w_dt_in, 16)
                act.activation(w_pair.high[:, :, :], core.w_dt[:, :, :], ACT.Copy).then_inc(w_high_ok, 1)
                act.wait_ge(core.params_in, 32)
                act.activation(rate[:, :], core.row[:, R_ALOG:R_ALOG + H2], ACT.Exp).then_inc(rate_ok, 1)
                for u in range(2):
                    core.pieces.round(act, u, u, 0)
                for s in range(2):
                    act.wait_ge(dtT_mm, s + 1)
                    act.activation(dtT[:, by_sequence(s)], core.bank[1 + s][0:H2, 0:SEQS[s]], ACT.Copy)\
                        .then_inc(dtT_ok, 1)
                act.wait_ge(raw_ok, 1)
                act.activation(low[:, :, :], low[:, :, :], ACT.Exp)
                act.drain()
                act.activation(low[:, :, :], low[:, :, :], ACT.Ln, bias=core.ones[:, 0:1]).then_inc(low_ok, 1)
                act.wait_ge(exp_in_ok, 1)
                for name in ("reach", "to_end", "decay"):
                    last = act.activation(tab[name], tab[name], ACT.Exp)
                last.then_inc(exp_ok, 1)

            @block.gpsimd
            def _(pool):
                for u in range(2):
                    core.pieces.lower(pool, u, u)

            @block.vector
            def _(dve):
                dve.wait_ge(w_high_ok, 1)
                dve.tensor_tensor(w_pair.low[:, :, :], core.w_dt[:, :, :], w_pair.high[:, :, :].bitcast(F32),
                                  ALU.subtract).then_inc(w_low_ok, 1)
                dve.wait_ge(dt_mm, 1)
                dve.wait_ge(core.params_in, 32)
                bias = core.row[:, R_DTB:R_DTB + H2].unsqueeze(1).to_broadcast([P, NT, H2])
                dve.tensor_tensor(raw[:, :, :], core.bank[0][:, 0:NT * H2].rearrange("p (t h) -> p t h", t=NT),
                                  bias, ALU.add)
                dve.drain()
                dve.scalar_tensor_tensor(low[:, :, :], raw[:, :, :], -1.0, raw[:, :, :], ALU.mult, ALU.min)\
                    .then_inc(raw_ok, 1)
                dve.wait_ge(low_ok, 1)
                dve.scalar_tensor_tensor(tab["dt"], raw[:, :, :], 0.0, low[:, :, :], ALU.max, ALU.add)
                dve.drain()
                dve.wait_ge(rate_ok, 1)
                dve.scalar_tensor_tensor(a[:, :, :], tab["dt"], -1.0,
                                         rate[:, :].unsqueeze(1).to_broadcast([P, NT, H2]),
                                         ALU.mult, ALU.mult).then_inc(a_ok, 1)
                dve.wait_ge(sums_done, 1)
                for d in range(2):
                    psum = core.bank[1 + d][:, 0:NT * SH].rearrange("p (t h) -> p t h", t=NT)
                    dve.tensor_copy(tab["cum"][:, :, d * SH:(d + 1) * SH], psum)
                total = core.bank[3][:, 0:NT * H2].rearrange("p (t h) -> p t h", t=NT)
                dve.tensor_copy(tab["decay"], total)
                dve.drain()
                dve.tensor_copy(tab["reach"], tab["cum"])
                dve.tensor_tensor(tab["to_end"], tab["decay"], tab["cum"], ALU.subtract).then_inc(exp_in_ok, 1)
                for d in range(2):
                    dve.wait_ge(sums_done, 2 + d)
                    dve.tensor_copy(sumT[:, d, 0:4 * P], core.bank[4 + 2 * d][0:SH, :])
                    dve.tensor_copy(sumT[:, d, 4 * P:TOK], core.bank[5 + 2 * d][0:SH, 0:TOK - 4 * P])\
                        .then_inc(sumT_ok, 1)
                dve.wait_ge(exp_ok, 1)
                dve.tensor_tensor(tab["to_end"], tab["to_end"], tab["dt"], ALU.mult)


class Pieces:

    def __init__(self, core, raw, pair, first):
        self.core, self.first, self.raw, self.pair = core, first, raw, pair
        self.loaded, self.rounded, self.split, self.used = core.piece_sems

    def of_stage(self, first):
        return Pieces(self.core, self.raw, self.pair, first)

    def load(self, sp, n, u, columns):
        sp.wait_ge(self.split, self.first + n + 1)
        sp.dma_start(self.raw[u][:, :, :], columns).then_inc(self.loaded[u], 16)

    def round(self, act, n, u, turn):
        act.wait_ge(self.loaded[u], 16 * (self.first // 2 + turn) + 16)
        act.wait_ge(self.used, self.first + n + 1)
        act.activation(self.pair[u].high[:, :, :], self.raw[u][:, :, :], ACT.Copy).then_inc(self.rounded, 1)

    def lower(self, pool, n, u):
        pool.wait_ge(self.rounded, self.first + n + 1)
        pool.tensor_tensor(self.pair[u].low[:, :, :], self.raw[u][:, :, :], self.pair[u].high[:, :, :].bitcast(F32),
                           ALU.subtract).then_inc(self.split, 1)

    def ready(self, pe, n):
        pe.wait_ge(self.split, self.first + n + 3)

    def release(self, pe):
        pe.drain().then_inc(self.used, 1)

    def parts(self, u):
        return [(self.pair[u].high[:, k, :], self.pair[u].low[:, k, :]) for k in range(KD)]


def new_pieces(core, sb, name, first):
    return Pieces(core, [sb(f"{name}_raw{u}", [P, KD, P]) for u in range(2)],
                  [Pair(sb, f"{name}_w{u}", [P, KD, P]) for u in range(2)], first)


def ssd_groups(core):
    nc = core.nc
    own, sb, sem = open_stage(core)
    STATES = []
    for d in range(2):
        for s in range(2):
            chunks = list(range(FIRST[s], FIRST[s] + TILES[s]))
            chunks = chunks if d == 0 else chunks[::-1]
            STATES += [(t, d, n == 0) for n, t in enumerate(chunks[:-1])]
    ENTERS = {(t + 1 if d == 0 else t - 1, d): n for n, (t, d, _) in enumerate(STATES)}
    NST = len(STATES)
    NY = NDEC = 3
    TABLES = ("dt", "cum", "reach", "to_end", "decay")
    HALVES = ((0, 4), (4, NT - 4))
    assert GC == NT and NT % NY == 0
    with own:
        w, following = core.pieces, core.pieces.of_stage(SSM_PIECE)
        raw = [sb(f"ssd_conv_in{u}", [P, RAW]) for u in range(2)]
        xc = sb("ssd_xc", [P, GC, CONV])
        cT = sb("ssd_cT", [P, CONV])
        xs = sb("ssd_xs", [P, NT, GW])
        b_tok = sb("ssd_b", [P, NT, NS])
        cb = sb("ssd_cb", [P, 2, NT, P])
        decays = [sb(f"ssd_decays{u}", [P, 2, HPG, P]) for u in range(NDEC)]
        x_dt = [sb(f"ssd_x_dt{u}", [P, 2, GW]) for u in range(2)]
        x_end = [sb(f"ssd_x_end{u}", [P, GW]) for u in range(2)]
        state = sb("ssd_state", [P, NST, GW])
        y = [sb(f"ssd_y{u}", [P, GW]) for u in range(NY)]
        part = sb("ssd_part", [P, GW])
        tabs = sb("ssd_tabs", [P, len(TABLES), NT, 2, HPG])
        conv_p = sb("ssd_conv_p", [P, GC, CW + 1])
        gt = {name: tabs[:, n] for n, name in enumerate(TABLES)}

        proj_mm, left, conv_done, silu_done, pads_ok, conv_p_ok = (
            sem("ssd_proj_mm"), sem("ssd_left"), sem("ssd_conv_done"), sem("ssd_silu_done"), sem("ssd_pads_ok"),
            sem("ssd_conv_p_ok"))
        tr_mm, tr_left, cb_mm, cb_ok, cT_ok = (
            sem("ssd_tr_mm"), sem("ssd_tr_left"), sem("ssd_cb_mm"), sem("ssd_cb_ok"),
            sem("ssd_cT_ok"))
        xend_ok, st_mm, st_ok, xdt_ok = sem("ssd_xend_ok"), sem("ssd_st_mm"), sem("ssd_st_ok"), sem("ssd_xdt_ok")
        sums_in = [sem(f"ssd_sums_in{u}") for u in range(NDEC)]
        diff_ok, capped, exp_ok, decay_ok, y_mm, y_ok = (
            sem("ssd_diff_ok"), sem("ssd_capped"), sem("ssd_exp_ok"), sem("ssd_decay_ok"), sem("ssd_y_mm"),
            sem("ssd_y_ok"))
        y_out = [sem(f"ssd_y_out{u}") for u in range(NY)]

        def off_banks(t):
            return (4, 5) if t % 2 == 0 else (6, 7)

        def heads(ap, width):
            return ap.unsqueeze(2).to_broadcast([P, HPG, width])

        def by_head(ap):
            return ap.rearrange("p (e c) -> p e c", e=HPG)

        def column(g, ct):
            if ct < GW // P:
                return XBC0 + ct * P + g * GW
            return XBC0 + DI + (SG * NS if ct > GW // P else 0) + g * NS

        def groups(eng, scan):
            with eng.Fori(0, SG - 2) as g:
                scan(g, True, True)
            scan(SG - 2, True, False)
            scan(SG - 1, False, False)

        with nc.Block() as block:

            @block.sync
            def _(sp):
                def load(g, ct):
                    w.load(sp, GC * g + ct, ct % 2, core.w_in_cols(column(g, ct), P))

                def load_sums(g, t):
                    sums = [core.sums[d][bass.ds(g * HPG, HPG), t * P:(t + 1) * P] for d in range(2)]
                    sp.wait_ge(y_mm, NT * g + t + NT - 2)
                    for d in range(2):
                        sp.dma_start(decays[t % NDEC][:, d, :, :], sums[d].partition_broadcast(P))\
                            .then_inc(sums_in[t % NDEC], 16)

                def store(g, t):
                    into = core.y_ssd[t * P:(t + 1) * P, bass.ds(g * GW, GW)]
                    sp.wait_ge(y_ok, NT * g + NT + t + 1)
                    sp.dma_start(into, y[t % NY][:, :])\
                        .then_inc(y_out[t % NY], 16)

                def scan(g, more, ahead):
                    if not more:
                        for u in range(2):
                            following.load(sp, u, u, core.w_in_cols(Z0 + u * P, P))
                    for t in range(NDEC):
                        load_sums(g, t)
                    for t in range(NT):
                        if more and t + 2 < GC:
                            load(g + 1, t + 2)
                        if ahead and t + 2 >= GC:
                            load(g + 2, t + 2 - GC)
                        if t:
                            store(g, t - 1)
                        if t + NDEC < NT:
                            load_sums(g, t + NDEC)
                    store(g, NT - 1)

                for n in range(2, GC + 2):
                    load(n // GC, n % GC)
                groups(sp, scan)
                for u in range(NY):
                    sp.wait_ge(y_out[u], 16 + SG * (NT // NY) * 16)

            @block.tensor
            def _(pe):
                def project(g, ct):
                    w.ready(pe, GC * g + ct)
                    for s in range(2):
                        pe.wait_ge(left, 2 * (GC * g + ct) + s + 1)
                        last = products(pe, core.bank[s][:, 0:SEQS[s]], w.parts(ct % 2),
                                        h_parts(core, FIRST[s] * P, SEQS[s]))
                        last.then_inc(proj_mm, 1)
                    w.release(pe)

                def scan(g, more, ahead):
                    pe.wait_ge(silu_done, GC * g + 4)
                    pe.wait_ge(y_ok, NT * g + NT - 1)
                    for t in range(NT):
                        if t >= 2:
                            pe.wait_ge(tr_left, 8 * g + t - 1)
                        for c in range(4):
                            last = pe.transpose(core.bank[4 + t % 2][:, c * P:(c + 1) * P],
                                                xc[:, c, POS[t]:POS[t] + P], core.ident)
                        last.then_inc(tr_mm, 1)
                    pe.wait_ge(silu_done, GC * g + 5)
                    for j, (t0, n) in enumerate(HALVES):
                        pe.wait_ge(tr_left, 8 * g + 5 + j)
                        for t in range(t0, t0 + n):
                            last = pe.transpose(core.bank[4 + j][:, (t % 4) * P:(t % 4 + 1) * P],
                                                xc[:, 4, POS[t]:POS[t] + P], core.ident)
                        last.then_inc(tr_mm, 1)
                    pe.wait_ge(silu_done, GC * g + 6)
                    pe.wait_ge(y_ok, NT * g + NT)
                    for j, (t0, n) in enumerate(HALVES):
                        for t in range(t0, t0 + n):
                            last = pe.matmul(core.bank[6 + j][:, (t % 4) * P:(t % 4 + 1) * P],
                                             xc[:, 4, POS[t]:POS[t] + P], xc[:, 5, POS[t]:POS[t] + P],
                                             start=True, stop=True)
                        last.then_inc(cb_mm, 1)
                    pe.wait_ge(tr_left, 8 * g + 8)
                    for n, (t, d, _) in enumerate(STATES):
                        pe.wait_ge(xend_ok, NST * g + n + 1)
                        if n >= 2:
                            pe.wait_ge(st_ok, NST * g + n - 1)
                        pe.matmul(core.bank[2 + n % 2][:, :], b_tok[:, t, :], x_end[n % 2][:, :],
                                  start=True, stop=True).then_inc(st_mm, 1)
                    pe.wait_ge(cb_ok, 2 * g + 2)
                    pe.wait_ge(st_ok, NST * g + NST)
                    pe.wait_ge(cT_ok, g + 1)
                    for t in range(NT):
                        if more:
                            project(g + 1, t)
                        if t >= 2:
                            pe.wait_ge(y_ok, NT * g + NT + t - 1)
                        for d in range(2):
                            if (t, d) in ENTERS:
                                pe.matmul(core.bank[off_banks(t)[d]][:, :], cT[:, POS[t]:POS[t] + P],
                                          state[:, ENTERS[t, d], :], start=True, stop=True)
                        pe.wait_ge(decay_ok, NT * g + t + 1)
                        pe.wait_ge(xdt_ok, NT * g + t + 1)
                        for e in range(HPG):
                            for d in range(2):
                                last = pe.matmul(core.bank[2 + t % 2][:, e * SP_:(e + 1) * SP_],
                                                 decays[t % NDEC][:, d, e, :],
                                                 x_dt[t % 2][:, d, e * SP_:(e + 1) * SP_],
                                                 start=(d == 0), stop=(d == 1))
                        last.then_inc(y_mm, 1)

                pe.sem_inc(y_mm, NT)
                for ct in range(GC):
                    project(0, ct)
                groups(pe, scan)

            @block.scalar
            def _(act):
                def leave(g, ct):
                    act.wait_ge(conv_done, GC * g + ct + 1)
                    for s in range(2):
                        act.wait_ge(proj_mm, 2 * (GC * g + ct) + s + 1)
                        at = FIRST[s] * P + PAD + 2 * PAD * s
                        act.activation(raw[ct % 2][:, at:at + SEQS[s]], core.bank[s][:, 0:SEQS[s]],
                                       ACT.Copy).then_inc(left, 1)

                def round_piece(g, ct):
                    w.round(act, GC * g + ct, ct % 2, GC // 2 * g + ct // 2)

                def silu(g, ct):
                    act.wait_ge(conv_done, GC * g + ct + 3)
                    act.activation(xc[:, ct, :], xc[:, ct, :], ACT.Silu).then_inc(silu_done, 1)

                def decay(g, t):
                    act.wait_ge(capped, NT * g + t + 1)
                    act.activation(decays[t % NDEC][:, :, :, :], decays[t % NDEC][:, :, :, :], ACT.Exp).then_inc(exp_ok, 1)

                def scan(g, more, ahead):
                    for t in range(NT):
                        act.wait_ge(tr_mm, 8 * g + t + 1)
                        act.activation(xs[:, t, :], core.bank[4 + t % 2][:, :], ACT.Copy).then_inc(tr_left, 1)
                    silu(g, GC - 2)
                    silu(g, GC - 1)
                    for j, (t0, n) in enumerate(HALVES):
                        act.wait_ge(tr_mm, 8 * g + NT + j + 1)
                        act.activation(b_tok[:, t0:t0 + n, :],
                                       core.bank[4 + j][:, 0:n * P].rearrange("p (t c) -> p t c", t=n),
                                       ACT.Copy).then_inc(tr_left, 1)
                    act.drain()
                    act.activation(cT[:, :], xc[:, GC - 1, :], ACT.Copy).then_inc(cT_ok, 1)
                    decay(g, 0)
                    for t in range(NT):
                        if t + 1 < NT:
                            decay(g, t + 1)
                        if more:
                            leave(g + 1, t)
                            if t + 2 < GC:
                                round_piece(g + 1, t + 2)
                            elif ahead:
                                round_piece(g + 2, t + 2 - GC)
                            if 0 < t < GC - 1:
                                silu(g + 1, t - 1)

                act.sem_inc(left, 2)
                act.wait_ge(pads_ok, 1)
                for ct in range(GC):
                    leave(0, ct)
                    round_piece((ct + 2) // GC, (ct + 2) % GC)
                    if 0 < ct < GC - 1:
                        silu(0, ct - 1)
                groups(act, scan)
                for u in range(2):
                    following.round(act, u, u, 0)

            @block.gpsimd
            def _(pool):
                def table(g, name, t, d):
                    return core.tables[:, (TABLES.index(name) * NT + t) * 2 + d, bass.ds(g * HPG, HPG)]

                def lower(g, ct):
                    w.lower(pool, GC * g + ct, ct % 2)

                def differences(g, t):
                    pool.wait_ge(sums_in[t % NDEC], NT // NDEC * 32 * g + 32 * (t // NDEC) + 32)
                    for d in range(2):
                        last = pool.tensor_tensor(decays[t % NDEC][:, d, :, :], decays[t % NDEC][:, d, :, :],
                                                  heads(table(g, "cum", t, d), P), ALU.subtract)
                    last.then_inc(diff_ok, 1)

                def inputs(g, t):
                    pool.wait_ge(y_mm, NT * g + t + NT - 1)
                    pool.wait_ge(y_out[t % NY], 16 * (NT // NY) * g + 16 * (t // NY) + 16)
                    for d in range(2):
                        pool.tensor_tensor(by_head(x_dt[t % 2][:, d, :]), by_head(xs[:, t, :]),
                                           heads(table(g, "dt", t, d), SP_), ALU.mult)
                    pool.tensor_tensor(by_head(y[t % NY][:, :]), by_head(xs[:, t, :]),
                                       heads(core.row[:, bass.ds(R_SKIP + g * HPG, HPG)], SP_), ALU.mult).then_inc(xdt_ok, 1)

                def scan(g, more, ahead):
                    differences(g, 0)
                    for n, (t, d, _) in enumerate(STATES):
                        pool.wait_ge(tr_left, 8 * g + t + 1)
                        if n >= 2:
                            pool.wait_ge(st_mm, NST * g + n - 1)
                        pool.tensor_tensor(by_head(x_end[n % 2][:, :]), by_head(xs[:, t, :]),
                                           heads(table(g, "to_end", t, d), SP_), ALU.mult).then_inc(xend_ok, 1)
                    inputs(g, 0)
                    differences(g, 1)
                    for t in range(NT):
                        if t + 2 < NT:
                            differences(g, t + 2)
                        if t + 1 < NT:
                            inputs(g, t + 1)
                        if more and t + 2 < GC:
                            lower(g + 1, t + 2)
                        if ahead and t + 2 >= GC:
                            lower(g + 2, t + 2 - GC)

                for u in range(NY):
                    pool.sem_inc(y_out[u], 16)
                for n in range(2, GC + 2):
                    lower(n // GC, n % GC)
                groups(pool, scan)
                for u in range(2):
                    following.lower(pool, u, u)

            @block.vector
            def _(dve):
                def parameters(g):
                    dve.tensor_copy(conv_p[:, :, :], core.feat[:, bass.ds(P_CONV + g * (GC * (CW + 1)), GC * (CW + 1))]
                                    .rearrange("p (c k) -> p c k", c=GC))
                    dve.drain()

                def convolve(g, ct):
                    dve.wait_ge(left, 2 * (GC * g + ct) + 4)
                    x = raw[ct % 2]
                    dve.tensor_scalar(xc[:, ct, :], x[:, 0:CONV], conv_p[:, ct, 0:1],
                                      conv_p[:, ct, CW:CW + 1], ALU.mult, ALU.add)
                    for k in range(1, CW):
                        dve.drain()
                        last = dve.scalar_tensor_tensor(xc[:, ct, :], x[:, k:k + CONV], conv_p[:, ct, k:k + 1],
                                                        xc[:, ct, :], ALU.mult, ALU.add)
                    last.then_inc(conv_done, 1)

                def cap(g, t):
                    dve.wait_ge(diff_ok, NT * g + t + 1)
                    flat = decays[t % NDEC][:, :, :, :].rearrange("p d e l -> p (d e l)")
                    dve.tensor_scalar(flat, flat, 0.0, None, ALU.min).then_inc(capped, 1)

                def decay(g, t):
                    dve.wait_ge(exp_ok, NT * g + t + 1)
                    for d in range(2):
                        last = dve.tensor_tensor(decays[t % NDEC][:, d, :, :], decays[t % NDEC][:, d, :, :],
                                                 cb[:, d, t, :].unsqueeze(1).to_broadcast([P, HPG, P]), ALU.mult)
                    last.then_inc(decay_ok, 1)

                def output(g, t):
                    dve.wait_ge(y_mm, NT * g + NT + t + 1)
                    out = y[t % NY][:, :]
                    last = dve.tensor_tensor(out, out, core.bank[2 + t % 2][:, :], ALU.add)
                    for d in range(2):
                        if (t, d) in ENTERS:
                            dve.tensor_tensor(by_head(part[:, :]), by_head(core.bank[off_banks(t)[d]][:, :]),
                                              heads(gt["reach"][:, t, d, :], SP_), ALU.mult)
                            dve.drain()
                            last = dve.tensor_tensor(out, out, part[:, :], ALU.add)
                            dve.drain()
                    last.then_inc(y_ok, 1)

                def tables(g):
                    dve.tensor_copy(tabs[:, :, :, :, :].rearrange("p n t d h -> p (n t d) h"),
                                    core.tables[:, :, bass.ds(g * HPG, HPG)])

                def scan(g, more, ahead):
                    if more:
                        parameters(g + 1)
                    for j, (t0, n) in enumerate(HALVES):
                        dve.wait_ge(cb_mm, 2 * g + j + 1)
                        psum = core.bank[6 + j][:, 0:n * P].rearrange("p (t c) -> p t c", t=n)
                        for d, tri in enumerate((core.upper, core.lower)):
                            last = dve.tensor_tensor(cb[:, d, t0:t0 + n, :], psum,
                                                     tri.unsqueeze(1).to_broadcast([P, n, P]), ALU.mult)
                        last.then_inc(cb_ok, 1)
                    cap(g, 0)
                    for n, (t, d, opens) in enumerate(STATES):
                        dve.wait_ge(st_mm, NST * g + n + 1)
                        if opens:
                            dve.tensor_copy(state[:, n, :], core.bank[2 + n % 2][:, :]).then_inc(st_ok, 1)
                        else:
                            dve.tensor_tensor(by_head(part[:, :]), by_head(state[:, n - 1, :]),
                                              heads(gt["decay"][:, t, d, :], SP_), ALU.mult)
                            dve.drain()
                            dve.tensor_tensor(state[:, n, :], part[:, :], core.bank[2 + n % 2][:, :], ALU.add)\
                                .then_inc(st_ok, 1)
                        dve.drain()
                    for t in range(NT):
                        decay(g, t)
                        if t + 1 < NT:
                            cap(g, t + 1)
                        if t:
                            output(g, t - 1)
                        if more:
                            convolve(g + 1, t)
                    output(g, NT - 1)
                    if more:
                        tables(g + 1)
                    dve.drain()

                dve.sem_inc(y_ok, NT)
                dve.sem_inc(conv_done, 2)
                for u in range(2):
                    for s in range(2):
                        at = FIRST[s] * P + 2 * PAD * s
                        dve.memset(raw[u][:, at:at + PAD], 0.0)
                        last = dve.memset(raw[u][:, at + PAD + SEQS[s]:at + 2 * PAD + SEQS[s]], 0.0)
                last.then_inc(pads_ok, 1)
                parameters(0)
                tables(0)
                for ct in range(GC):
                    convolve(0, ct)
                dve.drain()
                groups(dve, scan)


def pair_of_tiles(ap, i, u):
    return (ap.rearrange("p k (i u c) -> u p k i c", u=2, c=P)[u][:, :, bass.ds(i, 1), :]
            .rearrange("p k i c -> p k (i c)"))


def transposed_products(pe, core, w, u, rhs, done):
    for s in range(2):
        tokens = by_sequence(s)
        parts = [(rhs.high[:, k, tokens], rhs.low[:, k, tokens]) for k in range(KD)]
        products(pe, core.bank[2 * u + s][:, 0:SEQS[s]], w.parts(u), parts).then_inc(done, 1)


class GatedOutput:

    def __init__(self, core, sb, sem, w, name, first_piece):
        self.core, self.w, self.first = core, w, first_piece
        self.gate = [sb(f"{name}_gate{u}", [P, TOK]) for u in range(2)]
        self.mm, self.sig_ok, self.merged = sem(f"{name}_mm"), sem(f"{name}_sig_ok"), sem(f"{name}_merged")

    def pe_gate(self, pe, c):
        self.w.ready(pe, self.first + 2 * c)
        pe.wait_ge(self.sig_ok, c + 1)
        transposed_products(pe, self.core, self.w, 0, self.core.h, self.mm)
        self.w.release(pe)

    def pe_branch(self, pe, c, branch):
        self.w.ready(pe, self.first + 2 * c + 1)
        pe.wait_ge(self.merged, c + 1)
        transposed_products(pe, self.core, self.w, 1, branch, self.mm)
        self.w.release(pe)

    def act_tile(self, act, c, v):
        act.wait_ge(self.mm, 4 * c + 2)
        act.wait_ge(self.merged, c + 1)
        for s in range(2):
            last = act.activation(self.gate[v][:, by_sequence(s)], self.core.bank[s][:, 0:SEQS[s]], ACT.Sigmoid)
        last.then_inc(self.sig_ok, 1)


def ssm_branch(core):
    nc = core.nc
    own, sb, sem = open_stage(core)
    HALF_Z = DI // P // 2
    OUT = D // P
    assert HALF_Z == KD and OUT == KD
    Z = (0, HALF_Z + OUT)
    O0, G0 = HALF_Z, 2 * HALF_Z + OUT
    w_out = core.d["w_out_ssm"].rearrange("o (f k p) n -> (o p) f k n", p=P, f=2)
    with own:
        w, following = core.pieces.of_stage(SSM_PIECE), core.pieces.of_stage(QKV_PIECE)
        yb = [sb(f"ssm_yb{u}", [P, NT, P]) for u in range(2)]
        zs = [sb(f"ssm_zs{u}", [P, TOK]) for u in range(2)]
        square, total, rstd = sb("ssm_square", [P, TOK]), sb("ssm_total", [P, TOK]), sb("ssm_rstd", [P, TOK])
        y = Pair(sb, "ssm_y", [P, KD, TOK])
        out = GatedOutput(core, sb, sem, w, "ssm", G0)
        yb_in = [sem(f"ssm_yb_in{u}") for u in range(2)]
        z_mm, tr_mm, silu_ok, gated, high_ok, sq_ok, summed, y_ok = (
            sem("ssm_z_mm"), sem("ssm_tr_mm"), sem("ssm_silu_ok"), sem("ssm_gated"), sem("ssm_high_ok"),
            sem("ssm_sq_ok"), sem("ssm_summed"), sem("ssm_y_ok"))
        o_mm, o_left, mean_mm, roots_ok = (
            sem("ssm_o_mm"), sem("ssm_o_left"), sem("ssm_mean_mm"), sem("ssm_roots_ok"))

        with nc.Block() as block:

            @block.sync
            def _(sp):
                def z_tile(f, i, u, loaded=False):
                    ct = HALF_Z * f + 2 * i + u
                    if not loaded:
                        w.load(sp, Z[f] + 2 * i + u, u, core.w_in_cols(Z0 + ct * P, P))
                    y_tiles = core.y_ssd.rearrange("(t p) c -> p t c", p=P)
                    columns = y_tiles[:, :, ct * P:(ct + 1) * P] if loaded else \
                        pair_of_tiles(y_tiles, HALF_Z // 2 * f + i, u)
                    sp.wait_ge(tr_mm, ct + 1)
                    sp.dma_start(yb[u][:, :, :], columns).then_inc(yb_in[u], 16)

                def z_half(f):
                    for u in range(2):
                        z_tile(f, 0, u, loaded=(f == 0))
                    with sp.Fori(1, HALF_Z // 2) as i:
                        for u in range(2):
                            z_tile(f, i, u)

                z_half(0)
                with sp.Fori(0, OUT // 2) as i:
                    for u in range(2):
                        w.load(sp, O0 + 2 * i + u, u, w_out[:, 0, :, bass.ds((2 * i + u) * P, P)])
                z_half(1)
                with sp.Fori(0, OUT) as c:
                    w.load(sp, G0 + 2 * c, 0, core.w_in_cols(GS0 + c * P, P))
                    w.load(sp, G0 + 2 * c + 1, 1, w_out[:, 1, :, bass.ds(c * P, P)])
                for u in range(2):
                    following.load(sp, u, u, core.w_in_cols(u * P, P))

            @block.tensor
            def _(pe):
                def z_half(f):
                    with pe.Fori(0, HALF_Z // 2) as i:
                        for u in range(2):
                            ct = HALF_Z * f + 2 * i + u
                            w.ready(pe, Z[f] + 2 * i + u)
                            pe.wait_ge(silu_ok, ct + 1)
                            transposed_products(pe, core, w, u, core.h, z_mm)
                            w.release(pe)
                            pe.wait_ge(yb_in[u], 16 * (HALF_Z // 2 * f + i) + 16)
                            pe.wait_ge(gated, ct + 1)
                            for t in range(NT):
                                bank, at = (0, t * P) if t < FIRST[1] else (1, (t - FIRST[1]) * P)
                                last = pe.transpose(core.bank[4 + 2 * u + bank][:, at:at + P], yb[u][:, t, :],
                                                    core.ident)
                            last.then_inc(tr_mm, 1)

                pe.sem_inc(tr_mm, 2)
                pe.sem_inc(o_mm, 2)
                z_half(0)
                pe.wait_ge(silu_ok, HALF_Z + 2)
                pe.wait_ge(y_ok, HALF_Z)
                with pe.Fori(0, OUT // 2) as i:
                    for u in range(2):
                        w.ready(pe, O0 + 2 * i + u)
                        pe.wait_ge(o_left, 2 * i + u + 1)
                        transposed_products(pe, core, w, u, y, o_mm)
                        w.release(pe)
                pe.wait_ge(o_left, OUT + 2)
                z_half(1)
                pe.wait_ge(silu_ok, 2 * HALF_Z + 2)
                out.pe_gate(pe, 0)
                pe.wait_ge(gated, 2 * HALF_Z + 2)
                pe.wait_ge(summed, 2 * HALF_Z + 1)
                for s in range(2):
                    last = pe.matmul(core.bank[4 + s][:, 0:SEQS[s]], core.ones, total[:, by_sequence(s)],
                                     start=True, stop=True)
                last.then_inc(mean_mm, 1)
                pe.wait_ge(y_ok, 2 * HALF_Z)
                out.pe_branch(pe, 0, y)
                with pe.Fori(1, OUT) as c:
                    out.pe_gate(pe, c)
                    out.pe_branch(pe, c, y)

            @block.scalar
            def _(act):
                def z_half(f):
                    with act.Fori(0, HALF_Z // 2) as i:
                        for u in range(2):
                            k = 2 * i + u
                            ct, n = HALF_Z * f + k, Z[f] + k
                            act.wait_ge(z_mm, 2 * ct + 2)
                            for s in range(2):
                                last = act.activation(zs[u][:, by_sequence(s)], core.bank[2 * u + s][:, 0:SEQS[s]],
                                                      ACT.Silu)
                            last.then_inc(silu_ok, 1)
                            w.round(act, n + 2, u, Z[f] // 2 + i + 1)
                            act.wait_ge(gated, ct + 3)
                            act.wait_ge(o_mm, 2 * OUT * f + 2)
                            act.activation(y.high[:, bass.ds(k, 1), :].rearrange("p k t -> p (k t)"), zs[u][:, :],
                                           ACT.Copy, scale=core.feat[:, bass.ds(P_GSSM + ct, 1)])\
                                .then_inc(high_ok, 1)
                            act.wait_ge(summed, ct + 1)
                            act.activation(square[:, :], zs[u][:, :], ACT.Square, scale=DI ** -0.5)\
                                .then_inc(sq_ok, 1)

                act.sem_inc(silu_ok, 2)
                act.sem_inc(out.sig_ok, 1)
                z_half(0)
                with act.Fori(0, OUT // 2) as i:
                    for u in range(2):
                        w.round(act, O0 + 2 * i + u + 2, u, O0 // 2 + i + 1)
                z_half(1)
                act.wait_ge(mean_mm, 1)
                for s in range(2):
                    act.activation(rstd[:, by_sequence(s)], core.bank[4 + s][:, 0:SEQS[s]], ACT.Ln,
                                   bias=core.const[:, C_EPS:C_EPS + 1])
                act.drain()
                act.activation(rstd[:, :], rstd[:, :], ACT.Exp, scale=-0.5)
                act.drain()
                act.wait_ge(summed, 2 * HALF_Z + 1)
                act.activation(square[:, :], rstd[:, :], ACT.Square).then_inc(roots_ok, 1)

                with act.Fori(0, OUT // 2) as i:
                    for v in range(2):
                        c = 2 * i + v
                        out.act_tile(act, c, v)
                        for u in range(2):
                            w.round(act, G0 + 2 * c + 2 + u, u, G0 // 2 + c + 1)

            @block.gpsimd
            def _(pool):
                def z_half(f):
                    with pool.Fori(0, HALF_Z // 2) as i:
                        for u in range(2):
                            ct, n = HALF_Z * f + 2 * i + u, Z[f] + 2 * i + u
                            w.lower(pool, n + 2, u)
                            pool.wait_ge(sq_ok, ct + 1)
                            pool.tensor_tensor(total[:, :], total[:, :], square[:, :], ALU.add).then_inc(summed, 1)

                pool.memset(total[:, :], 0.0)
                pool.drain().then_inc(summed, 1)
                z_half(0)
                with pool.Fori(0, OUT // 2) as i:
                    for u in range(2):
                        w.lower(pool, O0 + 2 * i + u + 2, u)
                z_half(1)
                with pool.Fori(0, OUT) as c:
                    for u in range(2):
                        w.lower(pool, G0 + 2 * c + u + 2, u)

            @block.vector
            def _(dve):
                def z_half(f):
                    with dve.Fori(0, HALF_Z // 2) as i:
                        for u in range(2):
                            k = 2 * i + u
                            ct = HALF_Z * f + k
                            dve.wait_ge(tr_mm, ct + 3)
                            dve.wait_ge(silu_ok, ct + 3)
                            for s in range(2):
                                last = dve.tensor_tensor(zs[u][:, by_sequence(s)], zs[u][:, by_sequence(s)],
                                                         core.bank[4 + 2 * u + s][:, 0:SEQS[s]], ALU.mult)
                            last.then_inc(gated, 1)
                            dve.drain()
                            dve.wait_ge(high_ok, ct + 1)
                            low, high = (part[:, bass.ds(k, 1), :].rearrange("p k t -> p (k t)")
                                         for part in (y.low, y.high))
                            dve.scalar_tensor_tensor(low, zs[u][:, :], core.feat[:, bass.ds(P_GSSM + ct, 1)],
                                                     high.bitcast(F32), ALU.mult, ALU.subtract).then_inc(y_ok, 1)

                def merged(c):
                    return core.mergedT[:, bass.ds(c, 1), :].rearrange("p c t -> p (c t)")

                dve.sem_inc(gated, 2)
                dve.sem_inc(o_left, 2)
                dve.sem_inc(out.merged, 1)
                z_half(0)
                with dve.Fori(0, OUT // 2) as i:
                    for u in range(2):
                        c = 2 * i + u
                        dve.wait_ge(o_mm, 2 * c + 4)
                        for s in range(2):
                            last = dve.tensor_copy(merged(c)[:, by_sequence(s)], core.bank[2 * u + s][:, 0:SEQS[s]])
                        last.then_inc(o_left, 1)
                dve.drain()
                z_half(1)
                dve.wait_ge(roots_ok, 1)
                for s in range(2):
                    dve.scalar_tensor_tensor(square[:, by_sequence(s)], core.bank[4 + s][:, 0:SEQS[s]], EPS,
                                             square[:, by_sequence(s)], ALU.add, ALU.mult)
                dve.drain()
                dve.tensor_scalar(square[:, :], square[:, :], -0.5, 1.5, ALU.mult, ALU.add)
                dve.drain()
                dve.tensor_tensor(rstd[:, :], rstd[:, :], square[:, :], ALU.mult)
                dve.drain()
                with dve.Fori(0, OUT // 2) as i:
                    for v in range(2):
                        c = 2 * i + v
                        dve.wait_ge(out.sig_ok, c + 2)
                        dve.tensor_tensor(out.gate[v][:, :], out.gate[v][:, :], rstd[:, :], ALU.mult)
                        dve.wait_ge(out.mm, 4 * c + 4)
                        for s in range(2):
                            dve.tensor_tensor(merged(c)[:, by_sequence(s)], merged(c)[:, by_sequence(s)],
                                              core.bank[2 + s][:, 0:SEQS[s]], ALU.add)
                        dve.drain()
                        dve.tensor_tensor(merged(c), merged(c), out.gate[v][:, :], ALU.mult).then_inc(out.merged, 1)
                dve.drain()


def attention_output(core):
    nc = core.nc
    own, sb, sem = open_stage(core)
    OUT = D // P
    w_out = core.d["w_out_attn"].rearrange("o (k p) n -> (o p) k n", p=P)
    with own:
        w = new_pieces(core, sb, "att_out", OUT_PIECE)
        part = sb("att_out_part", [P, TOK])
        attn = Pair(sb, "attn", [P, KD, TOK])
        attn_high_ok, attn_ok = sem("att_high_ok"), sem("att_pair_ok")
        out = GatedOutput(core, sb, sem, w, "att_out", 0)
        with nc.Block() as block:

            @block.sync
            def _(sp):
                with sp.Fori(0, OUT // 2) as i:
                    for v in range(2):
                        c = 2 * i + v
                        w.load(sp, 2 * c, 0, core.w_in_cols(GA0 + c * P, P))
                        w.load(sp, 2 * c + 1, 1, pair_of_tiles(w_out, i, v))

            @block.tensor
            def _(pe):
                out.pe_gate(pe, 0)
                pe.wait_ge(attn_ok, KD)
                out.pe_branch(pe, 0, attn)
                with pe.Fori(1, OUT) as c:
                    out.pe_gate(pe, c)
                    out.pe_branch(pe, c, attn)

            @block.scalar
            def _(act):
                def tile(c, v, more=True):
                    out.act_tile(act, c, v)
                    if more:
                        w.round(act, 2 * c + 2, 0, c + 1)
                        w.round(act, 2 * c + 3, 1, c + 1)

                act.sem_inc(out.sig_ok, 1)
                for u in range(2):
                    w.round(act, u, u, 0)
                for k in range(KD):
                    act.activation(attn.high[:, k, :], core.attnT[:, k, :], ACT.Copy).then_inc(attn_high_ok, 1)
                with act.Fori(0, OUT // 2 - 1) as i:
                    for v in range(2):
                        tile(2 * i + v, v)
                tile(OUT - 2, 0)
                tile(OUT - 1, 1, more=False)

            @block.gpsimd
            def _(pool):
                with pool.Fori(0, OUT) as c:
                    for u in range(2):
                        w.lower(pool, 2 * c + u, u)

            @block.vector
            def _(dve):
                dve.sem_inc(out.merged, 1)
                for k in range(KD):
                    dve.wait_ge(attn_high_ok, k + 1)
                    dve.tensor_tensor(attn.low[:, k, :], core.attnT[:, k, :], attn.high[:, k, :].bitcast(F32),
                                      ALU.subtract).then_inc(attn_ok, 1)
                with dve.Fori(0, OUT // 2) as i:
                    for v in range(2):
                        c = 2 * i + v
                        dve.wait_ge(out.sig_ok, c + 2)
                        dve.wait_ge(out.mm, 4 * c + 4)
                        for s in range(2):
                            dve.tensor_tensor(part[:, by_sequence(s)], core.bank[2 + s][:, 0:SEQS[s]],
                                              out.gate[v][:, by_sequence(s)], ALU.mult)
                        dve.drain()
                        merged = core.mergedT[:, bass.ds(c, 1), :].rearrange("p c t -> p (c t)")
                        dve.tensor_tensor(merged, merged, part[:, :], ALU.add).then_inc(out.merged, 1)
                        dve.drain()


def project_qkv(core):
    nc = core.nc
    own, sb, sem = open_stage(core)
    NQKT, NV = NQK * HD // P, HKV * HD // P
    with own:
        w = core.pieces.of_stage(QKV_PIECE)
        x = [sb(f"qkv_x{u}", [P, TOK]) for u in range(2)]
        square = [sb(f"qkv_square{u}", [P, TOK]) for u in range(2)]
        part, root_sq = sb("qkv_part", [P, TOK]), sb("qkv_root_sq", [P, TOK])
        mm, x_ok, mean_mm, mean_left, roots_ok, x_gained, swapped, x_used = (
            sem("qkv_mm"), sem("qkv_x_ok"), sem("qkv_mean_mm"), sem("qkv_mean_left"), sem("qkv_roots_ok"),
            sem("qkv_x_gained"), sem("qkv_swapped"), sem("qkv_x_used"))
        v_left, v_tr, v_ok, k_copied = sem("qkv_v_left"), sem("qkv_v_tr"), sem("qkv_v_ok"), sem("qkv_k_copied")
        last_pair = NQKT // 2 - 1

        with nc.Block() as block:

            @block.sync
            def _(sp):
                with sp.Fori(1, (NQKT + NV) // 2) as i:
                    for u in range(2):
                        w.load(sp, 2 * i + u, u, pair_of_tiles(core.w_in[:, :, 0:(NQKT + NV) * P], i, u))
                sp.wait_ge(x_used, NQKT + 2)
                for kv in range(HKV):
                    for half in range(2):
                        k = core.qk[HD * (kv % 2):HD * (kv % 2) + HD, HQ // 2 + kv // 2, :]
                        sp.dma_start(core.k_both[half * HD:(half + 1) * HD, kv, :], k).then_inc(k_copied, 16)
                sp.wait_ge(k_copied, 2 * HKV * 16)

            @block.tensor
            def _(pe):
                def product(n, u):
                    w.ready(pe, n)
                    pe.wait_ge(x_ok, n + 1)
                    transposed_products(pe, core, w, u, core.h, mm)
                    w.release(pe)

                def mean(n, u):
                    pe.wait_ge(x_ok, n + 3)
                    pe.wait_ge(mean_left, n + 1)
                    for s in range(2):
                        last = pe.matmul(core.bank[4 + s][:, 0:SEQS[s]], core.head_mean,
                                         square[u][:, by_sequence(s)], start=True, stop=True)
                    last.then_inc(mean_mm, 1)

                def swap(n, u):
                    pe.wait_ge(x_gained, n + 2)
                    pe.wait_ge(x_used, n + 1)
                    for s in range(2):
                        last = pe.matmul(core.bank[6 + s][:, 0:SEQS[s]], core.swap, x[u][:, by_sequence(s)],
                                         start=True, stop=True)
                    last.then_inc(swapped, 1)

                product(0, 0)
                product(1, 1)
                mean(0, 0)
                with pe.Fori(1, NQKT // 2) as i:
                    product(2 * i, 0)
                    mean(2 * i - 1, 1)
                    swap(2 * i - 2, 0)
                    product(2 * i + 1, 1)
                    mean(2 * i, 0)
                    swap(2 * i - 1, 1)
                product(NQKT, 0)
                mean(NQKT - 1, 1)
                swap(NQKT - 2, 0)
                product(NQKT + 1, 1)
                swap(NQKT - 1, 1)
                for j in range(NV):
                    pe.wait_ge(v_left, j + 1)
                    pe.wait_ge(mean_left, NQKT + 1)
                    for t in range(NT):
                        bank, at = (0, t * P) if t < 4 else (1, (t - 4) * P)
                        if j and t == 0:
                            pe.wait_ge(v_ok, 1)
                        last = pe.transpose(core.bank[4 + bank][:, at:at + P], x[j][:, t * P:(t + 1) * P], core.ident)
                    last.then_inc(v_tr, 1)

            @block.scalar
            def _(act):
                def leave(n, u):
                    act.wait_ge(mm, 2 * n + 2)
                    act.wait_ge(x_used, n + 1)
                    for s in range(2):
                        act.activation(x[u][:, by_sequence(s)], core.bank[2 * u + s][:, 0:SEQS[s]], ACT.Copy)
                        last = act.activation(square[u][:, by_sequence(s)], core.bank[2 * u + s][:, 0:SEQS[s]],
                                              ACT.Square)
                    last.then_inc(x_ok, 1)

                def roots(n, u):
                    act.wait_ge(mean_mm, n + 1)
                    for s in range(2):
                        act.activation(square[u][:, by_sequence(s)], core.bank[4 + s][:, 0:SEQS[s]],
                                       ACT.Ln, bias=core.const[:, C_EPS:C_EPS + 1])
                    act.drain()
                    act.activation(square[u][:, :], square[u][:, :], ACT.Exp, scale=-0.5)
                    act.drain()
                    act.wait_ge(x_gained, n + 1)
                    act.activation(root_sq[:, :], square[u][:, :], ACT.Square).then_inc(roots_ok, 1)

                act.sem_inc(x_ok, 2)
                leave(0, 0)
                w.round(act, 2, 0, 1)
                leave(1, 1)
                w.round(act, 3, 1, 1)
                roots(0, 0)
                with act.Fori(1, NQKT // 2) as i:
                    roots(2 * i - 1, 1)
                    leave(2 * i, 0)
                    w.round(act, 2 * i + 2, 0, i + 1)
                    roots(2 * i, 0)
                    leave(2 * i + 1, 1)
                    w.round(act, 2 * i + 3, 1, i + 1)
                roots(NQKT - 1, 1)
                for j in range(NV):
                    act.wait_ge(mm, 2 * (NQKT + j) + 2)
                    act.wait_ge(x_used, NQKT + j + 1)
                    for s in range(2):
                        last = act.activation(x[j][:, by_sequence(s)], core.bank[2 * j + s][:, 0:SEQS[s]], ACT.Copy)
                    last.then_inc(v_left, 1)
                for j in range(NV):
                    act.wait_ge(v_tr, j + 1)
                    for bank, t0, n in ((0, 0, 4), (1, 4, NT - 4)):
                        last = act.activation(core.v[:, t0:t0 + n, j * P:(j + 1) * P],
                                              core.bank[4 + bank][:, 0:n * P].rearrange("p (t c) -> p t c", t=n),
                                              ACT.Copy)
                    last.then_inc(v_ok, 1)

            @block.gpsimd
            def _(pool):
                with pool.Fori(1, (NQKT + NV) // 2) as i:
                    for u in range(2):
                        w.lower(pool, 2 * i + u, u)

            @block.vector
            def _(dve):
                def normed(n, u):
                    dve.wait_ge(roots_ok, n + 1)
                    for s in range(2):
                        last = dve.scalar_tensor_tensor(root_sq[:, by_sequence(s)], core.bank[4 + s][:, 0:SEQS[s]], EPS,
                                                        root_sq[:, by_sequence(s)], ALU.add, ALU.mult)
                    last.then_inc(mean_left, 1)
                    dve.scalar_tensor_tensor(x[u][:, :], x[u][:, :], core.feat[:, bass.ds(P_GQK + n, 1)],
                                             square[u][:, :], ALU.mult, ALU.mult)
                    dve.drain()
                    dve.tensor_scalar(root_sq[:, :], root_sq[:, :], -0.5, 1.5, ALU.mult, ALU.add)
                    dve.drain()
                    dve.tensor_tensor(x[u][:, :], x[u][:, :], root_sq[:, :], ALU.mult).then_inc(x_gained, 1)
                    dve.drain()

                def rotated(n, u):
                    dve.wait_ge(swapped, n + 1)
                    into = core.qk[:, bass.ds(n, 1), :].rearrange("p k t -> p (k t)")
                    for s in range(2):
                        tokens = by_sequence(s)
                        dve.tensor_tensor(part[:, tokens], core.bank[6 + s][:, 0:SEQS[s]], core.sin[:, 0:SEQS[s]],
                                          ALU.mult)
                        dve.tensor_tensor(into[:, tokens], x[u][:, tokens], core.cos[:, 0:SEQS[s]], ALU.mult)
                    dve.drain()
                    dve.tensor_tensor(into, into, part[:, :], ALU.add).then_inc(x_used, 1)
                    dve.drain()

                dve.sem_inc(x_used, 2)
                dve.sem_inc(x_gained, 1)
                dve.sem_inc(mean_left, 1)
                normed(0, 0)
                with dve.Fori(0, last_pair) as i:
                    for u in range(2):
                        rotated(2 * i + u, u)
                        normed(2 * i + u + 1, 1 - u)
                rotated(NQKT - 2, 0)
                normed(NQKT - 1, 1)
                rotated(NQKT - 1, 1)


def attend(core):
    nc = core.nc
    own, sb, sem = open_stage(core)
    SCALE = HD ** -0.5
    GROUPS = [(t, kv) for t in range(NT) for kv in range(HKV)]

    def window(t):
        s = 0 if t < FIRST[1] else 1
        lo, hi = max(FIRST[s], t - 1), min(FIRST[s] + TILES[s] - 1, t + 1)
        return lo, hi - lo + 1

    PLAN = []
    for g, (t, kv) in enumerate(GROUPS):
        PLAN += [("probs", t, kv, QPK * g + c) for c in range(QPK)]
        if kv == 1 and t > 0:
            PLAN += [("out", t - 1, j, 0) for j in range(2)]
    PLAN += [("out", NT - 1, j, 0) for j in range(2)]
    ORDER = {item: n for n, item in enumerate(PLAN)}
    with own:
        score = [sb(f"att_score{u}", [P, QPK, WIDE]) for u in range(2)]
        top, den = sb("att_top", [P, NT, HQ]), sb("att_den", [P, NT, HQ])
        neg, sunk = sb("att_neg", [P, NT, HQ]), sb("att_sunk", [P, NT, HQ])
        pT = [sb(f"att_pT{u}", [P, WIDE]) for u in range(4)]
        o = [sb(f"att_o{u}", [P, HQ * HD]) for u in range(2)]
        s_mm, s_read, top_ok, p_ok, t_mm, t_free, pv_mm, o_ok = (
            sem("att_s_mm"), sem("att_s_read"), sem("att_top_ok"), sem("att_p_ok"), sem("att_t_mm"),
            sem("att_t_free"), sem("att_pv_mm"), sem("att_o_ok"))
        with nc.Block() as block:

            @block.sync
            def _(sp):
                for rows in (core.rows_in, core.rows_out[NEXP * CAP:ROWS, :]):
                    n = rows.shape[0] // CAP
                    for c in range(D // ZW):
                        blocks = rows[:, c * ZW:(c + 1) * ZW].rearrange("(b p) d -> p b d", p=CAP)
                        sp.dma_start(blocks, core.zeros[:, :].unsqueeze(1).to_broadcast([CAP, n, ZW]))\
                            .then_inc(core.zero_out, 16)

            @block.tensor
            def _(pe):
                def scores(g):
                    t, kv = GROUPS[g]
                    lo, n = window(t)
                    for c in range(QPK):
                        m = QPK * g + c
                        if m >= 2:
                            pe.wait_ge(s_read, m - 1)
                        half = slice(HD * (c % 2), HD * (c % 2) + HD)
                        pe.matmul(core.bank[m % 2][:, 0:n * P],
                                  core.qk[half, (QPK * kv + c) // 2, t * P:(t + 1) * P],
                                  core.k_both[half, kv, lo * P:(lo + n) * P], start=True, stop=True)\
                            .then_inc(s_mm, 1)

                def values(m):
                    t, kv = GROUPS[m // QPK]
                    head = m % HQ
                    lo, n = window(t)
                    pe.wait_ge(t_free, ORDER["probs", t, kv, m] + 1)
                    if head % 8 == 0 and t >= 2:
                        pe.wait_ge(o_ok, t - 1)
                    at = (head % 8) * HD
                    for b in range(n):
                        last = pe.matmul(core.bank[4 + 2 * (t % 2) + head // 8][:, at:at + HD],
                                         pT[m % 4][:, b * P:(b + 1) * P],
                                         core.v[:, lo + b, kv * HD:(kv + 1) * HD], start=(b == 0), stop=(b == n - 1))
                    last.then_inc(pv_mm, 1)

                scores(0)
                for r, (kind, t, j, m) in enumerate(PLAN):
                    if r >= 2:
                        pe.wait_ge(t_free, r - 1)
                    if kind == "probs":
                        if m % QPK == 0 and m // QPK + 1 < len(GROUPS):
                            scores(m // QPK + 1)
                        pe.wait_ge(p_ok, m + 1)
                        for b in range(window(t)[1]):
                            last = pe.transpose(core.bank[2 + r % 2][:, b * P:(b + 1) * P],
                                                score[(m // QPK) % 2][:, m % QPK, b * P:(b + 1) * P], core.ident)
                        last.then_inc(t_mm, 1)
                        if m >= 2:
                            values(m - 2)
                    else:
                        if t == NT - 1 and j == 0:
                            values(NT * HQ - 2)
                            values(NT * HQ - 1)
                        pe.wait_ge(o_ok, t + 1)
                        for c in range(4):
                            last = pe.transpose(core.bank[2 + r % 2][:, c * P:(c + 1) * P],
                                                o[t % 2][:, (4 * j + c) * P:(4 * j + c + 1) * P], core.ident)
                        last.then_inc(t_mm, 1)

            @block.scalar
            def _(act):
                def probabilities(g):
                    t, kv = GROUPS[g]
                    act.wait_ge(top_ok, g + 1)
                    h = QPK * kv
                    act.activation(sunk[:, t, h:h + QPK], sunk[:, t, h:h + QPK], ACT.Exp)
                    for c in range(QPK):
                        p = score[g % 2][:, c, 0:window(t)[1] * P]
                        act.activation(p, p, ACT.Exp, bias=neg[:, t, h + c:h + c + 1], scale=SCALE,
                                       accum_out=den[:, t, h + c:h + c + 1]).then_inc(p_ok, 1)

                probabilities(0)
                for r, (kind, t, j, m) in enumerate(PLAN):
                    act.wait_ge(t_mm, r + 1)
                    if kind == "probs":
                        width = window(t)[1] * P
                        if m >= 4:
                            act.wait_ge(pv_mm, m - 3)
                        act.activation(pT[m % 4][:, 0:width], core.bank[2 + r % 2][:, 0:width], ACT.Copy)\
                            .then_inc(t_free, 1)
                        if m % QPK == QPK - 1 and m // QPK + 1 < len(GROUPS):
                            probabilities(m // QPK + 1)
                    else:
                        act.activation(core.attnT[:, 4 * j:4 * j + 4, t * P:(t + 1) * P],
                                       core.bank[2 + r % 2][:, :].rearrange("p (k t) -> p k t", k=4),
                                       ACT.Copy).then_inc(t_free, 1)

            @block.vector
            def _(dve):
                def tops(g):
                    t, kv = GROUPS[g]
                    lo, n = window(t)
                    h = QPK * kv
                    mask = core.const[:, C_MASK + (lo - t + 1) * P:C_MASK + (lo - t + 1 + n) * P]
                    if g >= 2:
                        dve.wait_ge(t_mm, ORDER["probs", *GROUPS[g - 2], QPK * (g - 2) + QPK - 1] + 1)
                    for c in range(QPK):
                        m = QPK * g + c
                        dve.wait_ge(s_mm, m + 1)
                        dve.tensor_tensor_reduce(score[g % 2][:, c, 0:n * P], core.bank[m % 2][:, 0:n * P], mask,
                                                 1.0, -3e38, ALU.add, ALU.max,
                                                 top[:, t, h + c:h + c + 1]).then_inc(s_read, 1)
                    dve.drain()
                    sink = core.row[:, R_SINK + h:R_SINK + h + QPK]
                    dve.scalar_tensor_tensor(top[:, t, h:h + QPK], top[:, t, h:h + QPK], SCALE, sink,
                                             ALU.mult, ALU.max)
                    dve.drain()
                    dve.tensor_scalar(neg[:, t, h:h + QPK], top[:, t, h:h + QPK], -1.0, None, ALU.mult)
                    dve.tensor_tensor(sunk[:, t, h:h + QPK], sink, top[:, t, h:h + QPK], ALU.subtract)\
                        .then_inc(top_ok, 1)

                def finish(t):
                    dve.wait_ge(p_ok, HQ * (t + 1))
                    dve.tensor_tensor(den[:, t, :], den[:, t, :], sunk[:, t, :], ALU.add)
                    dve.drain()
                    dve.reciprocal(den[:, t, :], den[:, t, :])
                    dve.drain()
                    dve.wait_ge(pv_mm, HQ * (t + 1))
                    if t >= 2:
                        dve.wait_ge(t_mm, ORDER["out", t - 2, 1, 0] + 1)
                    for j in range(2):
                        last = dve.tensor_tensor(
                            o[t % 2][:, j * 512:(j + 1) * 512].rearrange("p (h c) -> p h c", h=8),
                            core.bank[4 + 2 * (t % 2) + j][:, :].rearrange("p (h c) -> p h c", h=8),
                            den[:, t, 8 * j:8 * j + 8].unsqueeze(2).to_broadcast([P, 8, HD]), ALU.mult)
                    last.then_inc(o_ok, 1)

                for g, (t, kv) in enumerate(GROUPS):
                    tops(g)
                    if kv == 1 and t > 0:
                        finish(t - 1)
                finish(NT - 1)


def mix_and_route(core):
    nc = core.nc
    own, sb, sem = open_stage(core)
    NL = NG + NEXP
    with own:
        wo = sb("mix_wo", [P, KD, D])
        wr = sb("mix_wr", [P, KD, NL])
        x = [sb(f"mix_x{u}", [P, D]) for u in range(2)]
        square = sb("mix_square", [P, D])
        mean, rstd = sb("mix_mean", [P, NT]), sb("mix_rstd", [P, NT])
        x1 = [sb(f"mix_x1_{u}", [P, D]) for u in range(2)]
        h2 = sb("mix_h2", [P, NT, D])
        h2T = [sb(f"mix_h2T{u}", [P, KD, P]) for u in range(2)]
        logit = sb("r_logit", [P, NT, NL])
        g_exp, g_pick, cand4 = sb("r_g_exp", [P, NT, NG]), sb("r_g_pick", [P, NT, NG]), sb("r_cand4", [P, NT, NG])
        g_top, g_best, g_w = sb("r_g_top", [P, NT]), sb("r_g_best", [P, NT]), sb("r_g_w", [P, NT])
        spread = sb("r_spread", [P, NT, NG, NE_G])
        e_logit, cand8 = sb("r_e_logit", [P, NT, NE_G]), sb("r_cand8", [P, NT, NE_G])
        e_top, e_best = sb("r_e_top", [P, 2, NT]), sb("r_e_best", [P, NT])
        e_pick = sb("r_e_pick", [P, 2, NT, NE_G])
        ratio = sb("r_ratio", [P, NT])
        takes = sb("r_takes", [P, 2, NT, NEXP])
        both, before = sb("r_both", [P, NT, NEXP]), sb("r_before", [P, NT + 1, NEXP])
        rank, slot = sb("r_rank", [P, NT, NEXP]), sb("r_slot", [P, NT, NEXP])
        counts, over, shift = sb("r_counts", [P, NEXP]), sb("r_over", [P, NEXP]), sb("r_shift", [P, NEXP])
        until = [sb(f"r_until{u}", [P, NEXP]) for u in range(2)]
        place = sb("r_place", [P, 2, NT])
        blocks = sb("r_blocks", [P, NBI, NEXP])
        owner = sb("r_owner", [P, NBI + 1])
        x_in = [sem(f"mix_x_in{u}") for u in range(2)]
        x1_out = [sem(f"mix_x1_out{u}") for u in range(2)]
        wo_in = [sem(f"mix_wo_in{j}") for j in range(2)]
        mm, x1_ok, mean_ok, rstd_ok, h2_ok, tr_mm, tr_free, r_mm = (
            sem("mix_mm"), sem("mix_x1_ok"), sem("mix_mean_ok"),
            sem("mix_rstd_ok"), sem("mix_h2_ok"), sem("mix_tr_mm"), sem("mix_tr_free"), sem("mix_r_mm"))
        exp_in_ok, exp_ok, both_ok, rank_mm, place_ok, scattered = (
            sem("r_exp_in_ok"), sem("r_exp_ok"), sem("r_both_ok"), sem("r_rank_mm"), sem("r_place_ok"),
            sem("r_scattered"))
        with nc.Block() as block:

            @block.sync
            def _(sp):
                w_view = core.d["w_o"].rearrange("o (k p) n -> (o p) k n", p=P)
                for j in range(2):
                    half = slice(j * 512, (j + 1) * 512)
                    sp.dma_start(wo[:, :, half], w_view[:, :, half]).then_inc(wo_in[j], 16)
                    if j == 0:
                        sp.dma_start(wr[:, :, :], core.d["router"].rearrange("(k p) n -> p k n", p=P))\
                            .then_inc(wo_in[1], 16)
                for t in range(NT + 2):
                    if t >= 2:
                        sp.wait_ge(x1_ok, t - 1)
                        sp.dma_start(core.x1[(t - 2) * P:(t - 1) * P, :], x1[t % 2][:, :]).then_inc(x1_out[t % 2], 16)
                    if t < NT:
                        sp.dma_start(x[t % 2][:, :], core.x_tile(t)).then_inc(x_in[t % 2], 16)
                for w, w_in, source in zip(core.first_weights, core.first_weights_in,
                                           (core.expert_rows("w_gate", 0, KD), core.expert_rows("w_up", 0, KD),
                                            core.expert_cols("w_down", 0))):
                    sp.dma_start(w[:, :, :], source).then_inc(w_in, 16)
                for u in range(2):
                    sp.wait_ge(x1_out[u], 16 * (NT // 2))

            @block.tensor
            def _(pe):
                def mix(t):
                    for j in range(2):
                        n = 2 * t + j
                        if n >= 4:
                            pe.wait_ge(x1_ok, n // 2 - 1)
                        if t == 0:
                            pe.wait_ge(wo_in[j], 16 * (j + 1))
                        for k in range(KD):
                            last = pe.matmul(core.bank[n % 4][:, :], core.mergedT[:, k, t * P:(t + 1) * P],
                                             wo[:, k, j * 512:(j + 1) * 512], start=(k == 0), stop=(k == KD - 1))
                    last.then_inc(mm, 1)

                def route(t):
                    pe.wait_ge(h2_ok, t + 1)
                    for j in range(2):
                        n = 2 * t + j
                        if n >= 2:
                            pe.wait_ge(tr_free, n - 1)
                        for c in range(4):
                            k = 4 * j + c
                            last = pe.transpose(core.bank[4 + n % 2][:, c * P:(c + 1) * P],
                                                h2[:, t, k * P:(k + 1) * P], core.ident)
                        last.then_inc(tr_mm, 1)
                    pe.wait_ge(tr_free, 2 * t + 2)
                    for k in range(KD):
                        last = pe.matmul(core.bank[6][:, t * NL:(t + 1) * NL], h2T[t % 2][:, k, :], wr[:, k, :],
                                         start=(k == 0), stop=(k == KD - 1))
                    last.then_inc(r_mm, 1)

                mix(0)
                for t in range(NT):
                    if t + 1 < NT:
                        mix(t + 1)
                    route(t)
                pe.wait_ge(both_ok, 1)
                pe.matmul(core.bank[7][:, 0:NT * NEXP], core.strict, both[:, :, :].rearrange("p t e -> p (t e)"),
                          start=True, stop=False)
                pe.matmul(core.bank[7][:, 0:NT * NEXP], core.ones, before[:, 0:NT, :].rearrange("p t e -> p (t e)"),
                          start=False, stop=True)
                pe.matmul(core.bank[7][:, NT * NEXP:(NT + 1) * NEXP], core.ones, before[:, NT, :],
                          start=True, stop=True).then_inc(rank_mm, 1)

            @block.scalar
            def _(act):
                for t in range(NT):
                    act.wait_ge(x1_ok, t + 1)
                    act.activation(square[:, :], x1[t % 2][:, :], ACT.Square, scale=D ** -0.5,
                                   accum_out=mean[:, t:t + 1]).then_inc(mean_ok, 1)
                    act.drain()
                    for j in range(2):
                        n = 2 * t + j
                        act.wait_ge(tr_mm, n + 1)
                        if t >= 2 and j == 0:
                            act.wait_ge(r_mm, t - 1)
                        act.activation(h2T[t % 2][:, 4 * j:4 * j + 4, :],
                                       core.bank[4 + n % 2][:, :].rearrange("p (k t) -> p k t", k=4),
                                       ACT.Copy).then_inc(tr_free, 1)
                act.wait_ge(exp_in_ok, 1)
                act.activation(g_exp[:, :, :], g_exp[:, :, :], ACT.Exp)
                act.activation(ratio[:, :], ratio[:, :], ACT.Exp).then_inc(exp_ok, 1)

            @block.gpsimd
            def _(pool):
                for t in range(NT):
                    pool.wait_ge(mean_ok, t + 1)
                    rsqrt(core, pool, rstd[:, t:t + 1], mean[:, t:t + 1]).then_inc(rstd_ok, 1)
                pool.wait_ge(core.zero_out, 2 * (D // ZW) * 16)
                pool.wait_ge(place_ok, 1)
                for n in range(2):
                    for t in range(NT):
                        pool.indirect_dma_start(
                            out=core.rows_in[:, :],
                            out_offset=bass.IndirectOffsetOnAxis(ap=core.place[:, n * NT + t:n * NT + t + 1], axis=0),
                            in_=h2[:, t, :], in_offset=None).then_inc(scattered, 16)
                pool.wait_ge(scattered, 2 * NT * 16)

            @block.vector
            def _(dve):
                for t in range(NT):
                    dve.wait_ge(mm, t + 1)
                    dve.wait_ge(x_in[t % 2], 16 * (t // 2 + 1))
                    if t >= 2:
                        dve.wait_ge(x1_out[t % 2], 16 * (t // 2))
                    for j in range(2):
                        last = dve.tensor_tensor(x1[t % 2][:, j * 512:(j + 1) * 512], core.bank[(2 * t + j) % 4][:, :],
                                                 x[t % 2][:, j * 512:(j + 1) * 512], ALU.add)
                    last.then_inc(x1_ok, 1)
                    dve.wait_ge(rstd_ok, t + 1)
                    dve.scalar_tensor_tensor(h2[:, t, :], x1[t % 2][:, :], rstd[:, t:t + 1],
                                             core.row[:, R_FFN:R_FFN + D], ALU.mult, ALU.mult).then_inc(h2_ok, 1)

                def then(*_):
                    dve.drain()

                def pick(out, values, peak, order, cand, best):
                    n = values.shape[-1]
                    wide = [P, NT, n]
                    then(dve.tensor_tensor(cand, values, peak.unsqueeze(2).to_broadcast(wide), ALU.is_equal))
                    then(dve.tensor_tensor(cand, cand, order.unsqueeze(1).to_broadcast(wide), ALU.mult))
                    then(dve.tensor_reduce(best, cand, AX.X, ALU.max))
                    then(dve.tensor_tensor(out, cand, best.unsqueeze(2).to_broadcast(wide), ALU.is_equal))

                dve.wait_ge(r_mm, NT)
                bias = core.row[:, R_BR:R_BR + NL].unsqueeze(1).to_broadcast([P, NT, NL])
                then(dve.tensor_tensor(logit[:, :, :],
                                       core.bank[6][:, 0:NT * NL].rearrange("p (t n) -> p t n", t=NT), bias, ALU.add))
                group = logit[:, :, 0:NG]
                then(dve.tensor_reduce(g_top[:, :], group, AX.X, ALU.max))
                pick(g_pick[:, :, :], group, g_top[:, :], core.const[:, C_R4:C_R4 + NG], cand4[:, :, :], g_best[:, :])
                then(dve.tensor_tensor(g_exp[:, :, :], group, g_top[:, :].unsqueeze(2).to_broadcast([P, NT, NG]),
                                       ALU.subtract))
                wide = [P, NT, NG, NE_G]
                then(dve.tensor_tensor(spread[:, :, :, :],
                                       logit[:, :, NG:NL].rearrange("p t (g e) -> p t g e", g=NG),
                                       g_pick[:, :, :].unsqueeze(3).to_broadcast(wide), ALU.mult))
                then(dve.tensor_reduce(e_logit[:, :, :], spread[:, :, :, :].rearrange("p t g e -> p t e g"),
                                       AX.X, ALU.add))
                for n in range(2):
                    then(dve.tensor_reduce(e_top[:, n, :], e_logit[:, :, :], AX.X, ALU.max))
                    pick(e_pick[:, n], e_logit[:, :, :], e_top[:, n, :], core.const[:, C_R8:C_R8 + NE_G],
                         cand8[:, :, :], e_best[:, :])
                    then(dve.tensor_tensor(takes[:, n].rearrange("p t (g e) -> p t g e", g=NG),
                                           g_pick[:, :, :].unsqueeze(3).to_broadcast(wide),
                                           e_pick[:, n].unsqueeze(2).to_broadcast(wide), ALU.mult))
                    if n == 0:
                        then(dve.scalar_tensor_tensor(e_logit[:, :, :], e_pick[:, 0], -BIG, e_logit[:, :, :],
                                                      ALU.mult, ALU.add))
                dve.tensor_tensor(ratio[:, :], e_top[:, 1, :], e_top[:, 0, :], ALU.subtract).then_inc(exp_in_ok, 1)
                then(dve.tensor_tensor(both[:, :, :], takes[:, 0], takes[:, 1], ALU.add),
                     dve.memset(before[:, 0, :], 0.0))
                for t in range(NT):
                    last = dve.tensor_tensor(before[:, t + 1, :], before[:, t, :], both[:, t, :], ALU.add)
                    if t + 1 < NT:
                        dve.drain()
                last.then_inc(both_ok, 1)
                dve.wait_ge(exp_ok, 1)
                then(dve.tensor_reduce(g_w[:, :], g_exp[:, :, :], AX.X, ALU.add))
                then(dve.scalar_tensor_tensor(g_w[:, :], ratio[:, :], 1.0, g_w[:, :], ALU.add, ALU.mult))
                then(dve.reciprocal(core.weight[:, 0:NT], g_w[:, :]))
                then(dve.tensor_tensor(core.weight[:, NT:2 * NT], core.weight[:, 0:NT], ratio[:, :], ALU.mult))
                dve.wait_ge(rank_mm, 1)
                then(dve.tensor_copy(rank[:, :, :], core.bank[7][:, 0:NT * NEXP].rearrange("p (t e) -> p t e", t=NT)),
                     dve.tensor_copy(counts[:, :], core.bank[7][:, NT * NEXP:(NT + 1) * NEXP]))
                then(dve.tensor_scalar(over[:, :], counts[:, :], float(CAP), None, ALU.is_gt))
                for n in range(2, NBLK):
                    then(dve.scalar_tensor_tensor(over[:, :], counts[:, :], float(n * CAP), over[:, :],
                                                  ALU.is_gt, ALU.add))
                then(dve.tensor_copy(until[0][:, :], over[:, :]))
                n, step = 0, 1
                while step < NEXP:
                    a, b = until[n % 2], until[(n + 1) % 2]
                    then(dve.tensor_copy(b[:, 0:step], a[:, 0:step]),
                         dve.tensor_tensor(b[:, step:NEXP], a[:, step:NEXP], a[:, 0:NEXP - step], ALU.add))
                    n, step = n + 1, 2 * step
                until_all = until[n % 2]
                then(dve.tensor_tensor(shift[:, :], until_all[:, :], over[:, :], ALU.subtract))
                then(dve.tensor_scalar(shift[:, :], shift[:, :], float(CAP), float((NEXP - 1) * CAP),
                                       ALU.mult, ALU.add))
                experts_row = core.const[:, C_EC:C_EC + NEXP]
                then(dve.tensor_tensor(shift[:, :], shift[:, :], experts_row, ALU.subtract))
                wide = [P, NT, NEXP]
                then(dve.scalar_tensor_tensor(slot[:, :, :], rank[:, :, :], float(CAP),
                                              shift[:, :].unsqueeze(1).to_broadcast(wide), ALU.is_ge, ALU.mult))
                then(dve.tensor_tensor(slot[:, :, :], slot[:, :, :], rank[:, :, :], ALU.add))
                then(dve.tensor_tensor(slot[:, :, :], slot[:, :, :], experts_row.unsqueeze(1).to_broadcast(wide),
                                       ALU.add))
                for n in range(2):
                    then(dve.tensor_tensor(takes[:, n], takes[:, n], slot[:, :, :], ALU.mult))
                    then(dve.tensor_reduce(place[:, n, :], takes[:, n], AX.X, ALU.add))
                dve.tensor_copy(core.place[:, :], place[:, :, :].rearrange("p n t -> p (n t)")).then_inc(place_ok, 1)
                wide = [P, NBI, NEXP]
                then(dve.tensor_tensor(blocks[:, :, :], until_all[:, :].unsqueeze(1).to_broadcast(wide),
                                       core.const[:, C_BLK:C_BLK + NBI].unsqueeze(2).to_broadcast(wide), ALU.is_le))
                then(dve.tensor_reduce(owner[:, 0:NBI], blocks[:, :, :], AX.X, ALU.add))
                then(dve.tensor_scalar(owner[:, 0:NBI], owner[:, 0:NBI], float(NEXP - 1), None, ALU.min),
                     dve.tensor_copy(owner[:, NBI:NBI + 1], until_all[:, NEXP - 1:NEXP]))
                dve.tensor_copy(core.overflow[:, :], owner[0:1, :])


def expert_weights(sb, name):
    return sb(f"{name}_wg", [P, KD, DE]), sb(f"{name}_wu", [P, KD, DE]), sb(f"{name}_wd", [P, KE, D])


def experts(core):
    nc = core.nc
    own, sb, sem = open_stage(core)
    with own:
        wg, wu, wd = (list(pair) for pair in zip(core.first_weights,
                                                 expert_weights(lambda *args: sb(*args), "e1")))
        x = [sb(f"e_x{u}", [CAP, D]) for u in range(2)]
        xT = [sb(f"e_xT{u}", [P, KD, CAP]) for u in range(2)]
        silu = [sb(f"e_silu{u}", [P, KE, CAP]) for u in range(2)]
        act_T = [sb(f"e_act{u}", [P, KE, CAP]) for u in range(2)]
        y = [sb(f"e_y{u}", [CAP, D]) for u in range(2)]
        wg_in, wu_in, wd_in = ([first, sem(name)] for first, name in
                               zip(core.first_weights_in, ("e1_wg_in", "e1_wu_in", "e1_wd_in")))
        x_in, y_out = ([sem(f"{name}{u}") for u in range(2)] for name in ("e_x_in", "e_y_out"))
        tr_mm, xt_ok, gate_mm, up_mm, silu_ok, act_ok, down_mm, y_ok = (
            sem("e_tr_mm"), sem("e_xt_ok"), sem("e_gate_mm"), sem("e_up_mm"), sem("e_silu_ok"), sem("e_act_ok"),
            sem("e_down_mm"), sem("e_y_ok"))

        def load_rows(sp, e, u):
            sp.dma_start(x[u][:, :], core.rows_in[bass.ds(e * CAP, CAP), :]).then_inc(x_in[u], 16)

        def load(sp, e, u, first=False, last=False):
            if not first:
                sp.wait_ge(gate_mm, e - 1)
            sp.dma_start(wg[u][:, :, :], core.expert_rows("w_gate", e, KD)).then_inc(wg_in[u], 16)
            if not first:
                sp.wait_ge(up_mm, e - 1)
            sp.dma_start(wu[u][:, :, :], core.expert_rows("w_up", e, KD)).then_inc(wu_in[u], 16)
            if not last:
                sp.wait_ge(tr_mm, e)
                load_rows(sp, e + 1, 1 - u)
            if not first:
                sp.wait_ge(down_mm, e - 1)
            sp.dma_start(wd[u][:, :, :], core.expert_cols("w_down", e)).then_inc(wd_in[u], 16)

        def pe_transpose(pe, e, u, i, first=False):
            pe.wait_ge(x_in[u], 16 * i + 16)
            if not first:
                pe.wait_ge(xt_ok, e)
            for j in range(2):
                for c in range(4):
                    last = pe.transpose(core.bank[j][:, c * CAP:(c + 1) * CAP], x[u][:, bass.ds(4 * j + c, P, KD)],
                                        core.ident[0:CAP, 0:CAP])
            last.then_inc(tr_mm, 1)

        def pe_hidden(pe, e, u, i, w, w_in, bank, done, first=False):
            pe.wait_ge(xt_ok, e + 1)
            if not first:
                pe.wait_ge(act_ok, e - 1)
            pe.wait_ge(w_in[u], 16 * i + 16)
            for j in range(KE):
                for k in range(KD):
                    last = pe.matmul(core.bank[bank + 2 * u][:, j * CAP:(j + 1) * CAP],
                                     w[u][:, k, j * P:(j + 1) * P], xT[u][:, k, :],
                                     start=(k == 0), stop=(k == KD - 1))
            last.then_inc(done, 1)

        def pe_down(pe, e, u, i, first=False):
            pe.wait_ge(wd_in[u], 16 * i + 16)
            pe.wait_ge(act_ok, e + 1)
            if not first:
                pe.wait_ge(y_ok, e)
            for j in range(2):
                for k in range(KE):
                    last = pe.matmul(core.bank[6 + j][0:CAP, :], act_T[u][:, k, :], wd[u][:, k, j * 512:(j + 1) * 512],
                                     start=(k == 0), stop=(k == KE - 1))
            last.then_inc(down_mm, 1)

        def dve_xt(dve, e, u, first=False):
            dve.wait_ge(tr_mm, e + 1)
            if not first:
                dve.wait_ge(up_mm, e - 1)
            for j in range(2):
                last = dve.tensor_copy(xT[u][:, 4 * j:4 * j + 4, :],
                                       core.bank[j][:, 0:4 * CAP].rearrange("p (k r) -> p k r", k=4))
            last.then_inc(xt_ok, 1)

        def dve_act(dve, e, u, first=False):
            dve.wait_ge(silu_ok, e + 1)
            dve.wait_ge(up_mm, e + 1)
            if not first:
                dve.wait_ge(down_mm, e - 1)
            dve.tensor_tensor(act_T[u][:, :, :], silu[u][:, :, :],
                              core.bank[3 + 2 * u][:, 0:KE * CAP].rearrange("p (k r) -> p k r", k=KE),
                              ALU.mult).then_inc(act_ok, 1)

        def act_silu(act, e, u, first=False):
            act.wait_ge(gate_mm, e + 1)
            if not first:
                act.wait_ge(act_ok, e - 1)
            act.activation(silu[u][:, :, :], core.bank[2 + 2 * u][:, 0:KE * CAP]
                           .rearrange("p (k r) -> p k r", k=KE), ACT.Silu).then_inc(silu_ok, 1)

        def act_y(act, e, u, i):
            act.wait_ge(down_mm, e + 1)
            act.wait_ge(y_out[u], 16 * i)
            for j in range(2):
                last = act.activation(y[u][:, j * 512:(j + 1) * 512], core.bank[6 + j][0:CAP, :], ACT.Copy)
            last.then_inc(y_ok, 1)

        def pool_store(pool, e, u):
            pool.wait_ge(y_ok, e + 1)
            pool.dma_start(core.rows_out[bass.ds(e * CAP, CAP), :], y[u][:, :]).then_inc(y_out[u], 16)

        LAST = NEXP // 2 - 1
        with nc.Block() as block:

            @block.sync
            def _(sp):
                load_rows(sp, 0, 0)
                load_rows(sp, 1, 1)
                load(sp, 1, 1, first=True)
                with sp.Fori(1, LAST) as i:
                    for u in range(2):
                        load(sp, 2 * i + u, u)
                load(sp, NEXP - 2, 0)
                load(sp, NEXP - 1, 1, last=True)
                sp.dma_start(core.x1_back[:, :, :], core.x1.rearrange("(t p) d -> p t d", p=P))\
                    .then_inc(core.x1_in, 16)

            @block.tensor
            def _(pe):
                def pair(i, first=False, last=False):
                    for u in range(2):
                        e = 2 * i + u
                        pe_hidden(pe, e, u, i, wg, wg_in, 2, gate_mm, first=first)
                        if not (last and u == 1):
                            pe_transpose(pe, e + 1, 1 - u, i + u)
                        pe_hidden(pe, e, u, i, wu, wu_in, 3, up_mm, first=first)
                        if not (first and u == 0):
                            pe_down(pe, e - 1, 1 - u, i - (1 - u), first=(first and u == 1))

                pe_transpose(pe, 0, 0, 0, first=True)
                pair(0, first=True)
                with pe.Fori(1, LAST) as i:
                    pair(i)
                pair(LAST, last=True)
                pe_down(pe, NEXP - 1, 1, LAST)

            @block.vector
            def _(dve):
                def pair(i, first=False, last=False):
                    for u in range(2):
                        e = 2 * i + u
                        if not (last and u == 1):
                            dve_xt(dve, e + 1, 1 - u, first=(first and u == 0))
                        dve_act(dve, e, u, first=first)

                dve_xt(dve, 0, 0, first=True)
                pair(0, first=True)
                with dve.Fori(1, LAST) as i:
                    pair(i)
                pair(LAST, last=True)

            @block.scalar
            def _(act):
                def pair(i, first=False):
                    for u in range(2):
                        e = 2 * i + u
                        act_silu(act, e, u, first=first)
                        if not (first and u == 0):
                            act_y(act, e - 1, 1 - u, i - (1 - u))

                pair(0, first=True)
                with act.Fori(1, NEXP // 2) as i:
                    pair(i)
                act_y(act, NEXP - 1, 1, LAST)

            @block.gpsimd
            def _(pool):
                with pool.Fori(0, NEXP // 2) as i:
                    for u in range(2):
                        pool_store(pool, 2 * i + u, u)
                for u in range(2):
                    pool.wait_ge(y_out[u], 16 * (NEXP // 2))


def overflow_blocks(core):
    nc = core.nc
    own, sb, sem = open_stage(core)
    with own:
        wg, wu = sb("o_wg", [P, KD, DE]), sb("o_wu", [P, KD, DE])
        wd = sb("o_wd", [P, KE, D])
        x, xT = sb("o_x", [CAP, D]), sb("o_xT", [P, KD, CAP])
        silu, act_T = sb("o_silu", [P, KE, CAP]), sb("o_act", [P, KE, CAP])
        y = sb("o_y", [CAP, D])
        loaded, tr_mm, xt_ok, gate_up_mm, silu_ok, act_ok, down_mm, y_ok, y_out = (
            sem(f"o_{n}") for n in ("loaded", "tr_mm", "xt_ok", "gate_up_mm", "silu_ok", "act_ok",
                                    "down_mm", "y_ok", "y_out"))

        def each_block(eng, body, skipped=None):
            there = eng.value_load(core.overflow[0:1, NBI:NBI + 1], min_val=0, max_val=NOV)
            with eng.If(there > 0):
                with eng.Fori(0, NOV) as b:
                    with eng.If(there > b):
                        body(b)
                    if skipped:
                        with eng.Else():
                            skipped(1)
            if skipped:
                with eng.Else():
                    skipped(NOV)

        with nc.Block() as block:

            @block.sync
            def _(sp):
                def body(b):
                    e = sp.value_load(core.overflow[0:1, bass.ds(b, 1)], min_val=0, max_val=NEXP - 1)
                    rows = (NEXP + b) * CAP
                    sp.dma_start(wg[:, :, :], core.expert_rows("w_gate", e, KD)).then_inc(loaded, 16)
                    sp.dma_start(x[:, :], core.rows_in[bass.ds(rows, CAP), :]).then_inc(loaded, 16)
                    sp.dma_start(wu[:, :, :], core.expert_rows("w_up", e, KD)).then_inc(loaded, 16)
                    sp.dma_start(wd[:, :, :], core.expert_cols("w_down", e)).then_inc(loaded, 16)
                    sp.wait_ge(y_ok, b + 1)
                    sp.dma_start(core.rows_out[bass.ds(rows, CAP), :], y[:, :]).then_inc(y_out, 16)

                def skipped(n):
                    sp.sem_inc(y_out, 16 * n)

                each_block(sp, body, skipped)
                sp.wait_ge(y_out, 16 * NOV + 16)

            @block.tensor
            def _(pe):
                def body(b):
                    pe.wait_ge(loaded, 64 * b + 64)
                    for j in range(2):
                        for c in range(4):
                            last = pe.transpose(core.bank[j][:, c * CAP:(c + 1) * CAP],
                                                x[:, bass.ds(4 * j + c, P, KD)], core.ident[0:CAP, 0:CAP])
                    last.then_inc(tr_mm, 1)
                    pe.wait_ge(xt_ok, b + 1)
                    for bank, w in ((2, wg), (3, wu)):
                        for j in range(KE):
                            for k in range(KD):
                                last = pe.matmul(core.bank[bank][:, j * CAP:(j + 1) * CAP],
                                                 w[:, k, j * P:(j + 1) * P], xT[:, k, :],
                                                 start=(k == 0), stop=(k == KD - 1))
                        last.then_inc(gate_up_mm, 1)
                    pe.wait_ge(act_ok, b + 1)
                    for j in range(2):
                        for k in range(KE):
                            last = pe.matmul(core.bank[6 + j][0:CAP, :], act_T[:, k, :],
                                             wd[:, k, j * 512:(j + 1) * 512], start=(k == 0), stop=(k == KE - 1))
                    last.then_inc(down_mm, 1)
                each_block(pe, body)

            @block.vector
            def _(dve):
                def body(b):
                    dve.wait_ge(tr_mm, b + 1)
                    for j in range(2):
                        last = dve.tensor_copy(xT[:, 4 * j:4 * j + 4, :],
                                               core.bank[j][:, 0:4 * CAP].rearrange("p (k r) -> p k r", k=4))
                    last.then_inc(xt_ok, 1)
                    dve.wait_ge(silu_ok, b + 1)
                    dve.wait_ge(gate_up_mm, 2 * b + 2)
                    dve.tensor_tensor(act_T[:, :, :], silu[:, :, :],
                                      core.bank[3][:, 0:KE * CAP].rearrange("p (k r) -> p k r", k=KE),
                                      ALU.mult).then_inc(act_ok, 1)
                each_block(dve, body)

            @block.scalar
            def _(act):
                def body(b):
                    act.wait_ge(gate_up_mm, 2 * b + 1)
                    act.activation(silu[:, :, :], core.bank[2][:, 0:KE * CAP].rearrange("p (k r) -> p k r", k=KE),
                                   ACT.Silu).then_inc(silu_ok, 1)
                    act.wait_ge(down_mm, b + 1)
                    act.wait_ge(y_out, 16 * b + 16)
                    for j in range(2):
                        last = act.activation(y[:, j * 512:(j + 1) * 512], core.bank[6 + j][0:CAP, :], ACT.Copy)
                    last.then_inc(y_ok, 1)
                act.sem_inc(y_out, 16)
                each_block(act, body)


def combine(core):
    nc = core.nc
    own, sb, sem = open_stage(core)
    with own:
        x1 = core.x1_back
        row = [[sb(f"c_row{n}_{u}", [P, D]) for u in range(3)] for n in range(2)]
        row_in = [sem(f"c_row_in{u}") for u in range(3)]
        used, stored = sem("c_used"), sem("c_stored")
        with nc.Block() as block:

            @block.gpsimd
            def _(pool):
                for t in range(NT):
                    if t >= 3:
                        pool.wait_ge(used, t - 2)
                    for n in range(2):
                        at = core.place[:, n * NT + t:n * NT + t + 1]
                        pool.indirect_dma_start(out=row[n][t % 3][:, :], out_offset=None, in_=core.rows_out[:, :],
                                                in_offset=bass.IndirectOffsetOnAxis(ap=at, axis=0))\
                            .then_inc(row_in[t % 3], 16)

            @block.vector
            def _(dve):
                dve.wait_ge(core.x1_in, 16)
                for t in range(NT):
                    dve.wait_ge(row_in[t % 3], 32 * (t // 3 + 1))
                    for n in range(2):
                        last = dve.scalar_tensor_tensor(x1[:, t, :], row[n][t % 3][:, :],
                                                        core.weight[:, n * NT + t:n * NT + t + 1], x1[:, t, :],
                                                        ALU.mult, ALU.add)
                        if n == 0:
                            dve.drain()
                    last.then_inc(used, 1)

            @block.sync
            def _(sp):
                for t in range(NT):
                    sp.wait_ge(used, t + 1)
                    sp.dma_start(core.out_tile(t), x1[:, t, :]).then_inc(stored, 16)
                sp.wait_ge(stored, 16 * NT)


def build(nc, d, out_prompt, out_sample):
    core = Core()
    core.nc, core.d = nc, d
    core.out = (out_prompt, out_sample)
    w_in = d["w_in"].rearrange("o (k p) n -> (o p) k n", p=P)

    def tile_rows(pair, t):
        s = 0 if t < FIRST[1] else 1
        at = (t - FIRST[s]) * P
        return pair[s][0, at:at + P, :]

    core.x_tile = lambda t: tile_rows((d["x_prompt"], d["x_sample"]), t)
    core.out_tile = lambda t: tile_rows(core.out, t)
    core.w_in = w_in
    core.w_in_cols = lambda col, width: w_in[:, :, bass.ds(col, width)]
    core.rows_in = nc.dram_tensor("rows_in", (ROWS, D), F32, kind="Internal").ap()
    core.rows_out = nc.dram_tensor("rows_out", (ROWS, D), F32, kind="Internal").ap()
    core.y_ssd = nc.dram_tensor("y_ssd", (TOK, DI), F32, kind="Internal").ap()
    core.x1 = nc.dram_tensor("x1_rows", (TOK, D), F32, kind="Internal").ap()
    core.sums = [nc.dram_tensor(f"decay_sums{u}", (SH, TOK), F32, kind="Internal").ap() for u in range(2)]
    core.expert_rows = lambda name, e, k: (d[name].rearrange("o e (p k) n -> (o e) p k n", k=k)
                                           [bass.ds(e, 1), :, :, :].rearrange("e p k n -> (e p) k n"))
    core.expert_cols = lambda name, e: (d[name].rearrange("o e (k p) n -> (o e) p k n", p=P)
                                        [bass.ds(e, 1), :, :, :].rearrange("e p k n -> (e p) k n"))
    with ExitStack() as life:
        def sb(name, shape, dt=F32, of=life):
            return of.enter_context(nc.sbuf_tensor(name, shape, dt))

        def right(name, shape, of):
            return of.enter_context(nc.sbuf_tensor(name, shape, F32, side="right"))

        core.const, core.feat, core.row = sb("const", [P, C_N]), sb("feat", [P, P_N]), sb("row", [P, R_N])
        core.place, core.weight = sb("place", [P, 2 * NT], I32), sb("weight", [P, 2 * NT])
        core.overflow = sb("overflow", [1, NBI + 1], I32)
        core.bank = [life.enter_context(nc.psum_tensor(f"bank{n}", [P, 512], F32)) for n in range(8)]
        core.ident, core.upper, core.lower, core.strict, core.ones = (
            core.const[:, c:c + P] for c in (C_ID, C_UP, C_LO, C_SU, C_ONE))
        core.head_mean, core.swap = core.const[:, C_MEAN:C_MEAN + P], core.const[:, C_SWAP:C_SWAP + P]
        core.cos, core.sin = core.const[:, C_COS:C_COS + NPOS], core.const[:, C_SIN:C_SIN + NPOS]
        core.zeros = sb("zeros", [CAP, ZW])
        core.zero_out = life.enter_context(nc.semaphore("zero_out"))
        core.piece_sems = ([life.enter_context(nc.semaphore(f"piece_loaded{u}")) for u in range(2)],
                           *(life.enter_context(nc.semaphore(f"piece_{n}")) for n in ("rounded", "split", "used")))
        core.params_in = life.enter_context(nc.semaphore("params_in"))
        core.w_dt_in = life.enter_context(nc.semaphore("w_dt_in"))
        with ExitStack() as mixer:
            with ExitStack() as projections:
                core.h = Pair(lambda *args: sb(*args, of=projections), "h", [P, KD, TOK])
                pieces = projections.enter_context(ExitStack())
                core.pieces = new_pieces(core, lambda *args: sb(*args, of=pieces), "w", 0)
                with ExitStack() as ssm:
                    steps = ssm.enter_context(ExitStack())
                    core.w_dt = right("w_dt", [P, KD, 2 * SH], steps)
                    norm_and_transpose(core)
                    tables = sb("ssd_tables", [P, 5 * NT * 2, SH], of=ssm)
                    core.tables = tables[:, :, :]
                    core.tab = {}
                    for n, name in enumerate(("dt", "cum", "reach", "to_end", "decay")):
                        core.tab[name] = tables[:, n * NT * 2:(n + 1) * NT * 2, :].rearrange("p (t d) h -> p t (d h)", d=2)
                    step_sizes(core)
                    steps.close()
                    ssd_groups(core)
                core.mergedT = right("mergedT", [P, KD, TOK], mixer)
                ssm_branch(core)
                with ExitStack() as attention:
                    core.attnT = right("attnT", [P, KD, TOK], attention)
                    with ExitStack() as heads:
                        core.qk = right("qk", [P, NQK * HD // P, TOK], heads)
                        core.k_both = right("k_both", [P, HKV, TOK], heads)
                        core.v = right("v", [P, NT, HKV * HD], heads)
                        project_qkv(core)
                        pieces.close()
                        attend(core)
                    attention_output(core)
            core.first_weights = expert_weights(sb, "e0")
            core.first_weights_in = [life.enter_context(nc.semaphore(f"e0_{n}_in")) for n in ("wg", "wu", "wd")]
            mix_and_route(core)
        core.x1_back, core.x1_in = sb("x1", [P, NT, D]), life.enter_context(nc.semaphore("x1_in"))
        experts(core)
        overflow_blocks(core)
        combine(core)


_WHOLE = ['x_prompt', 'x_sample', 'w_in', 'w_out_attn', 'w_out_ssm', 'w_o', 'w_gate', 'w_up', 'w_down']


def kernel(**inputs):
    import numpy as _np
    import concourse.bacc as _bacc
    from concourse import mybir as _mybir
    from concourse.bass_utils import run_bass_kernel_spmd as _run

    def a(name):
        return _np.ascontiguousarray(inputs[name])

    def by_feature(v):
        return v.reshape(-1, P).T

    conv = _np.concatenate([a('conv_w')[0], a('conv_b')], 0).T
    conv_groups = _np.concatenate([conv[:DI].reshape(SG, GW // P, P, CW + 1),
                                   conv[DI:DI + SG * NS].reshape(SG, 1, P, CW + 1),
                                   conv[DI + SG * NS:].reshape(SG, 1, P, CW + 1)], 1)
    packed = {
        'constants': pack_constants(),
        'features': _np.concatenate([by_feature(a('norm_mix')[0]), by_feature(a('ssm_norm')[0]),
                                     conv_groups.transpose(2, 0, 1, 3).reshape(P, -1),
                                     by_feature(_np.concatenate([_np.tile(a('q_norm')[0], HQ),
                                                                 _np.tile(a('k_norm')[0], HKV)]))], 1),
        'rows': _np.concatenate([a('dt_bias_fwd')[0], a('dt_bias_bwd')[0], a('a_log_fwd')[0], a('a_log_bwd')[0],
                                 a('d_skip')[0], a('attn_sink')[0], a('b_router_group')[0],
                                 a('b_router_expert')[0], a('norm_ffn')[0]]),
        'router': _np.concatenate([a('w_router_group')[0], a('w_router_expert')[0]], 1),
    }
    nc = _bacc.Bacc("TRN2", target_bir_lowering=False, num_devices=1)
    arrays, d = {}, {}
    for name, v in [(n, a(n)) for n in _WHOLE] + list(packed.items()):
        arrays[f"in_{name}"] = _np.ascontiguousarray(v)
        d[name] = nc.dram_tensor(f"in_{name}", v.shape, _mybir.dt.from_np(v.dtype), kind="ExternalInput").ap()
    outs = [nc.dram_tensor(f"out_{n}", (1, s, D), F32, kind="ExternalOutput").ap() for n, s in enumerate(SEQS)]
    build(nc, d, *outs)
    r = _run(nc, [arrays], core_ids=[0])
    return tuple(r.results[0][f"out_{n}"] for n in range(2))
```
